# Optimizing a Trainium2 kernel written in Bass

```python
import jax
import jax.numpy as jnp
from jax import lax
import numpy as np
import math
import jax, jax.numpy as jnp

D_MODEL = 1024
BATCH = 1
SEQ = 256
DEPTH = 2

CTX_LEN = 256
GRID_W = 64
HEAD_DIM = D_MODEL // 16
N_FOURIER_GROUPS = 4
N_NA_HEADS = 4
N_GLA_HEADS = 4
N_GQA_HEADS = 4
N_GQA_KV_HEADS = 2
GQA_GROUP = N_GQA_HEADS // N_GQA_KV_HEADS
GLA_DK = HEAD_DIM // 2
GLA_DV = HEAD_DIM
GLA_GATE_RANK = 16
GLA_TAU = 16.0
GLA_CHUNK = 64
NA_ROWS = 8
NA_COLS = 16
Q_BLOCK = 128
D_FF = 256 * ((8 * D_MODEL // 3 + 255) // 256)
ROPE_THETA = 10000.0
EPS = 1e-6
N_MOD = 9

W_FOURIER = N_FOURIER_GROUPS * HEAD_DIM
W_NA = N_NA_HEADS * HEAD_DIM
W_GLA = N_GLA_HEADS * GLA_DV
W_GQA = N_GQA_HEADS * HEAD_DIM
D_MIX = W_FOURIER + W_NA + W_GLA + W_GQA

IN_LAYOUT = (
    ('fourier', W_FOURIER),
    ('na_q', W_NA), ('na_k', W_NA), ('na_v', W_NA),
    ('gla_q', N_GLA_HEADS * GLA_DK), ('gla_k', N_GLA_HEADS * GLA_DK),
    ('gla_v', W_GLA), ('gla_r', W_GLA),
    ('gla_gf', GLA_GATE_RANK), ('gla_gb', GLA_GATE_RANK),
    ('gqa_q', W_GQA), ('gqa_k', N_GQA_KV_HEADS * HEAD_DIM), ('gqa_v', N_GQA_KV_HEADS * HEAD_DIM),
)
D_IN = sum(w for _, w in IN_LAYOUT)


def rms_norm(x, gain=None):
    xf = x.astype(jnp.float32)
    y = xf * lax.rsqrt(jnp.mean(xf * xf, axis=-1, keepdims=True) + EPS)
    if gain is not None:
        y = y * gain.astype(jnp.float32)
    return y.astype(x.dtype)

def modulate(h, shift, scale):
    return h * (1.0 + scale) + shift

def swiglu(h, w1, w3, w2):
    return (jax.nn.silu(h @ w1) * (h @ w3)) @ w2

def heads(t, n, d):
    return t.reshape(t.shape[:-1] + (n, d))

def split_in(h):
    offsets = np.cumsum([w for _, w in IN_LAYOUT])[:-1].tolist()
    parts = jnp.split(h, offsets, axis=-1)
    return {name: part for (name, _), part in zip(IN_LAYOUT, parts)}

def axial_rope(n_tokens):
    t = jnp.arange(n_tokens, dtype=jnp.int32)
    row = (t // GRID_W).astype(jnp.float32)
    col = (t % GRID_W).astype(jnp.float32)
    n_freq = HEAD_DIM // 4
    inv_freq = ROPE_THETA ** (-jnp.arange(n_freq, dtype=jnp.float32) / n_freq)
    ang = jnp.concatenate([row[:, None] * inv_freq, col[:, None] * inv_freq], axis=-1)
    return jnp.cos(ang)[:, None, :], jnp.sin(ang)[:, None, :]

def apply_rope(x, cos, sin):
    xf = x.astype(jnp.float32)
    x1, x2 = jnp.split(xf, 2, axis=-1)
    return jnp.concatenate([x1 * cos - x2 * sin, x1 * sin + x2 * cos], axis=-1).astype(x.dtype)

def fourier_mix(u):
    b_, l_, _ = u.shape
    uf = u.astype(jnp.float32).reshape(b_, l_, N_FOURIER_GROUPS, HEAD_DIM)
    y = jnp.fft.fft2(uf, axes=(1, 3), norm='ortho').real
    return y.reshape(b_, l_, W_FOURIER).astype(u.dtype)

def block_attention(q, k, v):
    b_, lq, hk, g, dh = q.shape
    nb = lq // Q_BLOCK
    qb = (q * dh ** -0.5).reshape(b_, nb, Q_BLOCK, hk, g, dh).swapaxes(0, 1)

    def one_block(q_blk):
        s = jnp.einsum('bqhgd,bkhd->bhgqk', q_blk, k).astype(jnp.float32)
        p = jax.nn.softmax(s, axis=-1).astype(v.dtype)
        return jnp.einsum('bhgqk,bkhd->bqhgd', p, v)

    o = lax.map(one_block, qb)
    return o.swapaxes(0, 1).reshape(b_, lq, hk * g * dh)

def neighborhood_attention(q, k, v, k_ctx, v_ctx, rpb):
    b_, s_, h_, dh = q.shape
    rows = s_ // GRID_W
    kr = min(NA_ROWS, rows)
    kg = k.reshape(b_, rows, GRID_W, h_, dh)
    vg = v.reshape(b_, rows, GRID_W, h_, dh)
    qg = q.reshape(b_, rows, GRID_W, h_, dh).transpose(1, 0, 2, 3, 4)
    r_pos = jnp.arange(rows)
    c_pos = jnp.arange(GRID_W)
    row_start = jnp.clip(r_pos - kr // 2, 0, rows - kr)
    rel_row = row_start[:, None] + jnp.arange(kr)[None, :] - r_pos[:, None]
    col_start = jnp.clip(c_pos - NA_COLS // 2, 0, GRID_W - NA_COLS)
    col_idx = col_start[:, None] + jnp.arange(NA_COLS)[None, :]
    rel_col = col_idx - c_pos[:, None]
    bias_col = rpb.astype(jnp.float32)[:, :, rel_col + NA_COLS - 1]
    scale = dh ** -0.5
    n_win = kr * NA_COLS

    def row_block(args):
        q_r, rs, rr = args
        k_blk = lax.dynamic_slice_in_dim(kg, rs, kr, axis=1)[:, :, col_idx]
        v_blk = lax.dynamic_slice_in_dim(vg, rs, kr, axis=1)[:, :, col_idx]
        bias = bias_col[:, rr + NA_ROWS - 1].transpose(0, 2, 1, 3)
        s_win = jnp.einsum('bchd,brckhd->bhcrk', q_r, k_blk).astype(jnp.float32) * scale + bias[None]
        s_ctx = jnp.einsum('bchd,bjhd->bhcj', q_r, k_ctx).astype(jnp.float32) * scale
        s = jnp.concatenate([s_win.reshape(b_, h_, GRID_W, n_win), s_ctx], axis=-1)
        p = jax.nn.softmax(s, axis=-1).astype(v.dtype)
        p_win = p[..., :n_win].reshape(b_, h_, GRID_W, kr, NA_COLS)
        p_ctx = p[..., n_win:]
        return (jnp.einsum('bhcrk,brckhd->bchd', p_win, v_blk)
                + jnp.einsum('bhcj,bjhd->bchd', p_ctx, v_ctx))

    out = lax.map(row_block, (qg, row_start, rel_row))
    return out.transpose(1, 0, 2, 3, 4).reshape(b_, s_, h_ * dh)

def gla_scan(q, k, v, log_a, s0):
    b_, h_, l_, _ = q.shape
    dv = v.shape[-1]
    n_chunks = l_ // GLA_CHUNK

    def chunks(t):
        return t.reshape(b_, h_, n_chunks, GLA_CHUNK, t.shape[-1]).transpose(2, 0, 1, 3, 4)

    lower_tri = jnp.tril(jnp.ones((GLA_CHUNK, GLA_CHUNK), dtype=bool))[None, None, :, :, None]

    def step(s, inp):
        qc, kc, vc, ac = inp
        qf, kf, vf = (t.astype(jnp.float32) for t in (qc, kc, vc))
        b = jnp.cumsum(ac.astype(jnp.float32), axis=2)
        rel = b[:, :, :, None, :] - b[:, :, None, :, :]
        decay = jnp.where(lower_tri, jnp.exp(jnp.minimum(rel, 0.0)), 0.0)
        scores = jnp.einsum('bhid,bhjd,bhijd->bhij', qf, kf, decay)
        o = (jnp.einsum('bhcd,bhde->bhce', qf * jnp.exp(b), s)
             + jnp.einsum('bhij,bhje->bhie', scores, vf))
        b_last = b[:, :, -1:, :]
        s_new = (jnp.exp(b_last[:, :, 0, :])[..., None] * s
                 + jnp.einsum('bhcd,bhce->bhde', kf * jnp.exp(b_last - b), vf))
        return s_new, o.astype(v.dtype)

    s_final, o = lax.scan(step, s0, (chunks(q), chunks(k), chunks(v), chunks(log_a)))
    return o.transpose(1, 2, 0, 3, 4).reshape(b_, h_, l_, dv), s_final

def bidir_gla(q, k, v, a_f, a_b, s0_f, s0_b):
    flip = lambda t: jnp.flip(t, axis=2)
    o_f, s_f = gla_scan(q, k, v, a_f, s0_f)
    o_b, s_b = gla_scan(flip(q), flip(k), flip(v), flip(a_b), s0_b)
    return o_f + flip(o_b), s_f, s_b

def gla_prepare(p, w_gf, b_gf, w_gb, b_gb):
    to_bhld = lambda t, d: heads(t, N_GLA_HEADS, d).transpose(0, 2, 1, 3)
    q = to_bhld(p['gla_q'] * GLA_DK ** -0.5, GLA_DK)
    k = to_bhld(p['gla_k'], GLA_DK)
    v = to_bhld(p['gla_v'], GLA_DV)
    a_f = to_bhld(jax.nn.log_sigmoid((p['gla_gf'] @ w_gf + b_gf).astype(jnp.float32)) / GLA_TAU, GLA_DK)
    a_b = to_bhld(jax.nn.log_sigmoid((p['gla_gb'] @ w_gb + b_gb).astype(jnp.float32)) / GLA_TAU, GLA_DK)
    return q, k, v, a_f, a_b

def gla_output(o, r, gain):
    b_, _, l_, _ = o.shape
    o = rms_norm(o.transpose(0, 2, 1, 3), gain).reshape(b_, l_, W_GLA)
    return o * jax.nn.silu(r)

def token_mixing(hx, hz, cos, sin, na_q_norm, na_k_norm, na_rpb, gla_w_gate_f, gla_b_gate_f,
                 gla_w_gate_b, gla_b_gate_b, gla_norm, gqa_q_norm, gqa_k_norm, with_ctx_out):
    px, pz = split_in(hx), split_in(hz)
    b_, s_ = hx.shape[0], hx.shape[1]
    lc = hz.shape[1]
    a_x = fourier_mix(px['fourier'])
    na_q = lambda p: rms_norm(heads(p['na_q'], N_NA_HEADS, HEAD_DIM), na_q_norm)
    na_k = lambda p: rms_norm(heads(p['na_k'], N_NA_HEADS, HEAD_DIM), na_k_norm)
    na_v = lambda p: heads(p['na_v'], N_NA_HEADS, HEAD_DIM)
    kz_na, vz_na = na_k(pz), na_v(pz)
    b_x = neighborhood_attention(na_q(px), na_k(px), na_v(px), kz_na, vz_na, na_rpb)
    gates = (gla_w_gate_f, gla_b_gate_f, gla_w_gate_b, gla_b_gate_b)
    s0 = jnp.zeros((b_, N_GLA_HEADS, GLA_DK, GLA_DV), jnp.float32)
    oz_gla, s_f, s_b = bidir_gla(*gla_prepare(pz, *gates), s0, s0)
    ox_gla, _, _ = bidir_gla(*gla_prepare(px, *gates), s_f, s_b)
    c_x = gla_output(ox_gla, px['gla_r'], gla_norm)
    gqa_q = lambda p: rms_norm(heads(p['gqa_q'], N_GQA_HEADS, HEAD_DIM), gqa_q_norm)
    gqa_k = lambda p: rms_norm(heads(p['gqa_k'], N_GQA_KV_HEADS, HEAD_DIM), gqa_k_norm)
    gqa_v = lambda p: heads(p['gqa_v'], N_GQA_KV_HEADS, HEAD_DIM)
    kz_gqa, vz_gqa = gqa_k(pz), gqa_v(pz)
    qx_gqa = apply_rope(gqa_q(px), cos, sin).reshape(b_, s_, N_GQA_KV_HEADS, GQA_GROUP, HEAD_DIM)
    kx_gqa = apply_rope(gqa_k(px), cos, sin)
    d_x = block_attention(qx_gqa, jnp.concatenate([kx_gqa, kz_gqa], axis=1),
                          jnp.concatenate([gqa_v(px), vz_gqa], axis=1))
    out_x = jnp.concatenate([a_x, b_x, c_x, d_x], axis=-1)
    if not with_ctx_out:
        return out_x, None
    a_z = fourier_mix(pz['fourier'])
    b_z = block_attention(na_q(pz)[:, :, :, None, :], kz_na, vz_na)
    c_z = gla_output(oz_gla, pz['gla_r'], gla_norm)
    d_z = block_attention(gqa_q(pz).reshape(b_, lc, N_GQA_KV_HEADS, GQA_GROUP, HEAD_DIM), kz_gqa, vz_gqa)
    return out_x, jnp.concatenate([a_z, b_z, c_z, d_z], axis=-1)

def first_inputs(seed: int = 0) -> dict:
    key = jax.random.key(seed)
    ks = iter(jax.random.split(key, 32))
    f32 = jnp.float32

    def nrm(shape, std):
        return jax.random.normal(next(ks), shape, f32) * std

    L, D = DEPTH, D_MODEL
    return {
        'x': nrm((BATCH, SEQ, D), 1.0),
        'c': nrm((BATCH, D), 1.0),
        'ctx': nrm((BATCH, CTX_LEN, D), 1.0),
        'c_ctx': nrm((D,), 1.0),
        'w_mod': nrm((L, D, N_MOD * D), 0.5 * D ** -0.5),
        'b_mod': nrm((L, N_MOD * D), 0.02),
        'ffn1_w1': nrm((L, D, D_FF), D ** -0.5),
        'ffn1_w3': nrm((L, D, D_FF), D ** -0.5),
        'ffn1_w2': nrm((L, D_FF, D), D_FF ** -0.5),
        'w_in': nrm((L, D, D_IN), D ** -0.5),
        'na_q_norm': 1.0 + nrm((L, HEAD_DIM), 0.1),
        'na_k_norm': 1.0 + nrm((L, HEAD_DIM), 0.1),
        'na_rpb': nrm((L, N_NA_HEADS, 2 * NA_ROWS - 1, 2 * NA_COLS - 1), 0.1),
        'gla_w_gate_f': nrm((L, GLA_GATE_RANK, N_GLA_HEADS * GLA_DK), GLA_GATE_RANK ** -0.5),
        'gla_b_gate_f': nrm((L, N_GLA_HEADS * GLA_DK), 0.1),
        'gla_w_gate_b': nrm((L, GLA_GATE_RANK, N_GLA_HEADS * GLA_DK), GLA_GATE_RANK ** -0.5),
        'gla_b_gate_b': nrm((L, N_GLA_HEADS * GLA_DK), 0.1),
        'gla_norm': 1.0 + nrm((L, GLA_DV), 0.1),
        'gqa_q_norm': 1.0 + nrm((L, HEAD_DIM), 0.1),
        'gqa_k_norm': 1.0 + nrm((L, HEAD_DIM), 0.1),
        'w_out': nrm((L, D_MIX, D), D_MIX ** -0.5),
        'ffn2_w1': nrm((L, D, D_FF), D ** -0.5),
        'ffn2_w3': nrm((L, D, D_FF), D ** -0.5),
        'ffn2_w2': nrm((L, D_FF, D), D_FF ** -0.5),
    }

def first_block(x, c, ctx, c_ctx, w_mod, b_mod, ffn1_w1, ffn1_w3, ffn1_w2, w_in,
              na_q_norm, na_k_norm, na_rpb, gla_w_gate_f, gla_b_gate_f, gla_w_gate_b, gla_b_gate_b,
              gla_norm, gqa_q_norm, gqa_k_norm, w_out, ffn2_w1, ffn2_w3, ffn2_w2):
    cos, sin = axial_rope(x.shape[1])
    z = ctx
    for l in range(DEPTH):
        last = l == DEPTH - 1
        mx = jnp.split((jax.nn.silu(c) @ w_mod[l] + b_mod[l])[:, None, :], N_MOD, axis=-1)
        mz = jnp.split(jax.nn.silu(c_ctx) @ w_mod[l] + b_mod[l], N_MOD, axis=-1)
        x = x + 0.5 * mx[2] * swiglu(modulate(rms_norm(x), mx[0], mx[1]), ffn1_w1[l], ffn1_w3[l], ffn1_w2[l])
        z = z + 0.5 * mz[2] * swiglu(modulate(rms_norm(z), mz[0], mz[1]), ffn1_w1[l], ffn1_w3[l], ffn1_w2[l])
        hx = modulate(rms_norm(x), mx[3], mx[4]) @ w_in[l]
        hz = modulate(rms_norm(z), mz[3], mz[4]) @ w_in[l]
        mix_x, mix_z = token_mixing(hx, hz, cos, sin, na_q_norm[l], na_k_norm[l], na_rpb[l],
                                    gla_w_gate_f[l], gla_b_gate_f[l], gla_w_gate_b[l], gla_b_gate_b[l],
                                    gla_norm[l], gqa_q_norm[l], gqa_k_norm[l], not last)
        x = x + mx[5] * (mix_x @ w_out[l])
        x = x + 0.5 * mx[8] * swiglu(modulate(rms_norm(x), mx[6], mx[7]), ffn2_w1[l], ffn2_w3[l], ffn2_w2[l])
        if not last:
            z = z + mz[5] * (mix_z @ w_out[l])
            z = z + 0.5 * mz[8] * swiglu(modulate(rms_norm(z), mz[6], mz[7]), ffn2_w1[l], ffn2_w3[l], ffn2_w2[l])
    return x


N_META = 16
MIX_WIDTH = D_MODEL
FOX_WIDTH = MIX_WIDTH // 2
RET_WIDTH = MIX_WIDTH - FOX_WIDTH
FOX_HEAD_DIM = 64
FOX_HEADS = FOX_WIDTH // FOX_HEAD_DIM
RET_HEADS = 4
RET_HEAD_DIM = RET_WIDTH // RET_HEADS
D_FF_2 = -(-8 * D_MODEL // (3 * 256)) * 256
BLOCK_Q = 128
RET_CHUNK = 128
ROPE_BASE = 10000.0
FGATE_BIAS_MEAN = 3.0
RET_LOG_GAMMA = tuple(math.log(1.0 - 2.0 ** (-5 - h)) for h in range(RET_HEADS))
IN_SIZES = (FOX_WIDTH, FOX_WIDTH, FOX_WIDTH, FOX_HEADS, RET_WIDTH, RET_WIDTH, RET_WIDTH, RET_WIDTH)
IN_COLS = sum(IN_SIZES)
SPLIT_POINTS = tuple(int(v) for v in np.cumsum(IN_SIZES)[:-1])


def rmsnorm(x, g):
    x32 = x.astype(jnp.float32)
    y = x32 * lax.rsqrt(jnp.mean(x32 * x32, axis=-1, keepdims=True) + EPS)
    return (y * g.astype(jnp.float32)).astype(x.dtype)

def rotate(x, cos, sin):
    half = x.shape[-1] // 2
    x1, x2 = x[..., :half], x[..., half:]
    c = cos[None, :, None, :].astype(x.dtype)
    s = sin[None, :, None, :].astype(x.dtype)
    return jnp.concatenate([x1 * c - x2 * s, x1 * s + x2 * c], axis=-1)

def fox_attention(q, k, v, logf):
    B, L, H, Dh = q.shape
    scale = Dh ** -0.5
    c = jnp.cumsum(logf, axis=1).transpose(0, 2, 1)
    qh = q.transpose(0, 2, 1, 3)
    kh = k.transpose(0, 2, 1, 3)
    vh = v.transpose(0, 2, 1, 3)
    pos = jnp.arange(L)

    def attend(q_blk, c_q, q_pos, k_, v_, c_k, k_pos):
        s = jnp.einsum('bhqd,bhkd->bhqk', q_blk, k_).astype(jnp.float32) * scale
        s = s + c_q[..., :, None] - c_k[..., None, :]
        s = jnp.where(k_pos[None, :] <= q_pos[:, None], s, -jnp.inf)
        p = jax.nn.softmax(s, axis=-1)
        return jnp.einsum('bhqk,bhkd->bhqd', p.astype(v_.dtype), v_)

    meta_out = attend(qh[:, :, :N_META], c[:, :, :N_META], pos[:N_META],
                      kh[:, :, :N_META], vh[:, :, :N_META], c[:, :, :N_META], pos[:N_META])
    n_blk = (L - N_META) // BLOCK_Q
    q_real = qh[:, :, N_META:].reshape(B, H, n_blk, BLOCK_Q, Dh).transpose(2, 0, 1, 3, 4)
    c_real = c[:, :, N_META:].reshape(B, H, n_blk, BLOCK_Q).transpose(2, 0, 1, 3)
    pos_real = pos[N_META:].reshape(n_blk, BLOCK_Q)
    real_out = lax.map(lambda a: attend(a[0], a[1], a[2], kh, vh, c, pos),
                       (q_real, c_real, pos_real))
    real_out = real_out.transpose(1, 2, 0, 3, 4).reshape(B, H, L - N_META, Dh)
    out = jnp.concatenate([meta_out, real_out], axis=2)
    return out.transpose(0, 2, 1, 3)

def retention_chunkwise(q, k, v):
    B, L, H, Dh = q.shape
    log_g = jnp.array(RET_LOG_GAMMA, dtype=jnp.float32)

    def intra(qc, kc, vc, n):
        idx = jnp.arange(n)
        diff = idx[:, None] - idx[None, :]
        dec = jnp.where(diff >= 0,
                        jnp.exp(jnp.maximum(diff, 0)[None].astype(jnp.float32) * log_g[:, None, None]),
                        0.0)
        s = jnp.einsum('bnhd,bmhd->bhnm', qc, kc).astype(jnp.float32) * dec
        return jnp.einsum('bhnm,bmhd->bnhd', s, vc.astype(jnp.float32))

    qm, km, vm = q[:, :N_META], k[:, :N_META], v[:, :N_META]
    o_meta = intra(qm, km, vm, N_META)
    m_idx = jnp.arange(N_META, dtype=jnp.float32)
    k_dec_meta = jnp.exp((N_META - 1 - m_idx)[:, None] * log_g[None, :])
    state0 = jnp.einsum('bmhd,bmhe->bhde', km.astype(jnp.float32) * k_dec_meta[None, :, :, None],
                        vm.astype(jnp.float32))

    C = RET_CHUNK
    n_chunks = (L - N_META) // C
    j_idx = jnp.arange(C, dtype=jnp.float32)
    q_dec = jnp.exp((j_idx + 1.0)[:, None] * log_g[None, :])[None, :, :, None]
    k_dec = jnp.exp((C - 1.0 - j_idx)[:, None] * log_g[None, :])[None, :, :, None]
    chunk_dec = jnp.exp(C * log_g)[None, :, None, None]

    def to_chunks(t):
        return t[:, N_META:].reshape(B, n_chunks, C, H, Dh).transpose(1, 0, 2, 3, 4)

    def step(state, xs):
        qc, kc, vc = xs
        o = intra(qc, kc, vc, C) + jnp.einsum('bjhd,bhde->bjhe', qc.astype(jnp.float32) * q_dec, state)
        state = chunk_dec * state + jnp.einsum('bjhd,bjhe->bhde', kc.astype(jnp.float32) * k_dec,
                                               vc.astype(jnp.float32))
        return state, o

    _, o_real = lax.scan(step, state0, (to_chunks(q), to_chunks(k), to_chunks(v)))
    o_real = o_real.transpose(1, 0, 2, 3, 4).reshape(B, L - N_META, H, Dh)
    return jnp.concatenate([o_meta, o_real], axis=1)

def head_groupnorm(o, g):
    mu = jnp.mean(o, axis=-1, keepdims=True)
    var = jnp.mean(jnp.square(o - mu), axis=-1, keepdims=True)
    y = (o - mu) * lax.rsqrt(var + EPS)
    B, L, H, Dh = o.shape
    return y.reshape(B, L, H * Dh) * g.astype(jnp.float32)

def hybrid_layer(h, attn_norm_g, w_in, b_fgate, ret_gn_g, w_out,
                 ffn_norm_g, w_gate, w_up, w_down, cos, sin):
    B, L, _ = h.shape
    xn = rmsnorm(h, attn_norm_g)
    proj = jnp.einsum('bld,dc->blc', xn, w_in)
    fq, fk, fv, flog, rq, rk, rv, rg = jnp.split(proj, SPLIT_POINTS, axis=-1)

    logf = jax.nn.log_sigmoid(flog.astype(jnp.float32) + b_fgate.astype(jnp.float32))
    fshape = (B, L, FOX_HEADS, FOX_HEAD_DIM)
    fox_out = fox_attention(fq.reshape(fshape), fk.reshape(fshape), fv.reshape(fshape), logf)
    fox_out = fox_out.reshape(B, L, FOX_WIDTH)

    rshape = (B, L, RET_HEADS, RET_HEAD_DIM)
    rq_ = rotate(rq.reshape(rshape), cos, sin)
    rk_ = rotate(rk.reshape(rshape), cos, sin) * (RET_HEAD_DIM ** -0.5)
    ret = retention_chunkwise(rq_, rk_, rv.reshape(rshape))
    ret = head_groupnorm(ret, ret_gn_g).astype(h.dtype)
    ret_out = jax.nn.silu(rg) * ret

    mix = jnp.concatenate([fox_out, ret_out], axis=-1)
    h = h + jnp.einsum('blc,cd->bld', mix, w_out)

    hn = rmsnorm(h, ffn_norm_g)
    ff = jax.nn.silu(jnp.einsum('bld,df->blf', hn, w_gate)) * jnp.einsum('bld,df->blf', hn, w_up)
    return h + jnp.einsum('blf,fd->bld', ff, w_down)

def second_inputs(seed: int = 0) -> dict:
    key = jax.random.key(seed)
    ks = jax.random.split(key, 12)
    f32 = jnp.float32
    x = jax.random.normal(ks[0], (BATCH, SEQ, D_MODEL), f32)
    meta_tokens = jax.random.normal(ks[1], (N_META, D_MODEL), f32)
    attn_norm = 1.0 + 0.02 * jax.random.normal(ks[2], (DEPTH, D_MODEL), f32)
    w_in = jax.random.normal(ks[3], (DEPTH, D_MODEL, IN_COLS), f32) * D_MODEL ** -0.5
    b_fgate = FGATE_BIAS_MEAN + 0.5 * jax.random.normal(ks[4], (DEPTH, FOX_HEADS), f32)
    ret_gn = 1.0 + 0.02 * jax.random.normal(ks[5], (DEPTH, RET_WIDTH), f32)
    w_out = jax.random.normal(ks[6], (DEPTH, MIX_WIDTH, D_MODEL), f32) * MIX_WIDTH ** -0.5
    ffn_norm = 1.0 + 0.02 * jax.random.normal(ks[7], (DEPTH, D_MODEL), f32)
    w_gate = jax.random.normal(ks[8], (DEPTH, D_MODEL, D_FF_2), f32) * D_MODEL ** -0.5
    w_up = jax.random.normal(ks[9], (DEPTH, D_MODEL, D_FF_2), f32) * D_MODEL ** -0.5
    w_down = jax.random.normal(ks[10], (DEPTH, D_FF_2, D_MODEL), f32) * D_FF_2 ** -0.5
    final_norm = 1.0 + 0.02 * jax.random.normal(ks[11], (D_MODEL,), f32)
    return {"x": x, "meta_tokens": meta_tokens, "attn_norm": attn_norm, "w_in": w_in,
            "b_fgate": b_fgate, "ret_gn": ret_gn, "w_out": w_out, "ffn_norm": ffn_norm,
            "w_gate": w_gate, "w_up": w_up, "w_down": w_down, "final_norm": final_norm}

def second_block(x, meta_tokens, attn_norm, w_in, b_fgate, ret_gn, w_out, ffn_norm,
              w_gate, w_up, w_down, final_norm):
    B = x.shape[0]
    meta = jnp.broadcast_to(meta_tokens[None].astype(x.dtype), (B, N_META, D_MODEL))
    h = jnp.concatenate([meta, x], axis=1)
    L = h.shape[1]
    inv_freq = ROPE_BASE ** (-jnp.arange(0, RET_HEAD_DIM, 2, dtype=jnp.float32) / RET_HEAD_DIM)
    ang = jnp.arange(L, dtype=jnp.float32)[:, None] * inv_freq[None, :]
    cos, sin = jnp.cos(ang), jnp.sin(ang)
    for i in range(DEPTH):
        h = hybrid_layer(h, attn_norm[i], w_in[i], b_fgate[i], ret_gn[i], w_out[i],
                         ffn_norm[i], w_gate[i], w_up[i], w_down[i], cos, sin)
    h = rmsnorm(h, final_norm)
    return h[:, N_META:]


def setup_inputs(seed=0):
    out = dict(first_inputs(seed))
    for name, value in second_inputs(seed + 1).items():
        if name != "x":
            out[name + "_2"] = value
    return out


def reference(
    x, c, ctx, c_ctx, w_mod, b_mod, ffn1_w1, ffn1_w3, ffn1_w2, w_in, na_q_norm, na_k_norm,
    na_rpb, gla_w_gate_f, gla_b_gate_f, gla_w_gate_b, gla_b_gate_b, gla_norm, gqa_q_norm,
    gqa_k_norm, w_out, ffn2_w1, ffn2_w3, ffn2_w2, meta_tokens_2, attn_norm_2, w_in_2, b_fgate_2,
    ret_gn_2, w_out_2, ffn_norm_2, w_gate_2, w_up_2, w_down_2, final_norm_2,
):
    x = first_block(
        x, c, ctx, c_ctx, w_mod, b_mod, ffn1_w1, ffn1_w3, ffn1_w2, w_in, na_q_norm, na_k_norm,
        na_rpb, gla_w_gate_f, gla_b_gate_f, gla_w_gate_b, gla_b_gate_b, gla_norm, gqa_q_norm,
        gqa_k_norm, w_out, ffn2_w1, ffn2_w3, ffn2_w2,
    )
    return second_block(
        x, meta_tokens_2, attn_norm_2, w_in_2, b_fgate_2, ret_gn_2, w_out_2, ffn_norm_2,
        w_gate_2, w_up_2, w_down_2, final_norm_2,
    )


_drawn_inputs = setup_inputs


def setup_inputs(seed=0):
    import zlib

    import numpy as np

    out = dict(_drawn_inputs(seed))
    spreads = {}
    factors = {'na_q_norm': 8.0,
     'na_k_norm': 8.0,
     'na_rpb': 8.0,
     'gla_b_gate_f': 7.765,
     'gla_b_gate_b': 7.277,
     'gqa_q_norm': 8.0,
     'gqa_k_norm': 8.0,
     'ret_gn_2': 4.833,
     'ffn_norm_2': 2.835,
     'final_norm_2': 2.667}
    for name, (base, spread) in spreads.items():
        noise = np.random.default_rng([zlib.crc32(name.encode()), seed]).standard_normal(out[name].shape)
        drawn = base * np.exp(spread * noise) if base else spread * noise
        out[name] = jnp.asarray(drawn.astype(out[name].dtype))
    for name, factor in factors.items():
        out[name] = (out[name] * factor).astype(out[name].dtype)
    return out
```

```python
import math
from contextlib import ExitStack

import numpy as np
import concourse.bass as bass
import concourse.mybir as mybir

F32 = mybir.dt.float32
I32 = mybir.dt.int32
ALU = mybir.AluOpType
ACT = mybir.ActivationFunctionType
AX = mybir.AxisListType

P = 128
D = 1024
KC = D // P
SEQ = 256
NX, NZ = 256, 256
N1 = NX + NZ
META = 16
N2 = META + SEQ
DEPTH = 2
FF = 2816
FC = FF // P
NMOD = 9
EPS = 1e-6
HD = 64
RING = 4
MOD_RING = 3
UNIT = 8 * P
NEG = -1e30
LN_EXP = "natural_log_exp_and_others"

FOUR, NAQ, NAK, GLAQ, GLAK, GLAR, GATE, GQAQ, GQAK = 0, 2, 4, 6, 7, 8, 10, 11, 13
NSLOT1 = 14
NAV, GLAV, GQAV = 0, 256, 512
NV1 = 640
PROJ1 = [("T", FOUR, P, False), ("T", FOUR + 1, P, False), ("T", NAQ, P, False), ("T", NAQ + 1, P, False),
         ("T", NAK, P, True), ("T", NAK + 1, P, True), ("V", NAV, P, True), ("V", NAV + P, P, True),
         ("T", GLAQ, P, False), ("T", GLAK, P, True), ("V", GLAV, P, True), ("V", GLAV + P, P, True),
         ("T", GLAR, P, False), ("T", GLAR + 1, P, False), ("T", GATE, 32, True),
         ("T", GQAQ, P, False), ("T", GQAQ + 1, P, False), ("T", GQAK, P, True), ("V", GQAV, P, True)]
FQ, FK, RQ, RK, RG = 0, 4, 8, 12, 16
NSLOT2 = 20
FLOG = -1
PROJ2 = ([("T", FQ + i, P) for i in range(4)] + [("T", FK + i, P) for i in range(4)]
         + [("V", P * i, P) for i in range(4)] + [("T", FLOG, 8)]
         + [("T", RQ + i, P) for i in range(4)] + [("T", RK + i, P) for i in range(4)]
         + [("V", 512 + P * i, P) for i in range(4)] + [("T", RG + i, P) for i in range(4)])
NV2 = 1024
TILES2 = [(0, 128), (128, 128), (256, 16)]

UNITS = DEPTH * (6 * FC + len(PROJ1) + KC) + DEPTH * (len(PROJ2) + KC + 3 * FC)

S_L1 = {"naq": 0, "nak": 1, "gqaq": 2, "gqak": 3, "gla": 4, "bf": 5, "bb": 6, "bmod": 7}
SW1 = 7 + NMOD * KC
S_L2 = {"attn": 0, "ffn": KC, "gn": 2 * KC, "bfg": 2 * KC + 4}
SW2 = 2 * KC + 5
S_FINAL = DEPTH * (SW1 + SW2)
SMALL = S_FINAL + KC

C_ONESD, C_ONES64, C_ONES128, C_IDENT, C_PERM64, C_PERM128 = (P * i for i in range(6))
C_DFTD = 6 * P
C_DFTL = C_DFTD + 2 * P
C_COS1 = C_DFTL + 2 * 2 * SEQ
C_SIN1 = C_COS1 + SEQ
C_COS2 = C_SIN1 + SEQ
C_SIN2 = C_COS2 + N2
C_CAUSAL = C_SIN2 + N2
C_DECAY = C_CAUSAL + 3 * P
CONSTS = C_DECAY + 4 * N2
LEVELS = 7


def constants():
    c = np.zeros((P, CONSTS), np.float64)
    c[:, C_ONESD:C_ONESD + P] = 1.0 / D
    half = np.arange(P) // HD
    c[:, C_ONES64:C_ONES64 + P] = (half[:, None] == half[None, :]) / HD
    c[:, C_ONES128:C_ONES128 + P] = 1.0 / P
    c[:, C_IDENT:C_IDENT + P] = np.eye(P)
    for at, n in ((C_PERM64, HD), (C_PERM128, P)):
        for i in range(P):
            j = i + n // 2 if i % n < n // 2 else i - n // 2
            c[j, at + i] = -1.0 if i % n < n // 2 else 1.0
    jd = np.arange(HD)
    ang = 2 * np.pi * (np.outer(jd, jd) % HD) / HD
    for g in range(2):
        s = slice(g * HD, (g + 1) * HD)
        c[s, C_DFTD + g * HD:C_DFTD + (g + 1) * HD] = np.cos(ang)
        c[s, C_DFTD + P + g * HD:C_DFTD + P + (g + 1) * HD] = np.sin(ang)
    jl = np.arange(SEQ)
    ang = 2 * np.pi * (np.outer(jl, jl) % SEQ) / SEQ
    norm = 1.0 / math.sqrt(SEQ * HD)
    for t in range(2):
        rows = ang[t * P:(t + 1) * P]
        at = C_DFTL + t * 2 * SEQ
        c[:, at:at + SEQ] = np.cos(rows) * norm
        c[:, at + SEQ:at + 2 * SEQ] = -np.sin(rows) * norm
    nf = HD // 4
    inv = 10000.0 ** (-np.arange(nf, dtype=np.float64) / nf)
    tok = np.arange(SEQ)
    ang = np.concatenate([(tok // 64)[None] * inv[:, None], (tok % 64)[None] * inv[:, None]], 0)
    c[:, C_COS1:C_COS1 + SEQ] = np.tile(np.cos(ang), (4, 1))
    c[:, C_SIN1:C_SIN1 + SEQ] = np.tile(np.sin(ang), (4, 1))
    inv = 10000.0 ** (-np.arange(0, P, 2, dtype=np.float64) / P)
    ang = inv[:, None] * np.arange(N2)[None]
    c[:, C_COS2:C_COS2 + N2] = np.tile(np.cos(ang), (2, 1))
    c[:, C_SIN2:C_SIN2 + N2] = np.tile(np.sin(ang), (2, 1))
    q = np.arange(P)
    c[:, C_CAUSAL + 2 * P:C_CAUSAL + 3 * P] = np.where(q[None, :] <= q[:, None], 0.0, NEG)
    for h in range(4):
        g = math.log(1.0 - 2.0 ** (-5 - h))
        diff = np.arange(N2)[None, :] - q[:, None]
        c[:, C_DECAY + h * N2:C_DECAY + (h + 1) * N2] = np.where(
            diff >= 0, np.exp(np.maximum(diff, 0) * g), 0.0) * P ** -0.5
    return c.astype(np.float32)


def level_masks():
    i = np.arange(P)
    out = np.zeros((P, LEVELS, P), np.int32)
    for v in range(LEVELS):
        m = 1 << v
        same = (i[:, None] // (2 * m)) == (i[None, :] // (2 * m))
        out[:, v] = same & ((i[:, None] // m) != (i[None, :] // m))
    return out.reshape(P, LEVELS * P)


class Events:

    def __init__(self, table=None, banks=None):
        self.known = table or {}
        self.bank_known = banks or {}
        self.counting = table is None
        self.table, self.banks, self.count = {}, {}, {}
        self.sems = {}


def build(nc, A, old=None):
    ev = Events(*(old or (None, None)))
    ctx = ExitStack()
    with ctx:
        def sb(name, cols, dt=F32):
            return ctx.enter_context(nc.sbuf_tensor(name, [P, cols], dt))[:, :]

        def sem(name):
            return ctx.enter_context(nc.semaphore(name))

        def made(name, *key, by=1, frees=None):
            if name not in ev.sems:
                ev.sems[name] = sem(name)
            ev.count[name] = ev.count.get(name, 0) + by
            ev.table[(name, *key)] = (name, ev.count[name])
            if frees is not None:
                ev.table[("free",) + frees] = (name, ev.count[name])
            return ev.sems[name], by

        def when(name, *key):
            if ev.counting:
                return unit_used, 1
            family, value = ev.known[(name, *key)]
            if family not in ev.sems:
                ev.sems[family] = sem(family)
            return ev.sems[family], value

        def bank(*key):
            return psum[ev.bank_known.get(key, 0)]

        unit_used = sem("unit_used")

        resid = sb("resid", KC * (META + N1)).rearrange("p (c n) -> p c n", c=KC)
        xn_flat = sb("xn", KC * N1)
        hid_flat = sb("hidden", FC * N1)
        mix_flat = sb("mix", KC * N1)
        ring = sb("ring", RING * UNIT).rearrange("p (s n) -> p s n", s=RING)
        mod_ring = sb("mod_ring", MOD_RING * D).rearrange("p (s n) -> p s n", s=MOD_RING)
        csilu = sb("csilu", 2 * D).rearrange("p (s n) -> p s n", s=2)
        junk = sb("mod_products", 2 * D, mybir.dt.bfloat16).rearrange("p (s n) -> p s n", s=2)
        mod_raw = sb("mod_raw", DEPTH * 2 * NMOD * KC).rearrange("p (l s n) -> p l s n", l=DEPTH, s=2)
        mod = sb("mod", DEPTH * 2 * NMOD * KC).rearrange("p (l s n) -> p l s n", l=DEPTH, s=2)
        small = sb("small", SMALL)
        const = sb("const", CONSTS)
        masks = sb("masks", LEVELS * P, I32).rearrange("p (v n) -> p v n", v=LEVELS)
        bias = sb("na_bias", 4 * 6 * 64)
        wgate = sb("wgate", DEPTH * 2 * P).rearrange("p (l n) -> p l n", l=DEPTH)
        squares = sb("squares", 2 * N1).rearrange("p (b n) -> p b n", b=2)
        sumsq = sb("sumsq", N1)
        rstd = sb("rstd", 2 * N1).rearrange("p (b n) -> p b n", b=2)
        act_out = sb("act_out", 2 * N1).rearrange("p (b n) -> p b n", b=2)
        probs_flat = sb("probs", 2 * N1)
        probs = probs_flat.rearrange("p (b n) -> p b n", b=2)
        biased = sb("biased", 2 * N2).rearrange("p (b n) -> p b n", b=2)
        stat = sb("softmax_stats", 4 * 8).rearrange("p (b n) -> p b n", b=4)
        probs_t_flat = sb("probs_t", 2 * 4 * N2)
        probs_t = probs_t_flat.rearrange("p (b k n) -> p b k n", b=2, k=4)
        cross = probs_t_flat[:, 0:16 * P].rearrange("p (h t n) -> p h t n", t=4, h=4)
        khat = probs_flat[:, 0:4 * P].rearrange("p (t n) -> p t n", t=4)
        state = probs_flat[:, 4 * P:8 * P].rearrange("p (g n) -> p g n", g=2)
        negc = bias[:, 0:3 * N2].rearrange("p (g n) -> p g n", g=3)
        gates = sb("gates", 2 * N1).rearrange("p (g n) -> p g n", g=2)
        decay = sb("decay", 2 * 2 * N1).rearrange("p (b g n) -> p b g n", b=2, g=2)
        eps_one = sb("eps_one", 2)
        psum = [ctx.enter_context(nc.psum_tensor(f"bank{i}", [P, 512], F32))[:, :] for i in range(8)]

        xn = xn_flat.rearrange("p (c n) -> p c n", c=KC)
        xn2 = xn_flat[:, 0:KC * N2].rearrange("p (c n) -> p c n", c=KC)
        dft_ab = xn_flat[:, 0:2048].rearrange("p (s t n) -> p s t n", s=2, t=2)
        gla_s = xn_flat[:, 2048:4096].rearrange("p (h t n) -> p h t n", t=4, h=4)
        proj1 = hid_flat[:, 0:NSLOT1 * N1].rearrange("p (c n) -> p c n", c=NSLOT1)
        v1 = hid_flat[:, NSLOT1 * N1:NSLOT1 * N1 + 4 * NV1].rearrange("p (t n) -> p t n", t=4)
        proj2 = hid_flat[:, 0:NSLOT2 * N2].rearrange("p (c n) -> p c n", c=NSLOT2)
        v2 = hid_flat[:, NSLOT2 * N2:NSLOT2 * N2 + 3 * NV2].rearrange("p (t n) -> p t n", t=3)
        mix1 = mix_flat.rearrange("p (c n) -> p c n", c=KC)
        mix2 = mix_flat[:, 0:KC * N2].rearrange("p (c n) -> p c n", c=KC)

        def cst(at, n=P, rows=P):
            return const[0:rows, at:at + n]

        def hidden(n):
            return hid_flat[:, 0:FC * n].rearrange("p (c n) -> p c n", c=FC)

        def scalar1(l, name, j=0):
            at = l * SW1 + S_L1[name] + j
            return small[:, at:at + 1]

        def scalar2(l, name, j=0, rows=P):
            at = DEPTH * SW1 + l * SW2 + S_L2[name] + j
            return small[0:rows, at:at + 1]

        unit_loaded = [sem(f"unit_loaded{i}") for i in range(RING)]

        BOTH = [(0, 0, NX), (1, NX, N1)]
        ONLY_X = [(0, 0, NX)]

        def softmax_heads(l):
            out = []
            for h in range(4):
                c, po = h // 2, (h % 2) * HD
                out.append(dict(id=("nax", l, h), po=po, q=proj1[po:po + HD, NAQ + c, 0:NX],
                                k=proj1[po:po + HD, NAK + c, 0:N1], tiles=[(0, P, N1), (P, P, N1)],
                                v=[(P, v1[:, t, NAV + h * HD:NAV + (h + 1) * HD]) for t in range(4)],
                                kind="na", h=h, out=mix1[po:po + HD, 2 + c, 0:NX], n=NX))
            for h in range(4):
                c, po, kv = h // 2, (h % 2) * HD, h % 2
                out.append(dict(id=("gqax", l, h), po=po, q=proj1[po:po + HD, GQAQ + c, 0:NX],
                                k=proj1[po:po + HD, GQAK, 0:N1], tiles=[(0, P, N1), (P, P, N1)],
                                v=[(P, v1[:, t, GQAV + kv * HD:GQAV + (kv + 1) * HD]) for t in range(4)],
                                kind="plain", h=h, out=mix1[po:po + HD, 6 + c, 0:NX], n=NX))
            if l == 0:
                for h in range(4):
                    c, po = h // 2, (h % 2) * HD
                    out.append(dict(id=("naz", l, h), po=po, q=proj1[po:po + HD, NAQ + c, NX:N1],
                                    k=proj1[po:po + HD, NAK + c, NX:N1], tiles=[(0, P, NZ), (P, P, NZ)],
                                    v=[(P, v1[:, t, NAV + h * HD:NAV + (h + 1) * HD]) for t in (2, 3)],
                                    kind="plain", h=h, out=mix1[po:po + HD, 2 + c, NX:N1], n=NZ))
                for h in range(4):
                    c, po, kv = h // 2, (h % 2) * HD, h % 2
                    out.append(dict(id=("gqaz", l, h), po=po, q=proj1[po:po + HD, GQAQ + c, NX:N1],
                                    k=proj1[po:po + HD, GQAK, NX:N1], tiles=[(0, P, NZ), (P, P, NZ)],
                                    v=[(P, v1[:, t, GQAV + kv * HD:GQAV + (kv + 1) * HD]) for t in (2, 3)],
                                    kind="plain", h=h, out=mix1[po:po + HD, 6 + c, NX:N1], n=NZ))
            return out

        def fox_heads(l):
            out = []
            for h in range(8):
                c, po = h // 2, (h % 2) * HD
                out.append(dict(id=("fox", l, h), po=po, q=proj2[po:po + HD, FQ + c, :],
                                k=proj2[po:po + HD, FK + c, :],
                                tiles=[(0, P, P), (P, P, 2 * P), (2 * P, META, N2)],
                                v=[(n, v2[0:n, t, h * HD:(h + 1) * HD]) for t, (_, n) in enumerate(TILES2)],
                                kind="fox", h=h, out=mix2[po:po + HD, c, :], n=N2))
            return out

        def norm_items(l):
            nq = N1 if l == 0 else NX
            return ([(NAQ, "naq", nq), (NAQ + 1, "naq", nq), (NAK, "nak", N1), (NAK + 1, "nak", N1),
                     (GQAQ, "gqaq", nq), (GQAQ + 1, "gqaq", nq), (GQAK, "gqak", N1)])

        rope_items = [GQAQ, GQAQ + 1, GQAK]
        block = ctx.enter_context(nc.Block())

        @block.sync
        def _(sp):
            sp.dma_start(const, A["consts"]).then_inc(*made("consts_loaded", 0, by=16))
            sp.dma_start(small, A["small"]).then_inc(*made("small_loaded", 0, by=16))
            for c in range(KC):
                sp.dma_start(resid[:, c, META:META + NX], A["x"][c]).then_inc(*made("resid_loaded", c, 0, by=16))
                sp.dma_start(resid[:, c, META + NX:META + N1], A["ctx"][c]).then_inc(
                    *made("resid_loaded", c, 1, by=16))
                sp.dma_start(resid[:, c, 0:META], A["meta"][c]).then_inc(*made("resid_loaded", c, 2, by=16))
            for s in range(RING):
                sp.dma_start(ring[:, s], A["stream"][s]).then_inc(unit_loaded[s], 16)
            turns = UNITS // RING
            with sp.Fori(1, turns) as turn:
                for s in range(RING):
                    sp.wait_ge(unit_used, turn * RING + (s + 1 - RING))
                    sp.dma_start(ring[:, s], A["stream"][turn * RING + s]).then_inc(unit_loaded[s], 16)
            for u in range(turns * RING, UNITS):
                sp.wait_ge(unit_used, u - RING + 1)
                sp.dma_start(ring[:, u % RING], A["stream"][u]).then_inc(unit_loaded[u % RING], 16)
            sp.wait_ge(*when("final_norm", KC - 1))
            sp.dma_start(A["out"], xn_flat[:, 0:KC * NX]).then_inc(*made("out_stored", 0, by=16))
            sp.wait_ge(*when("out_stored", 0))

        @block.gpsimd
        def _(pool):
            pool.dma_start(masks, A["masks"].rearrange("p (v n) -> p v n", v=LEVELS)).then_inc(
                *made("masks_loaded", 0, by=16))
            pool.dma_start(csilu[:, 0, :], A["c"].broadcast_to([P, D])).then_inc(*made("c_loaded", by=16))
            pool.dma_start(csilu[:, 1, :], A["c_ctx"].broadcast_to([P, D])).then_inc(*made("c_ctx_loaded", by=16))
            pool.dma_start(wgate[0:32], A["wgate"]).then_inc(*made("wgate_loaded", 0, by=16))

            def mod_loads(l):
                for j in range(NMOD * KC):
                    n = l * NMOD * KC + j
                    if n >= MOD_RING:
                        pool.wait_ge(*when("mod_dot", n - MOD_RING))
                    pool.dma_start(mod_ring[:, n % MOD_RING], A["w_mod"][l, j]).then_inc(
                        *made(f"mod_loaded{n % MOD_RING}", n, by=16))

            def gla_exponents(l):
                streams = 2 if l == 0 else 1
                n = streams * NX
                b, c = gates[:, 0, 0:n], gates[:, 1, 0:n]
                pool.wait_ge(*when("gate_sums", l, 1, 1))
                for v in range(LEVELS + 1):
                    m = 1 << v
                    if v >= 2:
                        pool.wait_ge(*when("pairs", l, v - 2, 3))
                    bv = b.rearrange("p (k t m) -> p k t m", t=2, m=m)
                    cv = c.rearrange("p (k t m) -> p k t m", t=2, m=m)
                    dq = decay[:, v % 2, 0, 0:n].rearrange("p (k t m) -> p k t m", t=2, m=m)
                    dk = decay[:, v % 2, 1, 0:n].rearrange("p (k t m) -> p k t m", t=2, m=m)
                    shape = [P, n // (2 * m), m]
                    b_mid = bv[:, :, 0, m - 1:m].broadcast_to(shape)
                    c_mid = cv[:, :, 1, 0:1].broadcast_to(shape)
                    pool.tensor_tensor(dq[:, :, 0, :], cv[:, :, 0, :], c_mid, ALU.subtract).then_inc(
                        *made("exponents", l, v, 0))
                    pool.tensor_tensor(dq[:, :, 1, :], bv[:, :, 1, :], b_mid, ALU.subtract).then_inc(
                        *made("exponents", l, v, 1))
                    pool.tensor_tensor(dk[:, :, 0, :], b_mid, bv[:, :, 0, :], ALU.subtract).then_inc(
                        *made("exponents", l, v, 2))
                    pool.tensor_tensor(dk[:, :, 1, :], c_mid, cv[:, :, 1, :], ALU.subtract).then_inc(
                        *made("exponents", l, v, 3))

            mod_loads(0)
            for l in range(DEPTH):
                if l > 0:
                    for key in [("gqax", l - 1, 3, 1), ("nax", l - 1, 3, 1)]:
                        pool.wait_ge(*when("exps", *key))
                pool.dma_start(bias, A["na_bias"][l]).then_inc(*made("bias_loaded", l, by=16))
                gla_exponents(l)
                if l + 1 < DEPTH:
                    mod_loads(l + 1)

        @block.tensor
        def _(pe):
            taken = [0]
            bank_user = {}

            def take(*key):
                b = taken[0] % 8
                taken[0] += 1
                if b in bank_user:
                    pe.wait_ge(*when("free", *bank_user[b]))
                bank_user[b] = key
                ev.banks[key] = b
                return psum[b]

            unit = [0]

            def weights():
                u = unit[0]
                unit[0] += 1
                pe.wait_ge(unit_loaded[u % RING], 16 * (u // RING + 1))
                return u, ring[:, u % RING].rearrange("p (b n) -> p b n", b=8)

            def product(first_of_unit, *args, **kw):
                mm = pe.matmul(*args, **kw)
                if first_of_unit and unit[0] >= 2:
                    mm.then_inc(unit_used, 1)
                return mm

            def mean_square(tag, n):
                pe.wait_ge(*when("sumsq", tag, KC - 1))
                pe.matmul(take("mean", tag)[:, 0:n], cst(C_ONESD), sumsq[:, 0:n], start=True,
                          stop=True).then_inc(*made("mean", tag))

            def ffn(tag, x, n, last_in):
                hid = hidden(n)
                for f in range(FC):
                    for what in ("gate", "up"):
                        p = take(what, tag, f)
                        _, w = weights()
                        for c in range(KC):
                            if f == 0 and what == "gate":
                                for s in last_in:
                                    pe.wait_ge(*when("xn", tag, c, s))
                            mm = product(c == 0, p[:, 0:n], w[:, c], x[:, c, 0:n],
                                         start=(c == 0), stop=(c == KC - 1))
                        mm.then_inc(*made(what, tag, f))
                j = 0
                for d in range(KC):
                    p = take("down", tag, d)
                    for f in range(FC):
                        if j % 8 == 0:
                            _, w = weights()
                        if d == 0:
                            pe.wait_ge(*when("hidden", tag, f))
                        mm = product(j % 8 == 0, p[:, 0:n], w[:, j % 8], hid[:, f, :],
                                     start=(f == 0), stop=(f == FC - 1))
                        j += 1
                    mm.then_inc(*made("down", tag, d))

            def project(tag, plan, x, l, n_of, vtiles, streams):
                for i, item in enumerate(plan):
                    kind, dst, width = item[:3]
                    _, w = weights()
                    p = take("proj", tag, i)
                    if kind == "T":
                        n = n_of(item)
                        for c in range(KC):
                            if i == 0:
                                for s in streams:
                                    pe.wait_ge(*when("xn", tag, c, s))
                            mm = product(c == 0, p[0:width, 0:n], w[:, c, 0:width], x[:, c, 0:n],
                                         start=(c == 0), stop=(c == KC - 1))
                    else:
                        for t, (t0, tn) in enumerate(vtiles):
                            for c in range(KC):
                                mm = product(c == 0 and t == 0, p[0:tn, t * P:(t + 1) * P],
                                             x[:, c, t0:t0 + tn], w[:, c, :],
                                             start=(c == 0), stop=(c == KC - 1))
                    mm.then_inc(*made("proj", tag, i))

            def project_out(tag, m, n, ready):
                for key in ready:
                    pe.wait_ge(*when(*key))
                for d in range(KC):
                    _, w = weights()
                    p = take("down", tag, d)
                    for c in range(KC):
                        mm = product(c == 0, p[:, 0:n], w[:, c], m[:, c, 0:n],
                                     start=(c == 0), stop=(c == KC - 1))
                    mm.then_inc(*made("down", tag, d))

            def fourier(l):
                streams = BOTH if l == 0 else ONLY_X
                pe.wait_ge(*when("consts_loaded", 0))
                for s, s0, _ in streams:
                    for t in range(2):
                        p = take("dft_d", l, s, t)
                        for g in range(2):
                            pe.wait_ge(*when("projected", ("mix1", l), g))
                            mm = pe.matmul(p[:, g * 2 * P:(g + 1) * 2 * P],
                                           proj1[:, FOUR + g, s0 + t * P:s0 + (t + 1) * P],
                                           cst(C_DFTD, 2 * P), start=True, stop=True)
                        mm.then_inc(*made("dft_d", l, s, t))
                for s, _, _ in streams:
                    p = take("dft_l", l, s)
                    for t in range(2):
                        pe.wait_ge(*when("dft_ab", l, s, t))
                    for g in range(2):
                        n = 0
                        for t in range(2):
                            for part in range(2):
                                mm = pe.matmul(p[:, g * SEQ:(g + 1) * SEQ],
                                               dft_ab[:, s, t, (2 * g + part) * P:(2 * g + part + 1) * P],
                                               cst(C_DFTL + (2 * t + part) * SEQ, SEQ),
                                               start=(n == 0), stop=(n == 3))
                                n += 1
                    mm.then_inc(*made("dft_l", l, s))

            def head_means(tag, items):
                for i, item in enumerate(items):
                    pe.wait_ge(*when("head_squares", tag, i))
                    pe.matmul(take("head_mean", tag, i)[:, 0:item[2]], cst(C_ONES64),
                              squares[:, i % 2, 0:item[2]], start=True, stop=True).then_inc(
                                  *made("head_mean", tag, i))

            def rotations(l, items, src, at, n, done):
                for i, slot in enumerate(items):
                    pe.wait_ge(*when(*done(i)))
                    pe.matmul(take("rotated", l, i)[:, 0:n], cst(at), src[:, slot, 0:n],
                              start=True, stop=True).then_inc(*made("rotated", l, i))

            def attention(heads, ready):
                tiles = [(hd, j) for hd in heads for j in range(len(hd["tiles"]))]

                def scores(i):
                    hd, j = tiles[i]
                    q0, nq, nk = hd["tiles"][j]
                    for key in ready(hd):
                        pe.wait_ge(*when(*key))
                    p = take("scores", *hd["id"], j)
                    fox = hd["kind"] == "fox"
                    mm = pe.matmul(p[0:nq, 0:nk], hd["q"][:, q0:q0 + nq], hd["k"][:, 0:nk],
                                   start=True, stop=not fox)
                    if fox:
                        mm = pe.matmul(p[0:nq, 0:nk], const[0:8, C_IDENT + hd["h"]:C_IDENT + hd["h"] + 1].broadcast_to([8, nq]),
                                       negc[0:8, 2, 0:nk], start=False, stop=True)
                    mm.then_inc(*made("scores", *hd["id"], j))

                def transposes(i):
                    hd, j = tiles[i]
                    _, nq, nk = hd["tiles"][j]
                    pe.wait_ge(*when("probs", *hd["id"], j))
                    p = take("turned", *hd["id"], j)
                    for kt in range((nk + P - 1) // P):
                        rows = min(P, nk - kt * P)
                        mm = pe.transpose(p[0:rows, kt * P:kt * P + nq],
                                          probs[0:nq, i % 2, kt * P:kt * P + rows], cst(C_IDENT, nq, nq))
                    mm.then_inc(*made("turned", *hd["id"], j))

                def values(hi):
                    hd = heads[hi]
                    for j in range(len(hd["tiles"])):
                        pe.wait_ge(*when("probs_t", *hd["id"], j))
                    p = take("attended", *hd["id"])
                    po, n = hd["po"], hd["n"]
                    for kt, (rows, v) in enumerate(hd["v"]):
                        q0 = kt * P if hd["kind"] == "fox" else 0
                        mm = pe.matmul(p[po:po + HD, q0:n], v, probs_t[0:rows, hi % 2, kt, q0:n],
                                       start=(kt == 0), stop=(kt == len(hd["v"]) - 1))
                    mm.then_inc(*made("attended", *hd["id"]))

                scores(0)
                hi = 0
                for i, (hd, j) in enumerate(tiles):
                    if i + 1 < len(tiles):
                        scores(i + 1)
                    transposes(i)
                    if j == len(hd["tiles"]) - 1:
                        values(hi)
                        hi += 1

            def gla(l):
                streams = BOTH if l == 0 else ONLY_X
                ntile = 2 * len(streams)
                pe.wait_ge(*when("wgate_loaded", 0))
                pe.wait_ge(*when("projected", ("mix1", l), 14))
                for g in range(2):
                    pe.matmul(take("gate_in", l, g), wgate[0:32, l, g * P:(g + 1) * P],
                              proj1[0:32, GATE, 0:N1], start=True, stop=True).then_inc(*made("gate_in", l, g))

                def pairs(v):
                    ps = [take("pairs", l, v, h) for h in range(4)]
                    for t in range(ntile):
                        other = t ^ 1 if v == LEVELS else t
                        for h in range(4):
                            r = slice(32 * h, 32 * h + 32)
                            if v < 0:
                                q, k = proj1[r, GLAQ], proj1[r, GLAK]
                            else:
                                q, k = decay[r, v % 2, 0], decay[r, v % 2, 1]
                            mm = pe.matmul(ps[h][:, t * P:(t + 1) * P], k[:, t * P:(t + 1) * P],
                                           q[:, other * P:(other + 1) * P], start=True, stop=True,
                                           skip_group_check=True)
                            if t == ntile - 1:
                                mm.then_inc(*made("pairs", l, v, h))

                for i in (8, 9):
                    pe.wait_ge(*when("projected", ("mix1", l), i))
                pairs(-1)
                pe.wait_ge(*when("khat_t", l))
                p = take("khat", l)
                for g in range(2):
                    for t in range(2):
                        mm = pe.transpose(p[:, (2 * g + t) * P:(2 * g + t + 1) * P],
                                          act_out[:, 0, g * NZ + t * P:g * NZ + (t + 1) * P], cst(C_IDENT))
                mm.then_inc(*made("khat", l))
                pe.wait_ge(*when("khat_sb", l))
                for i in (10, 11):
                    pe.wait_ge(*when("projected", ("mix1", l), i))
                p = take("state", l)
                for g in range(2):
                    for t in range(2):
                        mm = pe.matmul(p[:, g * SEQ:(g + 1) * SEQ], khat[:, 2 * g + t],
                                       v1[:, 2 + t, GLAV:GLAV + 256], start=(t == 0), stop=(t == 1))
                mm.then_inc(*made("state", l))
                for v in range(LEVELS + 1):
                    pe.wait_ge(*when("decayed", l, v))
                    pairs(v)
                pe.wait_ge(*when("state_sb", l))
                pe.wait_ge(*when("q_from_start", l))
                for h in range(4):
                    pe.wait_ge(*when("gla_scores", l, LEVELS - 1, h))
                    pe.wait_ge(*when("gla_cross", l, h))
                for s, s0, _ in streams:
                    for h in range(4):
                        po = (h % 2) * HD
                        p = take("gla_out", l, s, h)
                        vcol = slice(GLAV + h * HD, GLAV + (h + 1) * HD)
                        for i in range(2):
                            out = p[po:po + HD, i * P:(i + 1) * P]
                            t, u = 2 * s + i, 2 * s + 1 - i
                            pe.matmul(out, v1[:, t, vcol], gla_s[:, h, t], start=True, stop=False)
                            mm = pe.matmul(out, v1[:, u, vcol], cross[:, h, u], start=False, stop=(s == 1))
                            if s == 0:
                                r = slice(32 * h, 32 * h + 32)
                                for g in range(2):
                                    mm = pe.matmul(out, state[r, g, h * HD:(h + 1) * HD],
                                                   act_out[r, 1, g * NX + i * P:g * NX + (i + 1) * P],
                                                   start=False, stop=(g == 1))
                        mm.then_inc(*made("gla_out", l, s, h))

            def retention(l):
                for h in range(4):
                    pe.wait_ge(*when("roped", ("b2", l), h))
                    pe.wait_ge(*when("roped", ("b2", l), 4 + h))
                    p = take("ret_pairs", l, h)
                    at = 0
                    for j, (t0, tn) in enumerate(TILES2):
                        mm = pe.matmul(p[0:tn, at:at + N2 - t0], proj2[:, RK + h, t0:t0 + tn],
                                       proj2[:, RQ + h, t0:N2], start=True, stop=True,
                                       skip_group_check=True)
                        at += N2 - t0
                    mm.then_inc(*made("ret_pairs", l, h))
                    if h >= 1:
                        ret_values(l, h - 1)
                ret_values(l, 3)
                for h in range(4):
                    pe.wait_ge(*when("ret_sb", l, h))
                    pe.matmul(take("ret_mean", l, h)[:, 0:N2], cst(C_ONES128), mix2[:, 4 + h, :],
                              start=True, stop=True).then_inc(*made("ret_mean", l, h))
                for h in range(4):
                    pe.wait_ge(*when("ret_squares", l, h))
                    pe.matmul(take("ret_var", l, h)[:, 0:N2], cst(C_ONES128), squares[:, h % 2, 0:N2],
                              start=True, stop=True).then_inc(*made("ret_var", l, h))

            def ret_values(l, h):
                p = take("ret_out", l, h)
                for j, (t0, tn) in enumerate(TILES2):
                    pe.wait_ge(*when("ret_decayed", l, h, j))
                    mm = pe.matmul(p[:, t0:N2], v2[0:tn, j, 512 + h * P:512 + (h + 1) * P],
                                   probs_t[0:tn, h % 2, j, t0:N2], start=(j == 0), stop=(j == 2))
                mm.then_inc(*made("ret_out", l, h))

            pe.wait_ge(*when("consts_loaded", 0))
            mean_square(("start",), N1)
            for l in range(DEPTH):
                t1, tm, to, t2 = ("ffn1", l), ("mix1", l), ("out1", l), ("ffn2", l)
                ffn(t1, xn, N1, [0, 1])
                mean_square(t1, N1)
                project(tm, PROJ1, xn, l, lambda it: N1 if (l == 0 or it[3]) else NX,
                        [(t * P, P) for t in range(4)], [0, 1])
                fourier(l)
                head_means(tm, norm_items(l))
                rotations(l, rope_items, proj1, C_PERM64, NX, lambda i: ("head_normed", tm, 4 + i))
                gla(l)
                attention(softmax_heads(l), lambda hd: [("roped", tm, 2), ("projected", tm, 18),
                                                        ("projected", tm, 7)])
                n = N1 if l == 0 else NX
                head_means(("gla", l), [(0, 0, n), (1, 0, n)])
                project_out(to, mix1, n, [("mix_gla", l, 1), ("mix_done", l), ("dft_mix", l, 1 if l == 0 else 0)])
                mean_square(to, n)
                ffn(t2, xn, n, [0, 1] if l == 0 else [0])
                mean_square(t2, n if l == 0 else N2)
            for l in range(DEPTH):
                tp, to, tf = ("b2", l), ("out2", l), ("ffn", l)
                project(tp, PROJ2, xn2, l, lambda it: N2, TILES2, [0])
                rotations(("b2", l), [RQ, RQ + 1, RQ + 2, RQ + 3, RK, RK + 1, RK + 2, RK + 3], proj2,
                          C_PERM128, N2, lambda i: ("projected", tp, 13 + i))
                attention(fox_heads(l), lambda hd: [("negc", l), ("projected", tp, 11), ("projected", tp, 10),
                                                    ("projected", tp, 7), ("projected", tp, 6)])
                retention(l)
                project_out(to, mix2, N2, [("mix_ret", l, 3), ("mix_done", ("b2", l))])
                mean_square(to, N2)
                ffn(tf, xn2, N2, [0])
                mean_square(tf, N2)
            assert unit[0] == UNITS

        @block.scalar
        def _(act):
            def ln_exp():
                act.preload_act_table_set(LN_EXP)

            def inverse_root(out, p, n, tag, frees):
                act.activation(out[:, 0:n], p[:, 0:n], ACT.Ln, bias=eps_one[:, 0:1]).then_inc(
                    *made("ln_mean", tag, frees=frees))
                act.wait_ge(*when("ln_mean", tag))
                act.activation(out[:, 0:n], out[:, 0:n], ACT.Exp, scale=-0.5).then_inc(*made("rstd", tag))

            def squares_of(tag, cols, n, ready):
                for d in range(KC):
                    ready(d)
                    out = sumsq[:, 0:n] if d == 0 else squares[:, d % 2, 0:n]
                    if d >= 3:
                        act.wait_ge(*when("sumsq", tag, d - 2))
                    act.activation(out, resid[:, d, cols:cols + n], ACT.Square).then_inc(
                        *made("resid_squares", tag, d))

            def norm(tag, to, l, m, streams, n):
                ln_exp()
                act.wait_ge(*when("mean", tag))
                p = bank("mean", tag)
                inverse_root(rstd[:, 0], p, n, tag, ("mean", tag))
                for c in range(KC):
                    act.wait_ge(*when("scaled", to, c))
                    act.activation(xn[:, c, 0:NX], act_out[:, c % 2, 0:NX], ACT.Identity,
                                   bias=mod[:, l, 0, m * KC + c:m * KC + c + 1],
                                   scale=mod[:, l, 0, (m + 1) * KC + c:(m + 1) * KC + c + 1]).then_inc(
                                       *made("xn_x", to, c))

            def ffn(tag, n):
                for f in range(FC):
                    act.wait_ge(*when("gate", tag, f))
                    p = bank("gate", tag, f)
                    if f >= 2:
                        act.wait_ge(*when("hidden", tag, f - 2))
                    act.activation(act_out[:, f % 2, 0:n], p[:, 0:n], ACT.Silu).then_inc(
                        *made("silu", tag, f, frees=("gate", tag, f)))

            def projections(tag, plan, n_of, dst_of, l):
                for i, item in enumerate(plan):
                    if i % 2:
                        continue
                    kind, dst, width = item[:3]
                    act.wait_ge(*when("proj", tag, i))
                    p = bank("proj", tag, i)
                    if kind == "T":
                        scale = 1.0
                        if tag[0] == "mix1" and dst == GLAQ:
                            scale = 32 ** -0.5
                        if tag[0] == "b2" and FQ <= dst < FQ + 4:
                            scale = HD ** -0.5
                        n = n_of(item)
                        act.activation(dst_of(dst, width, n), p[0:width, 0:n], ACT.Copy, scale=scale).then_inc(
                            *made("projected_act", tag, i, frees=("proj", tag, i)))
                    else:
                        src = p.rearrange("p (t n) -> p t n", t=4)
                        if tag[0] == "mix1":
                            act.activation(v1[:, :, dst:dst + P], src, ACT.Copy).then_inc(
                                *made("projected_act", tag, i, frees=("proj", tag, i)))
                        else:
                            act.activation(v2[:, 0:2, dst:dst + P], src[:, 0:2], ACT.Copy)
                            act.activation(v2[0:META, 2, dst:dst + P], src[0:META, 2], ACT.Copy).then_inc(
                                *made("projected_act", tag, i, frees=("proj", tag, i)))
                    ev.table[("projected", tag, i)] = ev.table[("projected_act", tag, i)]

            def head_norms(tag, items, src):
                def square(i):
                    src_ap, n = src(items[i]), items[i][2]
                    if tag[0] == "mix1":
                        act.wait_ge(*when("projected", tag, slot_unit[items[i][0]]))
                    else:
                        act.wait_ge(*when("gla_sb", tag[1], items[i][0]))
                    if i >= 2:
                        act.wait_ge(*when("head_mean", tag, i - 2))
                    act.activation(squares[:, i % 2, 0:n], src_ap, ACT.Square).then_inc(
                        *made("head_squares", tag, i))
                square(0)
                for i, item in enumerate(items):
                    if i + 1 < len(items):
                        square(i + 1)
                    act.wait_ge(*when("head_mean", tag, i))
                    p = bank("head_mean", tag, i)
                    if i >= 2:
                        act.wait_ge(*when("head_normed", tag, i - 2))
                    inverse_root(rstd[:, i % 2], p, item[2], (tag, i), ("head_mean", tag, i))

            def attention(heads):
                i = 0
                for hi, hd in enumerate(heads):
                    for j, (q0, nq, nk) in enumerate(hd["tiles"]):
                        key = (*hd["id"], j)
                        st = stat[0:nq, i % 4]
                        act.wait_ge(*when("row_max", *key))
                        if i >= 2:
                            act.wait_ge(*when("turned", *prev2[1]))
                        out = probs[0:nq, i % 2]
                        if hd["kind"] == "na":
                            act.wait_ge(*when("scores", *key))
                            p = bank("scores", *key)
                            act.activation(out[:, 0:NX], biased[:, i % 2, 0:NX], ACT.Exp, bias=st[:, 3:4],
                                           accum_out=st[:, 4:5])
                            act.activation(out[:, NX:N1], p[:, NX:N1], ACT.Exp, bias=st[:, 3:4],
                                           accum_out=st[:, 5:6]).then_inc(*made("exps", *key, frees=("scores", *key)))
                        elif hd["kind"] == "fox":
                            act.activation(out[:, 0:nk], biased[0:nq, i % 2, 0:nk], ACT.Exp, bias=st[:, 3:4],
                                           accum_out=st[:, 4:5]).then_inc(*made("exps", *key))
                        else:
                            act.wait_ge(*when("scores", *key))
                            p = bank("scores", *key)
                            act.activation(out[:, 0:nk], p[:, 0:nk], ACT.Exp, bias=st[:, 3:4],
                                           accum_out=st[:, 4:5]).then_inc(*made("exps", *key, frees=("scores", *key)))
                        prev2 = (key, prev2[0]) if i else (key, None)
                        if i >= 1:
                            turned(heads, pend)
                        pend = (hi, j)
                        i += 1
                turned(heads, pend)

            def turned(heads, at):
                hi, j = at
                hd = heads[hi]
                q0, nq, nk = hd["tiles"][j]
                key = (*hd["id"], j)
                act.wait_ge(*when("turned", *key))
                p = bank("turned", *key)
                if hi >= 2 and j == 0:
                    act.wait_ge(*when("attended", *heads[hi - 2]["id"]))
                full = nk // P
                src = p.rearrange("p (k n) -> p k n", k=4)
                last = act.activation(probs_t[:, hi % 2, 0:full, q0:q0 + nq], src[:, 0:full, 0:nq], ACT.Copy)
                if nk % P:
                    last = act.activation(probs_t[0:nk % P, hi % 2, full, q0:q0 + nq],
                                          src[0:nk % P, full, 0:nq], ACT.Copy)
                last.then_inc(*made("probs_t", *key, frees=("turned", *key)))

            def gla_gates(l):
                for g in range(2):
                    act.wait_ge(*when("neg_abs", l, g))
                    act.activation(decay[:, 0, g], decay[:, 0, g], ACT.Exp).then_inc(*made("gate_exp", l, g))
                    act.wait_ge(*when("gate_exp", l, g))
                    act.activation(decay[:, 0, g], decay[:, 0, g], ACT.Ln, bias=eps_one[:, 1:2]).then_inc(
                        *made("gate_ln", l, g))
                act.wait_ge(*when("z_exponents", l, 1))
                act.activation(act_out[:, 0, :], act_out[:, 0, :], ACT.Exp, scale=1.0 / 16).then_inc(
                    *made("z_decays", l))
                act.wait_ge(*when("gate_sums", l, 1, 1))
                for g in range(2):
                    act.activation(act_out[:, 1, g * NX:(g + 1) * NX], gates[:, g, 0:NX], ACT.Exp,
                                   scale=1.0 / 16).then_inc(*made("x_decays", l, g))

            def gla_levels(l):
                n = N1 if l == 0 else NX
                act.wait_ge(*when("khat", l))
                p = bank("khat", l)
                act.activation(khat, p.rearrange("p (t n) -> p t n", t=4), ACT.Copy).then_inc(
                    *made("khat_sb", l, frees=("khat", l)))
                act.wait_ge(*when("state", l))
                p = bank("state", l)
                act.activation(state, p.rearrange("p (g n) -> p g n", g=2), ACT.Copy).then_inc(
                    *made("state_sb", l, frees=("state", l)))
                for v in range(LEVELS + 1):
                    act.wait_ge(*when("exponents", l, v, 3))
                    act.activation(decay[:, v % 2, :, 0:n], decay[:, v % 2, :, 0:n], ACT.Exp,
                                   scale=1.0 / 16).then_inc(*made("decays", l, v))
                for h in range(4):
                    act.wait_ge(*when("pairs", l, LEVELS, h))
                    p = bank("pairs", l, LEVELS, h)
                    act.activation(cross[:, h, 0:n // P], p[:, 0:n].rearrange("p (t n) -> p t n", n=P),
                                   ACT.Copy).then_inc(*made("gla_cross", l, h, frees=("pairs", l, LEVELS, h)))

            def silu_gates(tag, slots, src, n, units):
                for i, slot in enumerate(slots):
                    act.wait_ge(*when("projected", tag, units[i]))
                    act.activation(src[:, slot, 0:n], src[:, slot, 0:n], ACT.Silu).then_inc(
                        *made("silu_gate", tag, i))

            def retention(l):
                for h in range(4):
                    act.wait_ge(*when("ret_out", l, h))
                    p = bank("ret_out", l, h)
                    act.activation(mix2[:, 4 + h, :], p[:, 0:N2], ACT.Copy).then_inc(
                        *made("ret_sb", l, h, frees=("ret_out", l, h)))
                for h in range(4):
                    act.wait_ge(*when("ret_centred", l, h))
                    if h >= 2:
                        act.wait_ge(*when("ret_var", l, h - 2))
                    act.activation(squares[:, h % 2, 0:N2], mix2[:, 4 + h, :], ACT.Square).then_inc(
                        *made("ret_squares", l, h))
                    if h >= 1:
                        ret_root(l, h - 1)
                ret_root(l, 3)

            def ret_root(l, h):
                act.wait_ge(*when("ret_var", l, h))
                p = bank("ret_var", l, h)
                if h >= 2:
                    act.wait_ge(*when("ret_normed", l, h - 2))
                inverse_root(rstd[:, h % 2], p, N2, ("ret", l, h), ("ret_var", l, h))

            slot_unit = {item[1]: i for i, item in enumerate(PROJ1) if item[0] == "T"}

            for s in range(2):
                act.wait_ge(*when("c_ctx_loaded" if s else "c_loaded"))
                act.activation(csilu[:, s], csilu[:, s], ACT.Silu).then_inc(*made("c_silu", s))
            act.wait_ge(*when("eps_one", 1))
            squares_of(("start",), META, N1,
                       lambda d: [act.wait_ge(*when("resid_loaded", c, k)) for c, k in [(KC - 1, 2)]])
            norm(("start",), ("ffn1", 0), 0, 0, 2, N1)
            for l in range(DEPTH):
                t1, tm, to, t2 = ("ffn1", l), ("mix1", l), ("out1", l), ("ffn2", l)
                n = N1 if l == 0 else NX
                ffn(t1, N1)
                squares_of(t1, META, N1, lambda d: act.wait_ge(*when("resid", t1, d)))
                norm(t1, tm, l, 3, 2, N1)
                projections(tm, PROJ1, lambda it: N1 if (l == 0 or it[3]) else NX,
                            lambda dst, width, nn: proj1[0:width, dst, 0:nn], l)
                head_norms(tm, norm_items(l), lambda it: proj1[:, it[0], 0:it[2]])
                gla_gates(l)
                gla_levels(l)
                attention(softmax_heads(l))
                head_norms(("gla", l), [(0, 0, n), (1, 0, n)], lambda it: mix1[:, 4 + it[0], 0:it[2]])
                silu_gates(tm, [GLAR, GLAR + 1], proj1, n, [12, 13])
                squares_of(to, META, n, lambda d: act.wait_ge(*when("resid", to, d)))
                norm(to, t2, l, 6, 2 if l == 0 else 1, n)
                ffn(t2, n)
                if l == 0:
                    squares_of(t2, META, n, lambda d: act.wait_ge(*when("resid", t2, d)))
                    norm(t2, ("ffn1", 1), 1, 0, 2, N1)
                else:
                    squares_of(t2, 0, N2, lambda d: act.wait_ge(*when("resid", t2, d)))
                    ln_exp()
                    act.wait_ge(*when("mean", t2))
                    p = bank("mean", t2)
                    inverse_root(rstd[:, 0], p, N2, t2, ("mean", t2))
            for l in range(DEPTH):
                tp, to, tf = ("b2", l), ("out2", l), ("ffn", l)
                projections(tp, PROJ2, lambda it: N2,
                            lambda dst, width, nn: (negc[0:8, 0, :] if dst == FLOG else proj2[0:width, dst, 0:nn]), l)
                act.wait_ge(*when("flog_neg_abs", l))
                act.activation(negc[0:8, 1, :], negc[0:8, 1, :], ACT.Exp).then_inc(*made("flog_exp", l))
                act.wait_ge(*when("flog_exp", l))
                act.activation(negc[0:8, 1, :], negc[0:8, 1, :], ACT.Ln, bias=eps_one[0:8, 1:2]).then_inc(
                    *made("flog_ln", l))
                attention(fox_heads(l))
                retention(l)
                silu_gates(tp, [RG, RG + 1, RG + 2, RG + 3], proj2, N2, [25, 26, 27, 28])
                squares_of(to, 0, N2, lambda d: act.wait_ge(*when("resid", to, d)))
                ln_exp()
                act.wait_ge(*when("mean", to))
                p = bank("mean", to)
                inverse_root(rstd[:, 0], p, N2, to, ("mean", to))
                ffn(tf, N2)
                squares_of(tf, 0, N2, lambda d: act.wait_ge(*when("resid", tf, d)))
                ln_exp()
                act.wait_ge(*when("mean", tf))
                p = bank("mean", tf)
                inverse_root(rstd[:, 0], p, N2, tf, ("mean", tf))

        @block.vector
        def _(dve):
            def mod_dot(l, j):
                n = l * NMOD * KC + j
                streams = 1 if (l == 1 and j >= 5 * KC) else 2
                dve.wait_ge(*when(f"mod_loaded{n % MOD_RING}", n))
                for s in range(streams):
                    dve.wait_ge(*when("c_silu", s))
                    if dots[s] is not None:
                        dve.wait_ge(*when(*dots[s]))
                    dots[s] = ("mod_dot", n) if s == streams - 1 else ("mod_dot0", n)
                    dve.tensor_tensor_reduce(junk[:, s], mod_ring[:, n % MOD_RING], csilu[:, s], 1.0, 0.0,
                                             ALU.mult, ALU.add, mod_raw[:, l, s, j:j + 1]).then_inc(*made(*dots[s]))
                if j % KC == KC - 1:
                    mod_finish(l, j // KC, streams)

            dots = [None, None]

            def mod_finish(l, m, streams):
                cols = slice(m * KC, (m + 1) * KC)
                dve.wait_ge(*when("mod_dot", l * NMOD * KC + m * KC + KC - 1))
                dve.wait_ge(*when("small_loaded", 0))
                at = l * SW1 + S_L1["bmod"] + m * KC
                b = small[:, at:at + KC].unsqueeze(1).broadcast_to([P, streams, KC])
                add = 1.0 if m in (1, 4, 7) else 0.0
                dve.scalar_tensor_tensor(mod[:, l, 0:streams, cols], mod_raw[:, l, 0:streams, cols], add, b,
                                         ALU.add, ALU.add).then_inc(*made("mod_sum", l, m))
                dve.wait_ge(*when("mod_sum", l, m))
                half = 0.5 if m in (2, 8) else 1.0
                dve.tensor_scalar(mod[:, l, 0:streams, cols], mod[:, l, 0:streams, cols], half, None,
                                  ALU.mult).then_inc(*made("mod", l, m))

            def sum_squares(tag, n, d):
                if d == 0:
                    dve.wait_ge(*when("resid_squares", tag, 0))
                    return
                dve.wait_ge(*when("resid_squares", tag, d))
                if d >= 2:
                    dve.wait_ge(*when("sumsq", tag, d - 1))
                dve.tensor_tensor(sumsq[:, 0:n], sumsq[:, 0:n], squares[:, d % 2, 0:n], ALU.add).then_inc(
                    *made("sumsq", tag, d))

            def norm1(tag, to, l, m, n, z):
                dve.wait_ge(*when("mod", l, m))
                dve.wait_ge(*when("mod", l, m + 1))
                dve.wait_ge(*when("rstd", tag))
                for c in range(KC):
                    if c >= 2:
                        dve.wait_ge(*when("xn_x", to, c - 2))
                        if z:
                            dve.wait_ge(*when("xn_z", to, c - 2))
                    dve.tensor_tensor(act_out[:, c % 2, 0:n], resid[:, c, META:META + n], rstd[:, 0, 0:n],
                                      ALU.mult).then_inc(*made("scaled", to, c))
                    if z:
                        dve.wait_ge(*when("scaled", to, c))
                        dve.tensor_scalar(xn[:, c, NX:N1], act_out[:, c % 2, NX:N1],
                                          mod[:, l, 1, (m + 1) * KC + c:(m + 1) * KC + c + 1],
                                          mod[:, l, 1, m * KC + c:m * KC + c + 1],
                                          ALU.mult, ALU.add).then_inc(*made("xn_z", to, c))
                for c in range(KC):
                    ev.table[("xn", to, c, 0)] = ev.table[("xn_x", to, c)]
                    if z:
                        ev.table[("xn", to, c, 1)] = ev.table[("xn_z", to, c)]

            def norm2(tag, to, gain, out, cols, n, name="xn_2"):
                dve.wait_ge(*when("rstd", tag))
                for c in range(KC):
                    dve.scalar_tensor_tensor(out[:, c, 0:n], resid[:, c, cols:cols + n], gain(c),
                                             rstd[:, 0, cols:cols + n], ALU.mult, ALU.mult).then_inc(
                                                 *(made(name, to, c) if name == "xn_2" else made(name, c)))
                    if name == "xn_2":
                        ev.table[("xn", to, c, 0)] = ev.table[("xn_2", to, c)]

            def hidden_product(tag, hid, f, n):
                dve.wait_ge(*when("up", tag, f))
                p = bank("up", tag, f)
                dve.wait_ge(*when("silu", tag, f))
                dve.tensor_tensor(hid[:, f, :], act_out[:, f % 2, 0:n], p[:, 0:n], ALU.mult).then_inc(
                    *made("hidden", tag, f, frees=("up", tag, f)))

            def residual(tag, l, m, streams, n, cols, nsq):
                for d in range(KC):
                    dve.wait_ge(*when("down", tag, d))
                    p = bank("down", tag, d)
                    if m is None:
                        last = dve.tensor_tensor(resid[:, d, cols:cols + n], resid[:, d, cols:cols + n], p[:, 0:n],
                                                 ALU.add)
                    else:
                        dve.wait_ge(*when("mod", l, m))
                        for s, a, b in streams:
                            last = dve.scalar_tensor_tensor(resid[:, d, META + a:META + b], p[:, a:b],
                                                            mod[:, l, s, m * KC + d:m * KC + d + 1],
                                                            resid[:, d, META + a:META + b], ALU.mult, ALU.add)
                    last.then_inc(*made("resid", tag, d, frees=("down", tag, d)))
                    if d >= 1:
                        sum_squares(tag, nsq, d - 1)
                sum_squares(tag, nsq, KC - 1)

            def projections(tag, plan, n_of, dst_of):
                for i, item in enumerate(plan):
                    if i % 2 == 0:
                        continue
                    kind, dst, width = item[:3]
                    dve.wait_ge(*when("proj", tag, i))
                    p = bank("proj", tag, i)
                    if kind == "T":
                        n = n_of(item)
                        if tag[0] == "b2" and FQ <= dst < FQ + 4:
                            last = dve.tensor_scalar(dst_of(dst, width, n), p[0:width, 0:n], HD ** -0.5, None, ALU.mult)
                        else:
                            last = dve.tensor_copy(dst_of(dst, width, n), p[0:width, 0:n])
                    else:
                        src = p.rearrange("p (t n) -> p t n", t=4)
                        if tag[0] == "mix1":
                            last = dve.tensor_copy(v1[:, :, dst:dst + P], src)
                        else:
                            dve.tensor_copy(v2[:, 0:2, dst:dst + P], src[:, 0:2])
                            last = dve.tensor_copy(v2[0:META, 2, dst:dst + P], src[0:META, 2])
                    last.then_inc(*made("projected_dve", tag, i, frees=("proj", tag, i)))
                    ev.table[("projected", tag, i)] = ev.table[("projected_dve", tag, i)]

            def fourier(l):
                streams = BOTH if l == 0 else ONLY_X
                for s, _, _ in streams:
                    for t in range(2):
                        dve.wait_ge(*when("dft_d", l, s, t))
                        p = bank("dft_d", l, s, t)
                        dve.tensor_copy(dft_ab[:, s, t], p).then_inc(*made("dft_ab", l, s, t, frees=("dft_d", l, s, t)))
                for s, s0, s1 in streams:
                    dve.wait_ge(*when("dft_l", l, s))
                    p = bank("dft_l", l, s)
                    dve.tensor_copy(mix1[:, 0:2, s0:s1], p.rearrange("p (g n) -> p g n", g=2)).then_inc(
                        *made("dft_mix", l, s, frees=("dft_l", l, s)))

            def head_norms(tag, items, src, gain):
                for i, item in enumerate(items):
                    dve.wait_ge(*when("rstd", (tag, i)))
                    ap = src(item)
                    if tag[0] == "mix1":
                        dve.wait_ge(*when("projected", tag, slot_unit[item[0]]))
                    dve.scalar_tensor_tensor(ap, ap, gain(item), rstd[:, i % 2, 0:item[2]], ALU.mult,
                                             ALU.mult).then_inc(*made("head_normed", tag, i))

            slot_unit = {item[1]: i for i, item in enumerate(PROJ1) if item[0] == "T"}

            def rope(l, items, src, cos, sin, n, tag):
                for i, slot in enumerate(items):
                    x = src[:, slot, 0:n]
                    dve.wait_ge(*when("rotated", l, i))
                    p = bank("rotated", l, i)
                    if i >= 1:
                        dve.wait_ge(*when("roped", tag, i - 1))
                    if tag[0] == "b2":
                        dve.wait_ge(*when("projected", tag, 13 + i))
                    else:
                        dve.wait_ge(*when("head_normed", tag, 4 + i))
                    dve.tensor_tensor(biased[:, 0, 0:n], p[:, 0:n], cst(sin, n), ALU.mult).then_inc(
                        *made("rope_sin", tag, i, frees=("rotated", l, i)))
                    dve.tensor_tensor(biased[:, 1, 0:n], x, cst(cos, n), ALU.mult).then_inc(*made("rope_cos", tag, i))
                    dve.wait_ge(*when("rope_cos", tag, i))
                    dve.tensor_tensor(x, biased[:, 0, 0:n], biased[:, 1, 0:n], ALU.add).then_inc(*made("roped", tag, i))

            def attention(heads):
                tiles = [(hi, j) for hi, hd in enumerate(heads) for j in range(len(hd["tiles"]))]

                def maxima(i):
                    hi, j = tiles[i]
                    hd = heads[hi]
                    q0, nq, nk = hd["tiles"][j]
                    key = (*hd["id"], j)
                    st = stat[0:nq, i % 4]
                    dve.wait_ge(*when("scores", *key))
                    p = bank("scores", *key)
                    if i >= 2:
                        h2, j2 = tiles[i - 2]
                        dve.wait_ge(*when("exps", *heads[h2]["id"], j2))
                    if hd["kind"] == "na":
                        dve.wait_ge(*when("bias_loaded", hd["id"][1]))
                        at = hd["h"] * 6 * 64 + (2 - 2 * j) * 64
                        dve.tensor_tensor_reduce(biased[:, i % 2, 0:NX], p[:, 0:NX], bias[:, at:at + NX], 1.0, -3e38,
                                                 ALU.add, ALU.max, st[:, 0:1]).then_inc(*made("win_max", *key))
                        dve.tensor_reduce(st[:, 1:2], p[:, NX:N1], AX.X, ALU.max).then_inc(*made("ctx_max", *key))
                        dve.wait_ge(*when("win_max", *key))
                        dve.wait_ge(*when("ctx_max", *key))
                        dve.tensor_scalar(st[:, 3:4], st[:, 0:1], st[:, 1:2], -1.0, ALU.max, ALU.mult).then_inc(
                            *made("row_max", *key))
                        return
                    if hd["kind"] == "fox":
                        dve.tensor_tensor_reduce(biased[0:nq, i % 2, 0:nk], p[0:nq, 0:nk],
                                                 cst(C_CAUSAL + 2 * P - q0, nk, nq), 1.0, -3e38, ALU.add, ALU.max,
                                                 st[:, 0:1]).then_inc(*made("win_max", *key, frees=("scores", *key)))
                    else:
                        dve.tensor_reduce(st[:, 0:1], p[0:nq, 0:nk], AX.X, ALU.max).then_inc(*made("win_max", *key))
                    dve.wait_ge(*when("win_max", *key))
                    dve.tensor_scalar(st[:, 3:4], st[:, 0:1], -1.0, None, ALU.mult).then_inc(*made("row_max", *key))

                def normalise(i):
                    hi, j = tiles[i]
                    hd = heads[hi]
                    q0, nq, nk = hd["tiles"][j]
                    key = (*hd["id"], j)
                    st = stat[0:nq, i % 4]
                    dve.wait_ge(*when("exps", *key))
                    src = st[:, 4:5]
                    if hd["kind"] == "na":
                        dve.tensor_tensor(st[:, 6:7], st[:, 4:5], st[:, 5:6], ALU.add).then_inc(*made("row_sum", *key))
                        dve.wait_ge(*when("row_sum", *key))
                        src = st[:, 6:7]
                    dve.reciprocal(st[:, 7:8], src).then_inc(*made("row_inv", *key))
                    dve.wait_ge(*when("row_inv", *key))
                    dve.tensor_scalar(probs[0:nq, i % 2, 0:nk], probs[0:nq, i % 2, 0:nk], st[:, 7:8], None,
                                      ALU.mult).then_inc(*made("probs", *key))

                def attended(hi):
                    hd = heads[hi]
                    dve.wait_ge(*when("attended", *hd["id"]))
                    p = bank("attended", *hd["id"])
                    dve.tensor_copy(hd["out"], p[hd["po"]:hd["po"] + HD, 0:hd["n"]]).then_inc(
                        *made("attended_sb", *hd["id"], frees=("attended", *hd["id"])))

                maxima(0)
                done = 0
                for i in range(len(tiles)):
                    if i + 1 < len(tiles):
                        maxima(i + 1)
                    normalise(i)
                    while done < tiles[i][0] and (done, len(heads[done]["tiles"]) - 1) != tiles[i]:
                        attended(done)
                        done += 1
                attended(len(heads) - 1)

            def gla_gates(l):
                for g in range(2):
                    dve.wait_ge(*when("gate_in", l, g))
                    p = bank("gate_in", l, g)
                    y, e = decay[:, 1, g], decay[:, 0, g]
                    dve.tensor_scalar(y, p, scalar1(l, "bf" if g == 0 else "bb"), None, ALU.add).then_inc(
                        *made("gate_y", l, g, frees=("gate_in", l, g)))
                    dve.wait_ge(*when("gate_y", l, g))
                    dve.scalar_tensor_tensor(e, y, -1.0, y, ALU.mult, ALU.min).then_inc(*made("neg_abs", l, g))
                for g in range(2):
                    y, e = decay[:, 1, g], decay[:, 0, g]
                    dve.wait_ge(*when("gate_ln", l, g))
                    dve.scalar_tensor_tensor(e, y, 0.0, e, ALU.min, ALU.subtract).then_inc(*made("log_gate", l, g))
                    dve.wait_ge(*when("log_gate", l, g))
                    for s in range(2):
                        a, b = s * NX, (s + 1) * NX
                        if g == 0:
                            o, i = gates[:, 0, a:b], e[:, a:b]
                        else:
                            stop = a - 1 if a else None
                            o, i = gates[:, 1, b - 1:stop:-1], e[:, b - 1:stop:-1]
                        dve.tensor_tensor_scan(o, eps_one[:, 1:2].broadcast_to([P, NX]), i, 0.0, ALU.mult, ALU.add).then_inc(
                            *made("gate_sums", l, g, s))
                dve.wait_ge(*when("gate_sums", l, 1, 1))
                for g, edge in ((0, N1 - 1), (1, NX)):
                    dve.tensor_scalar(act_out[:, 0, g * NZ:(g + 1) * NZ], gates[:, g, NX:N1], gates[:, g, edge:edge + 1],
                                      -1.0, ALU.subtract, ALU.mult).then_inc(*made("z_exponents", l, g))
                dve.wait_ge(*when("projected", ("mix1", l), 8))
                dve.wait_ge(*when("projected", ("mix1", l), 9))
                dve.wait_ge(*when("z_decays", l))
                dve.tensor_tensor(act_out[:, 0].rearrange("p (g n) -> p g n", g=2),
                                  act_out[:, 0].rearrange("p (g n) -> p g n", g=2),
                                  proj1[:, GLAK:GLAK + 1, NX:N1].broadcast_to([P, 2, NZ]), ALU.mult).then_inc(
                                      *made("khat_t", l))
                dve.wait_ge(*when("x_decays", l, 1))
                dve.tensor_tensor(act_out[:, 1].rearrange("p (g n) -> p g n", g=2),
                                  act_out[:, 1].rearrange("p (g n) -> p g n", g=2),
                                  proj1[:, GLAQ:GLAQ + 1, 0:NX].broadcast_to([P, 2, NX]), ALU.mult).then_inc(
                                      *made("q_from_start", l))

            def gla_levels(l):
                n = N1 if l == 0 else NX
                ntile = n // P
                for h in range(4):
                    dve.wait_ge(*when("pairs", l, -1, h))
                    p = bank("pairs", l, -1, h)
                    dve.tensor_scalar(gla_s[:, h, 0:ntile], p[:, 0:n].rearrange("p (t n) -> p t n", n=P), 2.0, None,
                                      ALU.mult).then_inc(*made("gla_scores", l, -1, h, frees=("pairs", l, -1, h)))
                dve.wait_ge(*when("masks_loaded", 0))

                def decayed(v):
                    dve.wait_ge(*when("decays", l, v))
                    dve.tensor_tensor(decay[:, v % 2, :, 0:n], decay[:, v % 2, :, 0:n],
                                      proj1[:, GLAQ:GLAK + 1, 0:n], ALU.mult).then_inc(*made("decayed", l, v))

                decayed(0)
                for v in range(LEVELS + 1):
                    if v + 1 <= LEVELS:
                        decayed(v + 1)
                    if v == LEVELS:
                        break
                    for h in range(4):
                        dve.wait_ge(*when("pairs", l, v, h))
                        p = bank("pairs", l, v, h)
                        dve.wait_ge(*when("gla_scores", l, v - 1, h))
                        dve.copy_predicated(gla_s[:, h, 0:ntile], masks[:, v:v + 1].broadcast_to([P, ntile, P]),
                                            p[:, 0:n].rearrange("p (t n) -> p t n", n=P)).then_inc(
                                                *made("gla_scores", l, v, h, frees=("pairs", l, v, h)))

            def gla_out(l):
                streams = BOTH if l == 0 else ONLY_X
                for s, s0, s1 in streams:
                    for h in range(4):
                        po = (h % 2) * HD
                        dve.wait_ge(*when("gla_out", l, s, h))
                        p = bank("gla_out", l, s, h)
                        dve.tensor_copy(mix1[po:po + HD, 4 + h // 2, s0:s1], p[po:po + HD, 0:NX]).then_inc(
                            *made("gla_out_sb", l, s, h, frees=("gla_out", l, s, h)))

            def gated(name, tag, idx, x, g, ready):
                dve.wait_ge(*when(*ready))
                dve.wait_ge(*when("silu_gate", tag, idx))
                dve.tensor_tensor(x, x, g, ALU.mult).then_inc(*made(name, tag[1], idx))

            def retention(l):
                for h in range(4):
                    dve.wait_ge(*when("ret_pairs", l, h))
                    p = bank("ret_pairs", l, h)
                    if h >= 2:
                        dve.wait_ge(*when("ret_out", l, h - 2))
                    at = 0
                    for j, (t0, tn) in enumerate(TILES2):
                        n = N2 - t0
                        last = dve.tensor_tensor(probs_t[0:tn, h % 2, j, t0:N2], p[0:tn, at:at + n],
                                                 cst(C_DECAY + h * N2, n, tn), ALU.mult)
                        last.then_inc(*made("ret_decayed", l, h, j, frees=("ret_pairs", l, h)))
                        at += n
                for h in range(4):
                    dve.wait_ge(*when("ret_mean", l, h))
                    p = bank("ret_mean", l, h)
                    dve.wait_ge(*when("ret_sb", l, h))
                    dve.tensor_tensor(mix2[:, 4 + h, :], mix2[:, 4 + h, :], p[:, 0:N2], ALU.subtract).then_inc(
                        *made("ret_centred", l, h, frees=("ret_mean", l, h)))
                for h in range(4):
                    dve.wait_ge(*when("rstd", ("ret", l, h)))
                    dve.scalar_tensor_tensor(mix2[:, 4 + h, :], mix2[:, 4 + h, :], scalar2(l, "gn", h),
                                             rstd[:, h % 2, 0:N2], ALU.mult, ALU.mult).then_inc(
                                                 *made("ret_normed", l, h))
                for h in range(4):
                    gated("mix_ret", ("b2", l), h, mix2[:, 4 + h, :], proj2[:, RG + h, :], ("ret_normed", l, h))

            dve.memset(eps_one[:, 0:1], EPS).then_inc(*made("eps_one", 0))
            dve.memset(eps_one[:, 1:2], 1.0).then_inc(*made("eps_one", 1))
            dve.wait_ge(*when("small_loaded", 0))
            for l in range(DEPTH):
                for name in ("naq", "gqaq"):
                    dve.tensor_scalar(scalar1(l, name), scalar1(l, name), HD ** -0.5, None, ALU.mult).then_inc(
                        *made("gain_scaled", l, name))
            dve.wait_ge(*when("gain_scaled", DEPTH - 1, "gqaq"))
            for d in range(KC):
                sum_squares(("start",), N1, d)
            for j in range(2 * KC):
                mod_dot(0, j)
            norm1(("start",), ("ffn1", 0), 0, 0, N1, True)
            for l in range(DEPTH):
                t1, tm, to, t2 = ("ffn1", l), ("mix1", l), ("out1", l), ("ffn2", l)
                n = N1 if l == 0 else NX
                streams = BOTH if l == 0 else ONLY_X
                todo = 2 * KC
                for f in range(FC):
                    hidden_product(t1, hidden(N1), f, N1)
                    if l == 0:
                        upto = 2 * KC + (7 * KC * (f + 1) + FC - 1) // FC
                        for j in range(todo, upto):
                            mod_dot(0, j)
                        todo = upto
                residual(t1, l, 2, BOTH, N1, META, N1)
                norm1(t1, tm, l, 3, N1, True)
                projections(tm, PROJ1, lambda it: N1 if (l == 0 or it[3]) else NX,
                            lambda dst, width, nn: proj1[0:width, dst, 0:nn])
                fourier(l)
                head_norms(tm, norm_items(l), lambda it: proj1[:, it[0], 0:it[2]], lambda it: scalar1(l, it[1]))
                rope(l, rope_items, proj1, C_COS1, C_SIN1, NX, tm)
                gla_gates(l)
                gla_levels(l)
                gla_out(l)
                for c in range(2):
                    ev.table[("gla_sb", l, c)] = ev.table[("gla_out_sb", l, len(streams) - 1, 2 * c + 1)]
                hds = softmax_heads(l)
                attention(hds)
                ev.table[("mix_done", l)] = ev.table[("attended_sb", *hds[-1]["id"])]
                head_norms(("gla", l), [(0, 0, n), (1, 0, n)], lambda it: mix1[:, 4 + it[0], 0:it[2]],
                           lambda it: scalar1(l, "gla"))
                for c in range(2):
                    gated("mix_gla", tm, c, mix1[:, 4 + c, 0:n], proj1[:, GLAR + c, 0:n], ("head_normed", ("gla", l), c))
                residual(to, l, 5, streams, n, META, n)
                norm1(to, t2, l, 6, n, l == 0)
                todo = 0
                for f in range(FC):
                    hidden_product(t2, hidden(n), f, n)
                    if l == 0:
                        upto = (NMOD * KC * (f + 1) + FC - 1) // FC
                        for j in range(todo, upto):
                            mod_dot(1, j)
                        todo = upto
                residual(t2, l, 8, streams, n, META, n if l == 0 else N2)
                if l == 0:
                    norm1(t2, ("ffn1", 1), 1, 0, N1, True)
                else:
                    norm2(t2, ("b2", 0), lambda c: scalar2(0, "attn", c), xn2, 0, N2)
            for l in range(DEPTH):
                tp, to, tf = ("b2", l), ("out2", l), ("ffn", l)
                projections(tp, PROJ2, lambda it: N2,
                            lambda dst, width, nn: (negc[0:8, 0, :] if dst == FLOG else proj2[0:width, dst, 0:nn]))
                y, e = negc[0:8, 0, :], negc[0:8, 1, :]
                dve.wait_ge(*when("projected", tp, 12))
                dve.tensor_scalar(y, y, scalar2(l, "bfg", 0, 8), None, ALU.add).then_inc(*made("flog_y", l))
                dve.wait_ge(*when("flog_y", l))
                dve.scalar_tensor_tensor(e, y, -1.0, y, ALU.mult, ALU.min).then_inc(*made("flog_neg_abs", l))
                rope(("b2", l), [RQ, RQ + 1, RQ + 2, RQ + 3, RK, RK + 1, RK + 2, RK + 3], proj2, C_COS2, C_SIN2,
                     N2, tp)
                dve.wait_ge(*when("flog_ln", l))
                dve.scalar_tensor_tensor(e, y, 0.0, e, ALU.min, ALU.subtract).then_inc(*made("flog_log", l))
                dve.wait_ge(*when("flog_log", l))
                dve.tensor_tensor_scan(negc[0:8, 2, :], eps_one[0:8, 1:2].broadcast_to([8, N2]), e, 0.0, ALU.mult, ALU.subtract).then_inc(
                    *made("negc", l))
                hds = fox_heads(l)
                attention(hds)
                ev.table[("mix_done", ("b2", l))] = ev.table[("attended_sb", *hds[-1]["id"])]
                retention(l)
                residual(to, l, None, None, N2, 0, N2)
                norm2(to, tf, lambda c: scalar2(l, "ffn", c), xn2, 0, N2)
                for f in range(FC):
                    hidden_product(tf, hidden(N2), f, N2)
                residual(tf, l, None, None, N2, 0, N2)
                if l + 1 < DEPTH:
                    norm2(tf, ("b2", l + 1), lambda c: scalar2(l + 1, "attn", c), xn2, 0, N2)
                else:
                    norm2(tf, None, lambda c: small[:, S_FINAL + c:S_FINAL + c + 1],
                          xn_flat[:, 0:KC * NX].rearrange("p (c n) -> p c n", c=KC), META, NX, "final_norm")
    return ev


def blocks(w):
    k, m = w.shape
    mb = -(-m // P)
    if m % P:
        w = np.concatenate([w, np.zeros((k, mb * P - m), w.dtype)], 1)
    return w.reshape(k // P, P, mb, P).transpose(2, 1, 0, 3).reshape(mb, P, -1)


def down_blocks(w):
    b = w.reshape(FC, P, KC, P).transpose(2, 0, 1, 3).reshape(FC, 8, P, P)
    return b.transpose(0, 2, 1, 3).reshape(FC, P, UNIT)


def ffn_units(w1, w3, w2):
    up = np.stack([blocks(w1), blocks(w3)], 1).reshape(2 * FC, P, UNIT)
    return [up, down_blocks(w2)]


def swap_heads(w, at, axis):
    idx = np.arange(w.shape[axis])
    idx[at:at + 4 * HD] = at + np.concatenate([np.arange(HD) + HD * h for h in (0, 2, 1, 3)])
    return np.take(w, idx, axis)


def columns(v):
    return v.reshape(-1, P).T


def kernel(**inputs):
    import concourse.bacc as bacc
    from concourse.bass_utils import run_bass_kernel_spmd

    a = {k: np.asarray(v) for k, v in inputs.items()}
    units = []
    for l in range(DEPTH):
        units += ffn_units(a["ffn1_w1"][l], a["ffn1_w3"][l], a["ffn1_w2"][l])
        w = a["w_in"][l]
        gates = 256 * 4 + 128 * 2 + 256 * 2
        w = swap_heads(w, gates + 32, 1)
        units += [blocks(w[:, :gates]), blocks(w[:, gates:gates + 32]), blocks(w[:, gates + 32:])]
        units.append(blocks(swap_heads(a["w_out"][l], 768, 0)))
        units += ffn_units(a["ffn2_w1"][l], a["ffn2_w3"][l], a["ffn2_w2"][l])
    for l in range(DEPTH):
        w = a["w_in_2"][l]
        units += [blocks(w[:, :1536]), blocks(w[:, 1536:1544]), blocks(w[:, 1544:])]
        units.append(blocks(a["w_out_2"][l]))
        units += ffn_units(a["w_gate_2"][l], a["w_up_2"][l], a["w_down_2"][l])

    two = lambda v: np.concatenate([v, v])[:, None]
    small = []
    for l in range(DEPTH):
        small += [two(a[n][l]) for n in ("na_q_norm", "na_k_norm", "gqa_q_norm", "gqa_k_norm", "gla_norm")]
        small += [a["gla_b_gate_f"][l][:, None], a["gla_b_gate_b"][l][:, None], columns(a["b_mod"][l])]
    for l in range(DEPTH):
        fg = np.zeros((P, 1), np.float32)
        fg[:8, 0] = a["b_fgate_2"][l]
        small += [columns(a["attn_norm_2"][l]), columns(a["ffn_norm_2"][l]), columns(a["ret_gn_2"][l]), fg]
    small.append(columns(a["final_norm_2"]))

    wgate = np.zeros((32, DEPTH, 2 * P), np.float32)
    for l in range(DEPTH):
        wgate[0:16, l, 0:P] = a["gla_w_gate_f"][l]
        wgate[16:32, l, P:2 * P] = a["gla_w_gate_b"][l]

    cq = np.arange(64)
    start = np.clip(cq - 8, 0, 48)
    ck = np.arange(64)
    inside = (ck[None] >= start[:, None]) & (ck[None] < start[:, None] + 16)
    col = np.clip(ck[None] - cq[:, None] + 15, 0, 30)
    na_bias = np.full((DEPTH, 2, 64, 4, 6, 64), NEG, np.float32)
    for half in range(2):
        for j in range(6):
            rows = a["na_rpb"][:, :, j - 2 - half + 7]
            got = rows[:, :, col]
            na_bias[:, half, :, :, j] = np.where(inside[None, None], got, np.float32(NEG)).transpose(0, 2, 1, 3)
    na_bias = na_bias.reshape(DEPTH, P, 4 * 6 * 64)

    tr = lambda v: np.ascontiguousarray(v.T.reshape(KC, P, -1))
    arrays = {
        "stream": np.concatenate(units, 0),
        "w_mod": np.ascontiguousarray(a["w_mod"].transpose(0, 2, 1)).reshape(DEPTH, NMOD * KC, P, D),
        "x": tr(a["x"][0]), "ctx": tr(a["ctx"][0]), "meta": tr(a["meta_tokens_2"]),
        "c": a["c"].reshape(1, D), "c_ctx": a["c_ctx"].reshape(1, D),
        "small": np.concatenate(small, 1), "consts": constants(), "masks": level_masks(),
        "wgate": wgate, "na_bias": na_bias,
    }
    arrays = {k: np.ascontiguousarray(v) for k, v in arrays.items()}

    def program(old):
        nc = bacc.Bacc("TRN2", target_bir_lowering=False, num_devices=1)
        A = {k: nc.dram_tensor(f"{k}_dram", v.shape, mybir.dt.from_np(v.dtype), kind="ExternalInput").ap()
             for k, v in arrays.items()}
        A["out"] = nc.dram_tensor("out_dram", (P, KC * NX), F32, kind="ExternalOutput").ap()
        return nc, build(nc, A, old)

    _, counted = program(None)
    nc, _ = program((counted.table, counted.banks))
    r = run_bass_kernel_spmd(nc, [{f"{k}_dram": v for k, v in arrays.items()}], core_ids=[0])
    out = r.results[0]["out_dram"].reshape(P, KC, NX)
    return np.ascontiguousarray(out.transpose(2, 1, 0)).reshape(1, NX, D)
```

```python
import math
from contextlib import ExitStack

import numpy as np
import concourse.bass as bass
import concourse.mybir as mybir

F32 = mybir.dt.float32
F32R = mybir.dt.float32r
I32 = mybir.dt.int32
ALU = mybir.AluOpType
ACT = mybir.ActivationFunctionType
AX = mybir.AxisListType

P = 128
D = 1024
KC = D // P
SEQ = 256
NX, NZ = 256, 256
N1 = NX + NZ
META = 16
N2 = META + SEQ
DEPTH = 2
FF = 2816
FC = FF // P
NMOD = 9
EPS = 1e-6
HD = 64
RING = 3
MOD_RING = 3
UNIT = 8 * P
NEG = -1e30
LN_EXP = "natural_log_exp_and_others"

FIRST_MOD = 2 * KC
FIRST_SLOTS = 9

FOUR, NAQ, NAK, GLAQ, GLAK, GLAR, GATE, GQAQ, GQAK = 0, 2, 4, 6, 7, 8, 10, 11, 13
NSLOT1 = 14
NAV, GLAV, GQAV = 0, 256, 512
NV1 = 640
PROJ1 = [("V", NAV, P, True), ("V", NAV + P, P, True), ("V", GQAV, P, True), ("V", GLAV, P, True),
         ("V", GLAV + P, P, True),
         ("T", NAQ, P, False), ("T", NAQ + 1, P, False), ("T", NAK, P, True), ("T", NAK + 1, P, True),
         ("T", GQAQ, P, False), ("T", GQAQ + 1, P, False), ("T", GQAK, P, True),
         ("T", GATE, 32, True), ("T", GLAK, P, True), ("T", GLAQ, P, False),
         ("T", GLAR, P, False), ("T", GLAR + 1, P, False), ("T", FOUR, P, False), ("T", FOUR + 1, P, False)]
VTEMP1 = {0: GLAR, 1: GLAR + 1, 2: FOUR, 3: FOUR + 1, 4: GATE}
MIX1 = [FOUR, FOUR + 1, NAQ, NAQ + 1, GLAQ, GLAK, GQAQ, GQAQ + 1]
FQ, FK, RQ, RK, RG = 0, 4, 8, 12, 16
NSLOT2 = 20
FLOG = -1
PROJ2 = ([("V", P * i, P) for i in range(4)] + [("T", FLOG, 8)]
         + [("T", FQ + i, P) for i in range(4)] + [("T", FK + i, P) for i in range(4)]
         + [("V", 512 + P * i, P) for i in range(4)]
         + [("T", RQ + i, P) for i in range(4)] + [("T", RK + i, P) for i in range(4)]
         + [("T", RG + i, P) for i in range(4)])
VTEMP2 = {i: RG + i % 4 for i in (0, 1, 2, 3)} | {13 + i: RG + i for i in range(4)}
MIX2 = [FQ, FQ + 1, FQ + 2, FQ + 3, RQ, RQ + 1, RQ + 2, RQ + 3]
SLOT1 = {item[1]: i for i, item in enumerate(PROJ1) if item[0] == "T"}
SLOT2 = {item[1]: i for i, item in enumerate(PROJ2) if item[0] == "T"}
NV2 = 1024
TILES2 = [(0, 128), (128, 128), (256, 16)]

UNITS = DEPTH * (6 * FC + len(PROJ1) + KC) + DEPTH * (len(PROJ2) + KC + 3 * FC)

S_L1 = {"naq": 0, "nak": 1, "gqaq": 2, "gqak": 3, "gla": 4, "bf": 5, "bb": 6, "bmod": 7}
SW1 = 7 + NMOD * KC
S_L2 = {"attn": 0, "ffn": KC, "gn": 2 * KC, "bfg": 2 * KC + 4}
SW2 = 2 * KC + 5
S_FINAL = DEPTH * (SW1 + SW2)
SMALL = S_FINAL + KC

C_ONESD, C_ONES64, C_IDENT, C_PERM64 = (P * i for i in range(4))
C_COS1 = 4 * P
C_SIN1 = C_COS1 + SEQ
CONSTS = C_SIN1 + SEQ
C_DFTD = 0
C_DFTL = C_DFTD + 2 * P
DFT = C_DFTL + 2 * 2 * SEQ
C_ONES128, C_PERM128 = 0, P
C_COS2 = 2 * P
C_SIN2 = C_COS2 + N2
C_CAUSAL = C_SIN2 + N2
C_DECAY = C_CAUSAL + 3 * P
CONSTS2 = C_DECAY + 4 * N2
LEVELS = 7


def constants():
    c = np.zeros((P, CONSTS), np.float64)
    f = np.zeros((P, DFT), np.float64)
    d = np.zeros((P, CONSTS2), np.float64)
    c[:, C_ONESD:C_ONESD + P] = 1.0 / D
    half = np.arange(P) // HD
    c[:, C_ONES64:C_ONES64 + P] = (half[:, None] == half[None, :]) / HD
    d[:, C_ONES128:C_ONES128 + P] = 1.0 / P
    c[:, C_IDENT:C_IDENT + P] = np.eye(P)
    for t, at, n in ((c, C_PERM64, HD), (d, C_PERM128, P)):
        for i in range(P):
            j = i + n // 2 if i % n < n // 2 else i - n // 2
            t[j, at + i] = -1.0 if i % n < n // 2 else 1.0
    jd = np.arange(HD)
    ang = 2 * np.pi * (np.outer(jd, jd) % HD) / HD
    for g in range(2):
        s = slice(g * HD, (g + 1) * HD)
        f[s, C_DFTD + g * HD:C_DFTD + (g + 1) * HD] = np.cos(ang)
        f[s, C_DFTD + P + g * HD:C_DFTD + P + (g + 1) * HD] = np.sin(ang)
    jl = np.arange(SEQ)
    ang = 2 * np.pi * (np.outer(jl, jl) % SEQ) / SEQ
    norm = 1.0 / math.sqrt(SEQ * HD)
    for t in range(2):
        rows = ang[t * P:(t + 1) * P]
        at = C_DFTL + t * 2 * SEQ
        f[:, at:at + SEQ] = np.cos(rows) * norm
        f[:, at + SEQ:at + 2 * SEQ] = -np.sin(rows) * norm
    nf = HD // 4
    inv = 10000.0 ** (-np.arange(nf, dtype=np.float64) / nf)
    tok = np.arange(SEQ)
    ang = np.concatenate([(tok // 64)[None] * inv[:, None], (tok % 64)[None] * inv[:, None]], 0)
    c[:, C_COS1:C_COS1 + SEQ] = np.tile(np.cos(ang), (4, 1))
    c[:, C_SIN1:C_SIN1 + SEQ] = np.tile(np.sin(ang), (4, 1))
    inv = 10000.0 ** (-np.arange(0, P, 2, dtype=np.float64) / P)
    ang = inv[:, None] * np.arange(N2)[None]
    d[:, C_COS2:C_COS2 + N2] = np.tile(np.cos(ang), (2, 1))
    d[:, C_SIN2:C_SIN2 + N2] = np.tile(np.sin(ang), (2, 1))
    q = np.arange(P)
    d[:, C_CAUSAL + 2 * P:C_CAUSAL + 3 * P] = np.where(q[None, :] <= q[:, None], 0.0, NEG)
    for h in range(4):
        g = math.log(1.0 - 2.0 ** (-5 - h))
        diff = np.arange(N2)[None, :] - q[:, None]
        d[:, C_DECAY + h * N2:C_DECAY + (h + 1) * N2] = np.where(
            diff >= 0, np.exp(np.maximum(diff, 0) * g), 0.0) * P ** -0.5
    return c.astype(np.float32), f.astype(np.float32), d.astype(np.float32)


def level_masks():
    i = np.arange(P)
    out = np.zeros((P, LEVELS, P), np.int32)
    for v in range(LEVELS):
        m = 1 << v
        same = (i[:, None] // (2 * m)) == (i[None, :] // (2 * m))
        out[:, v] = same & ((i[:, None] // m) != (i[None, :] // m))
    return out.reshape(P, LEVELS * P)


class Events:

    def __init__(self, table=None, banks=None):
        self.known = table or {}
        self.bank_known = banks or {}
        self.counting = table is None
        self.table, self.banks, self.count = {}, {}, {}
        self.sems = {}


class Events:

    def __init__(self, table=None, banks=None):
        self.known = table or {}
        self.bank_known = banks or {}
        self.counting = table is None
        self.table, self.banks, self.count = {}, {}, {}
        self.sems = {}


def mod_chunks(l, f):
    first, n = (2 * KC, 7 * KC) if l == 0 else (0, NMOD * KC)
    return range(first + n * f // FC, first + n * (f + 1) // FC)


def build(nc, A, old=None):
    ev = Events(*(old or (None, None)))
    ctx = ExitStack()
    with ctx:
        top = [nc.sbuf_base + (-nc.sbuf_base) % 64]

        def sb(name, cols, dt=F32, over=None):
            if over is None:
                over = top[0] = -(-top[0] // 64) * 64
                top[0] += cols * mybir.dt.size(dt)
            place_of[name] = over
            return nc.alloc_sbuf_tensor_at(name, [P, cols], dt, offset=over)[:, :]

        place_of = {}

        def sem(name):
            return ctx.enter_context(nc.semaphore(name))

        def made(name, *key, by=1, frees=None, unit=None):
            if name not in ev.sems:
                ev.sems[name] = sem(name)
            ev.count[name] = ev.count.get(name, 0) + by
            ev.table[(name, *key)] = (name, ev.count[name])
            if frees is not None:
                ev.table[("free",) + frees] = (name, ev.count[name])
            if unit is not None:
                ev.table[("unit_used", unit)] = (name, ev.count[name])
            return ev.sems[name], by

        def when(name, *key):
            if ev.counting:
                return high_parts, 1
            family, value = ev.known[(name, *key)]
            if family not in ev.sems:
                ev.sems[family] = sem(family)
            return ev.sems[family], value

        def bank(*key):
            return psum[ev.bank_known.get(key, 0)]

        resid = sb("resid", KC * (META + N1)).rearrange("p (c n) -> p c n", c=KC)
        const = sb("const", CONSTS)
        small = sb("small", SMALL)
        eps_one = sb("eps_one", 2)
        ring = sb("ring", RING * UNIT).rearrange("p (s n) -> p s n", s=RING)
        high = sb("ring_high", RING * UNIT, F32R)
        low = sb("ring_low", RING * UNIT, F32R)
        high_f = high.bitcast(F32).rearrange("p (s n) -> p s n", s=RING)
        high = high.rearrange("p (s n) -> p s n", s=RING)
        low = low.rearrange("p (s n) -> p s n", s=RING)
        xr = sb("x_parts", 2 * KC * N1, F32R)
        xf = sb("x_place", 2 * KC * N1, F32, over=place_of["x_parts"])
        dft_ab = xf[:, 0:2048].rearrange("p (s t n) -> p s t n", s=2, t=2)
        cross = xf[:, 0:2048].rearrange("p (h t n) -> p h t n", h=4, t=4)
        gla_s = xf[:, 2048:4096].rearrange("p (h t n) -> p h t n", h=4, t=4)
        gates = xf[:, 4096:5120].rearrange("p (g n) -> p g n", g=2)
        decay = xf[:, 5120:7168].rearrange("p (b g n) -> p b g n", b=2, g=2)
        khat = xf[:, 7168:7680].rearrange("p (t n) -> p t n", t=4)
        state = xf[:, 7680:8192].rearrange("p (g n) -> p g n", g=2)
        ret_p = xf[:, 0:2 * 3 * N2].rearrange("p (b k n) -> p b k n", b=2, k=3)
        HID = 2 * FC * N2
        top[0] = -(-top[0] // 64) * 64
        hid_r = sb("hidden_parts", HID, F32R, over=top[0])
        arena = sb("arena", 15008)
        proj1 = arena[:, 0:NSLOT1 * N1].rearrange("p (c n) -> p c n", c=NSLOT1)
        v1 = arena[:, NSLOT1 * N1:NSLOT1 * N1 + 4 * NV1].rearrange("p (t n) -> p t n", t=4)
        proj2 = arena[:, 0:NSLOT2 * N2].rearrange("p (c n) -> p c n", c=NSLOT2)
        v2 = arena[:, NSLOT2 * N2:NSLOT2 * N2 + 3 * NV2].rearrange("p (t n) -> p t n", t=3)
        probs_t = arena[:, 9728:11904].rearrange("p (b k n) -> p b k n", b=2, k=4)
        probs = arena[:, 11904:12928].rearrange("p (b n) -> p b n", b=2)
        biased = arena[:, 12928:13472].rearrange("p (b n) -> p b n", b=2)
        bias = arena[:, 13472:15008]
        negc = bias[:, 0:3 * N2].rearrange("p (g n) -> p g n", g=3)
        scaled = arena[:, 0:KC * N1].rearrange("p (c n) -> p c n", c=KC)
        first_mod = arena[:, KC * N1:KC * N1 + FIRST_SLOTS * UNIT].rearrange("p (s k n) -> p s k n", s=FIRST_SLOTS, k=2)
        first_rows = arena[0:2, 0:FIRST_MOD * P]
        mod_flat = sb("mod_ring", MOD_RING * D)
        mod_ring = mod_flat.rearrange("p (s n) -> p s n", s=MOD_RING)
        const2 = mod_flat[:, 0:CONSTS2]
        c_cols = sb("c_cols", 2 * KC).rearrange("p (c s) -> p c s", c=KC)
        csilu = sb("csilu", 2 * D).rearrange("p (s n) -> p s n", s=2)
        junk = sb("mod_products", 2 * D, mybir.dt.bfloat16).rearrange("p (s n) -> p s n", s=2)
        mod_raw = sb("mod_raw", DEPTH * 2 * NMOD * KC).rearrange("p (l s n) -> p l s n", l=DEPTH, s=2)
        mod = sb("mod", DEPTH * 2 * NMOD * KC).rearrange("p (l s n) -> p l s n", l=DEPTH, s=2)
        dft = sb("dft", DFT)
        masks = sb("masks", LEVELS * P, I32).rearrange("p (v n) -> p v n", v=LEVELS)
        wgate = sb("wgate", DEPTH * 2 * P).rearrange("p (l n) -> p l n", l=DEPTH)
        squares = sb("squares", 2 * N1).rearrange("p (b n) -> p b n", b=2)
        sumsq = sb("sumsq", N1)
        rstd = sb("rstd", 2 * N1).rearrange("p (b n) -> p b n", b=2)
        act_out = sb("act_out", 2 * N1).rearrange("p (b n) -> p b n", b=2)
        fresh = sb("fresh", 2 * N1).rearrange("p (b n) -> p b n", b=2)
        stat = sb("softmax_stats", 4 * 8).rearrange("p (b n) -> p b n", b=4)
        assert top[0] <= nc.sbuf_usable_end, (top[0], nc.sbuf_usable_end)
        psum = [ctx.enter_context(nc.psum_tensor(f"bank{i}", [P, 512], F32))[:, :] for i in range(8)]

        def x_parts(n):
            v = xr[:, 0:2 * KC * n].rearrange("p (k c n) -> p k c n", k=2, c=KC)
            return v[:, 0], v[:, 1]

        def hidden_parts(n, parts):
            nf = FC // parts
            v = hid_r[:, 0:2 * nf * n].rearrange("p (k c n) -> p k c n", k=2, c=nf)
            return v[:, 0], v[:, 1]

        def cst(at, n=P, rows=P):
            return const[0:rows, at:at + n]

        def cst2(at, n=P, rows=P):
            return const2[0:rows, at:at + n]

        def scalar1(l, name, j=0):
            at = l * SW1 + S_L1[name] + j
            return small[:, at:at + 1]

        def scalar2(l, name, j=0, rows=P):
            at = DEPTH * SW1 + l * SW2 + S_L2[name] + j
            return small[0:rows, at:at + 1]

        unit_loaded = [sem(f"unit_loaded{i}") for i in range(RING)]
        high_parts = sem("high_parts")
        low_parts = sem("low_parts")

        BOTH = [(0, 0, NX), (1, NX, N1)]
        ONLY_X = [(0, 0, NX)]

        def width1(l, item):
            return N1 if l == 0 or item[3] else NX

        def na_heads(l):
            out = []
            for h in range(4):
                c, po = h // 2, (h % 2) * HD
                out.append(dict(id=("nax", l, h), po=po, q=proj1[po:po + HD, NAQ + c, 0:NX],
                                k=proj1[po:po + HD, NAK + c, 0:N1], tiles=[(0, P, N1), (P, P, N1)],
                                v=[(P, v1[:, t, NAV + h * HD:NAV + (h + 1) * HD]) for t in range(4)],
                                kind="na", h=h, out=proj1[po:po + HD, NAQ + c, 0:NX], n=NX))
                if l == 0:
                    out.append(dict(id=("naz", l, h), po=po, q=proj1[po:po + HD, NAQ + c, NX:N1],
                                    k=proj1[po:po + HD, NAK + c, NX:N1], tiles=[(0, P, NZ), (P, P, NZ)],
                                    v=[(P, v1[:, t, NAV + h * HD:NAV + (h + 1) * HD]) for t in (2, 3)],
                                    kind="plain", h=h, out=proj1[po:po + HD, NAQ + c, NX:N1], n=NZ))
            return out

        def gqa_heads(l):
            out = []
            for h in range(4):
                c, po, kv = h // 2, (h % 2) * HD, h % 2
                out.append(dict(id=("gqax", l, h), po=po, q=proj1[po:po + HD, GQAQ + c, 0:NX],
                                k=proj1[po:po + HD, GQAK, 0:N1], tiles=[(0, P, N1), (P, P, N1)],
                                v=[(P, v1[:, t, GQAV + kv * HD:GQAV + (kv + 1) * HD]) for t in range(4)],
                                kind="plain", h=h, out=proj1[po:po + HD, GQAQ + c, 0:NX], n=NX))
                if l == 0:
                    out.append(dict(id=("gqaz", l, h), po=po, q=proj1[po:po + HD, GQAQ + c, NX:N1],
                                    k=proj1[po:po + HD, GQAK, NX:N1], tiles=[(0, P, NZ), (P, P, NZ)],
                                    v=[(P, v1[:, t, GQAV + kv * HD:GQAV + (kv + 1) * HD]) for t in (2, 3)],
                                    kind="plain", h=h, out=proj1[po:po + HD, GQAQ + c, NX:N1], n=NZ))
            return out

        def fox_heads(l):
            out = []
            for h in range(8):
                c, po = h // 2, (h % 2) * HD
                out.append(dict(id=("fox", l, h), po=po, q=proj2[po:po + HD, FQ + c, :],
                                k=proj2[po:po + HD, FK + c, :],
                                tiles=[(0, P, P), (P, P, 2 * P), (2 * P, META, N2)],
                                v=[(n, v2[0:n, t, h * HD:(h + 1) * HD]) for t, (_, n) in enumerate(TILES2)],
                                kind="fox", h=h, out=proj2[po:po + HD, FQ + c, :], n=N2))
            return out

        def norm_items(l):
            nq = N1 if l == 0 else NX
            return ([(NAQ, "naq", nq), (NAQ + 1, "naq", nq), (NAK, "nak", N1), (NAK + 1, "nak", N1),
                     (GQAQ, "gqaq", nq), (GQAQ + 1, "gqaq", nq), (GQAK, "gqak", N1)])

        rope_items = [GQAQ, GQAQ + 1, GQAK]

        def on_act(tag, i):
            plan = PROJ1 if tag[0] == "mix1" else PROJ2
            kind, dst = plan[i][:2]
            if kind == "T" and (dst in (GLAQ, GLAR, GLAR + 1) if tag[0] == "mix1" else dst >= RG):
                return True
            return i % 2 == 0

        every = [hd for l in range(DEPTH) for hd in na_heads(l) + gqa_heads(l)] + \
                [hd for l in range(DEPTH) for hd in fox_heads(l)]
        tile_keys = [(*hd["id"], j) for hd in every for j in range(len(hd["tiles"]))]
        tile_no = {key: i for i, key in enumerate(tile_keys)}
        head_no = {hd["id"]: i for i, hd in enumerate(every)}
        block = ctx.enter_context(nc.Block())

        @block.sync
        def _(sp):
            sp.dma_start(c_cols, A["c_cols"].rearrange("p (c s) -> p c s", c=KC)).then_inc(
                *made("c_cols_loaded", 0, by=16))
            sp.dma_start(resid[:, :, META:META + NX], A["x"]).then_inc(*made("x_loaded", 0, by=16))
            sp.dma_start(resid[:, :, META + NX:META + N1], A["ctx"]).then_inc(*made("ctx_loaded", 0, by=16))
            sp.dma_start(const, A["consts"]).then_inc(*made("consts_loaded", 0, by=16))
            sp.dma_start(small, A["small"]).then_inc(*made("small_loaded", 0, by=16))
            for s in range(RING):
                sp.dma_start(ring[:, s], A["stream"][s]).then_inc(unit_loaded[s], 16)
            sp.dma_start(resid[:, :, 0:META], A["meta"]).then_inc(*made("meta_loaded", 0, by=16))
            turns = UNITS // RING
            with sp.Fori(1, turns) as turn:
                for s in range(RING):
                    sp.wait_ge(low_parts, turn * RING + (s + 1 - RING))
                    sp.dma_start(ring[:, s], A["stream"][turn * RING + s]).then_inc(unit_loaded[s], 16)
            for u in range(turns * RING, UNITS):
                sp.wait_ge(low_parts, u - RING + 1)
                sp.dma_start(ring[:, u % RING], A["stream"][u]).then_inc(unit_loaded[u % RING], 16)
            sp.wait_ge(*when("final_norm", KC - 1))
            sp.dma_start(A["out"], xf[:, 0:KC * NX]).then_inc(*made("out_stored", 0, by=16))
            sp.wait_ge(*when("out_stored", 0))

        @block.gpsimd
        def _(pool):
            loaded = [FIRST_MOD]

            def mod_loads(upto):
                for n in range(loaded[0], min(upto, DEPTH * NMOD * KC)):
                    if n >= FIRST_MOD + MOD_RING:
                        pool.wait_ge(*when("mod_dot", n - MOD_RING))
                    pool.dma_start(mod_ring[:, n % MOD_RING], A["w_mod"][n // (NMOD * KC), n % (NMOD * KC)]).then_inc(
                        *made(f"mod_loaded{n % MOD_RING}", n, by=16))
                loaded[0] = max(loaded[0], upto)

            def low_part(tag, out, c, n, whole, ready="x_high"):
                pool.wait_ge(*when(ready, tag, c))
                hi, lo = out
                pool.tensor_tensor(lo[:, c, 0:n], whole, hi[:, c, 0:n].bitcast(F32), ALU.subtract).then_inc(
                    *made("x_low_pool", tag, c))
                ev.table[("x_low", tag, c)] = ev.table[("x_low_pool", tag, c)]

            def norm1(tag, n):
                for c in range(1, KC, 2):
                    low_part(tag, x_parts(N1), c, n, scaled[:, c, 0:n], "shifted")

            def norm2(tag):
                for c in range(1, KC, 2):
                    low_part(tag, x_parts(N2), c, N2, scaled[:, c, 0:N2])

            def hidden_low(tag, n, parts, l=None):
                hi, lo = hidden_parts(n, parts)
                nf = FC // parts
                for h in range(parts):
                    for f in range(nf):
                        pool.wait_ge(*when("hidden_high", tag, h, f))
                        pool.tensor_tensor(lo[:, f], fresh[:, f % 2, 0:n], hi[:, f].bitcast(F32),
                                           ALU.subtract).then_inc(*made("hidden_low", tag, h, f))
                        if l is not None:
                            mod_loads(l * NMOD * KC + mod_chunks(l, h * nf + f).stop + MOD_RING)

            def gla_exponents(l):
                n = N1 if l == 0 else NX
                b, c = gates[:, 0, 0:n], gates[:, 1, 0:n]
                pool.wait_ge(*when("gate_sums", l, 1, 1))
                for v in range(LEVELS + 1):
                    m = 1 << v
                    if v >= 2:
                        pool.wait_ge(*when("pairs", l, v - 2, 3))
                    bv = b.rearrange("p (k t m) -> p k t m", t=2, m=m)
                    cv = c.rearrange("p (k t m) -> p k t m", t=2, m=m)
                    dq = decay[:, v % 2, 0, 0:n].rearrange("p (k t m) -> p k t m", t=2, m=m)
                    dk = decay[:, v % 2, 1, 0:n].rearrange("p (k t m) -> p k t m", t=2, m=m)
                    shape = [P, n // (2 * m), m]
                    b_mid = bv[:, :, 0, m - 1:m].broadcast_to(shape)
                    c_mid = cv[:, :, 1, 0:1].broadcast_to(shape)
                    pool.tensor_tensor(dq[:, :, 0, :], cv[:, :, 0, :], c_mid, ALU.subtract).then_inc(
                        *made("exponents", l, v, 0))
                    pool.tensor_tensor(dq[:, :, 1, :], bv[:, :, 1, :], b_mid, ALU.subtract).then_inc(
                        *made("exponents", l, v, 1))
                    pool.tensor_tensor(dk[:, :, 0, :], b_mid, bv[:, :, 0, :], ALU.subtract).then_inc(
                        *made("exponents", l, v, 2))
                    pool.tensor_tensor(dk[:, :, 1, :], c_mid, cv[:, :, 1, :], ALU.subtract).then_inc(
                        *made("exponents", l, v, 3))

            def mixed_low(tag, slots, src, n, nn):
                for c in range(1, KC, 2):
                    low_part(tag, x_parts(n), c, nn, src[:, slots[c], 0:nn])

            for j in range(FIRST_MOD):
                if j >= FIRST_SLOTS:
                    pool.wait_ge(*when("first_mod", j - FIRST_SLOTS))
                pool.dma_start(first_mod[:, j % FIRST_SLOTS], A["w_mod_first"][j].rearrange("p (k n) -> p k n", k=2)).then_inc(
                    *made(f"first_mod_loaded{j % FIRST_SLOTS}", j, by=16))
            pool.dma_start(csilu[:, 0, :], A["c"].broadcast_to([P, D])).then_inc(*made("c_loaded", by=16))
            pool.dma_start(csilu[:, 1, :], A["c_ctx"].broadcast_to([P, D])).then_inc(*made("c_ctx_loaded", by=16))
            mod_loads(2 * KC + MOD_RING)
            pool.dma_start(masks, A["masks"].rearrange("p (v n) -> p v n", v=LEVELS)).then_inc(
                *made("masks_loaded", 0, by=16))
            pool.dma_start(wgate[0:32], A["wgate"]).then_inc(*made("wgate_loaded", 0, by=16))
            pool.dma_start(dft, A["dft"]).then_inc(*made("dft_loaded", 0, by=16))
            pool.dma_start(bias, A["na_bias"][0]).then_inc(*made("bias_loaded", 0, by=16))
            norm1(("ffn1", 0), N1)
            for l in range(DEPTH):
                n = N1 if l == 0 else NX
                hidden_low(("ffn1", l), N1, 2, 0 if l == 0 else None)
                norm1(("mix1", l), N1)
                gla_exponents(l)
                mixed_low(("out1", l), MIX1, proj1, N1, n)
                norm1(("ffn2", l), n)
                if l == 0:
                    pool.wait_ge(*when("exps", "nax", 0, 3, 1))
                    pool.dma_start(bias, A["na_bias"][1]).then_inc(*made("bias_loaded", 1, by=16))
                hidden_low(("ffn2", l), n, 2 - l, 1 if l == 0 else None)
                if l == 0:
                    pool.wait_ge(*when("mod_dot", DEPTH * NMOD * KC - 1))
                    pool.dma_start(const2, A["consts2"]).then_inc(*made("consts2_loaded", 0, by=16))
                    norm1(("ffn1", 1), N1)
                else:
                    norm2(("b2", 0))
            for l in range(DEPTH):
                mixed_low(("out2", l), MIX2, proj2, N2, N2)
                norm2(("ffn", l))
                hidden_low(("ffn", l), N2, 1)
                if l + 1 < DEPTH:
                    norm2(("b2", l + 1))

        @block.tensor
        def _(pe):
            taken = [0]
            bank_user = {}

            def take(*key):
                b = taken[0] % 8
                taken[0] += 1
                if b in bank_user:
                    pe.wait_ge(*when("free", *bank_user[b]))
                bank_user[b] = key
                ev.banks[key] = b
                return psum[b]

            unit = [0]

            def weights():
                u = unit[0]
                unit[0] += 1
                pe.wait_ge(low_parts, u + 1)
                return [w[:, u % RING].rearrange("p (b n) -> p b n", b=8) for w in (high, low)]

            def product(out, w, b, xh, xl, start, stop):
                pe.matmul(out, w[0][:, b], xh, start=start, stop=False)
                pe.matmul(out, w[0][:, b], xl, start=False, stop=False)
                return pe.matmul(out, w[1][:, b], xh, start=False, stop=stop)

            def mean_square(tag, n):
                pe.wait_ge(*when("sumsq", tag, KC - 1))
                pe.matmul(take("mean", tag)[:, 0:n], cst(C_ONESD), sumsq[:, 0:n], start=True,
                          stop=True).then_inc(*made("mean", tag))

            def first_units(tag, keys, ns, xh, xl, order):
                ps = [take(*key) for key in keys]
                ws = [weights() for key in keys]
                for c in order:
                    pe.wait_ge(*when("x_low", tag, c))
                    for i, key in enumerate(keys):
                        n = ns[i]
                        mm = product(ps[i][:, 0:n], ws[i], c, xh[:, c, 0:n], xl[:, c, 0:n],
                                     c == order[0], c == order[-1])
                        if c == order[-1]:
                            mm.then_inc(*made(*key, unit=unit[0] - len(keys) + i))

            def ffn(tag, nx, n, parts):
                xh, xl = x_parts(nx)
                hh, hl = hidden_parts(n, parts)
                nf = FC // parts
                for h in range(parts):
                    for f in range(nf):
                        if h == 0 and f == 0:
                            first_units(tag, [("gate", tag, 0, 0), ("up", tag, 0, 0)], [n, n], xh, xl, range(KC))
                            continue
                        for what in ("gate", "up"):
                            p = take(what, tag, h, f)
                            w = weights()
                            for c in range(KC):
                                mm = product(p[:, 0:n], w, c, xh[:, c, 0:n], xl[:, c, 0:n],
                                             c == 0, c == KC - 1)
                            mm.then_inc(*made(what, tag, h, f, unit=unit[0] - 1))
                    j = 0
                    for d in range(KC):
                        p = take("down", tag, h, d)
                        for f in range(nf):
                            if j % 8 == 0:
                                w = weights()
                            if d == 0:
                                pe.wait_ge(*when("hidden_low", tag, h, f))
                            mm = product(p[:, 0:n], w, j % 8, hh[:, f], hl[:, f], f == 0, f == nf - 1)
                            j += 1
                            if f < nf - 1 and j % 8 == 0:
                                mm.then_inc(*made("unit_read", unit[0] - 1, unit=unit[0] - 1))
                        mm.then_inc(*made("down", tag, h, d, unit=unit[0] - 1 if j % 8 == 0 else None))

            def project(tag, plan, i, nx, n, src, vtemp, vtiles):
                xh, xl = x_parts(nx)
                if i == 0:
                    first_units(tag, [("proj", tag, 0), ("proj", tag, 1)], [n, n], xh, xl, range(KC))
                    return
                if i >= 2:
                    w = weights()
                    p = take("proj", tag, i)
                    for c in range(KC):
                        mm = product(p[:, 0:n], w, c, xh[:, c, 0:n], xl[:, c, 0:n], c == 0, c == KC - 1)
                    mm.then_inc(*made("proj", tag, i, unit=unit[0] - 1))
                if i and plan[i - 1][0] == "V":
                    pe.wait_ge(*when("projected", tag, i - 1))
                    p = take("v_turned", tag, i - 1)
                    for t, (t0, tn) in enumerate(vtiles):
                        mm = pe.transpose(p[0:tn, t * P:(t + 1) * P], src[:, vtemp[i - 1], t0:t0 + tn], cst(C_IDENT))
                    mm.then_inc(*made("v_turned", tag, i - 1))

            def project_out(tag, nx, n, order):
                xh, xl = x_parts(nx)
                first_units(tag, [("down", tag, 0, 0), ("down", tag, 0, 1)], [n, n], xh, xl, order)
                for d in range(2, KC):
                    w = weights()
                    p = take("down", tag, 0, d)
                    for c in range(KC):
                        mm = product(p[:, 0:n], w, c, xh[:, c, 0:n], xl[:, c, 0:n], c == 0, c == KC - 1)
                    mm.then_inc(*made("down", tag, 0, d, unit=unit[0] - 1))

            def dft_features(l, s):
                s0 = s * NX
                for t in range(2):
                    p = take("dft_d", l, s, t)
                    for g in range(2):
                        pe.wait_ge(*when("projected", ("mix1", l), SLOT1[FOUR + g]))
                        mm = pe.matmul(p[:, g * 2 * P:(g + 1) * 2 * P],
                                       proj1[:, FOUR + g, s0 + t * P:s0 + (t + 1) * P],
                                       dft[:, C_DFTD:C_DFTD + 2 * P], start=True, stop=True)
                    mm.then_inc(*made("dft_d", l, s, t))

            def dft_tokens(l, s):
                p = take("dft_l", l, s)
                for t in range(2):
                    pe.wait_ge(*when("dft_ab", l, s, t))
                for g in range(2):
                    n = 0
                    for t in range(2):
                        for part in range(2):
                            at = C_DFTL + (2 * t + part) * SEQ
                            mm = pe.matmul(p[:, g * SEQ:(g + 1) * SEQ],
                                           dft_ab[:, s, t, (2 * g + part) * P:(2 * g + part + 1) * P],
                                           dft[:, at:at + SEQ], start=(n == 0), stop=(n == 3))
                            n += 1
                mm.then_inc(*made("dft_l", l, s))

            def head_mean(tag, i, n):
                pe.wait_ge(*when("head_squares", tag, i))
                pe.matmul(take("head_mean", tag, i)[:, 0:n], cst(C_ONES64),
                          squares[:, i % 2, 0:n], start=True, stop=True).then_inc(*made("head_mean", tag, i))

            def attention(heads, beside):
                tiles = [(hd, j) for hd in heads for j in range(len(hd["tiles"]))]

                def scores(i):
                    hd, j = tiles[i]
                    q0, nq, nk = hd["tiles"][j]
                    p = take("scores", *hd["id"], j)
                    fox = hd["kind"] == "fox"
                    mm = pe.matmul(p[0:nq, 0:nk], hd["q"][:, q0:q0 + nq], hd["k"][:, 0:nk],
                                   start=True, stop=not fox)
                    if fox:
                        one_hot = const[0:8, C_IDENT + hd["h"]:C_IDENT + hd["h"] + 1].broadcast_to([8, nq])
                        mm = pe.matmul(p[0:nq, 0:nk], one_hot, negc[0:8, 2, 0:nk], start=False, stop=True)
                    mm.then_inc(*made("scores", *hd["id"], j))

                def turn(i):
                    hd, j = tiles[i]
                    _, nq, nk = hd["tiles"][j]
                    b = tile_no[(*hd["id"], j)] % 2
                    pe.wait_ge(*when("probs", *hd["id"], j))
                    p = take("turned", *hd["id"], j)
                    for kt in range((nk + P - 1) // P):
                        rows = min(P, nk - kt * P)
                        mm = pe.transpose(p[0:rows, kt * P:kt * P + nq],
                                          probs[0:nq, b, kt * P:kt * P + rows], cst(C_IDENT, nq, nq))
                    mm.then_inc(*made("turned", *hd["id"], j))

                def values(hd):
                    for j in range(len(hd["tiles"])):
                        pe.wait_ge(*when("probs_t", *hd["id"], j))
                    p = take("attended", *hd["id"])
                    po, n, b = hd["po"], hd["n"], head_no[hd["id"]] % 2
                    for kt, (rows, v) in enumerate(hd["v"]):
                        q0 = kt * P if hd["kind"] == "fox" else 0
                        mm = pe.matmul(p[po:po + HD, q0:n], v, probs_t[0:rows, b, kt, q0:n],
                                       start=(kt == 0), stop=(kt == len(hd["v"]) - 1))
                    mm.then_inc(*made("attended", *hd["id"]))

                scores(0)
                owed = None
                for i, (hd, j) in enumerate(tiles):
                    if i + 1 < len(tiles):
                        scores(i + 1)
                    beside(i)
                    turn(i)
                    if owed is not None:
                        values(owed)
                        owed = None
                    if j == len(hd["tiles"]) - 1:
                        owed = hd
                values(owed)

            def gla_pairs(l, v):
                ntile = 4 if l == 0 else 2
                if v < 0:
                    pe.wait_ge(*when("projected", ("mix1", l), SLOT1[GLAQ]))
                    pe.wait_ge(*when("projected", ("mix1", l), SLOT1[GLAK]))
                else:
                    pe.wait_ge(*when("decayed", l, v))
                ps = [take("pairs", l, v, h) for h in range(4)]
                for t in range(ntile):
                    other = t ^ 1 if v == LEVELS else t
                    for h in range(4):
                        r = slice(32 * h, 32 * h + 32)
                        if v < 0:
                            q, k = proj1[r, GLAQ], proj1[r, GLAK]
                        else:
                            q, k = decay[r, v % 2, 0], decay[r, v % 2, 1]
                        mm = pe.matmul(ps[h][:, t * P:(t + 1) * P], k[:, t * P:(t + 1) * P],
                                       q[:, other * P:(other + 1) * P], start=True, stop=True,
                                       skip_group_check=True)
                        if t == ntile - 1:
                            mm.then_inc(*made("pairs", l, v, h))

            def gla_khat(l):
                pe.wait_ge(*when("khat_t", l))
                p = take("khat", l)
                for g in range(2):
                    for t in range(2):
                        mm = pe.transpose(p[:, (2 * g + t) * P:(2 * g + t + 1) * P],
                                          act_out[:, 0, g * NZ + t * P:g * NZ + (t + 1) * P], cst(C_IDENT))
                mm.then_inc(*made("khat", l))

            def gla_state(l):
                pe.wait_ge(*when("khat_sb", l))
                p = take("state", l)
                for g in range(2):
                    for t in range(2):
                        mm = pe.matmul(p[:, g * SEQ:(g + 1) * SEQ], khat[:, 2 * g + t],
                                       v1[:, 2 + t, GLAV:GLAV + 256], start=(t == 0), stop=(t == 1))
                mm.then_inc(*made("state", l))

            def gla_out(l, s, h):
                po = (h % 2) * HD
                p = take("gla_out", l, s, h)
                vcol = slice(GLAV + h * HD, GLAV + (h + 1) * HD)
                pe.wait_ge(*when("gla_scores", l, LEVELS - 1, h))
                pe.wait_ge(*when("gla_cross", l, h))
                for i in range(2):
                    out = p[po:po + HD, i * P:(i + 1) * P]
                    t, u = 2 * s + i, 2 * s + 1 - i
                    pe.matmul(out, v1[:, t, vcol], gla_s[:, h, t], start=True, stop=False)
                    mm = pe.matmul(out, v1[:, u, vcol], cross[:, h, u], start=False, stop=(s == 1))
                    if s == 0:
                        r = slice(32 * h, 32 * h + 32)
                        for g in range(2):
                            mm = pe.matmul(out, state[r, g, h * HD:(h + 1) * HD],
                                           act_out[r, 1, g * NX + i * P:g * NX + (i + 1) * P],
                                           start=False, stop=(g == 1))
                mm.then_inc(*made("gla_out", l, s, h))

            def rotation(tag, i, src, at, slot, n):
                pe.matmul(take("rotated", tag, i)[:, 0:n], at, src[:, slot, 0:n],
                          start=True, stop=True).then_inc(*made("rotated", tag, i))

            def beside_na(l, k):
                tm = ("mix1", l)
                if k < 7:
                    project(tm, PROJ1, 12 + k, N1, width1(l, PROJ1[12 + k]), proj1, VTEMP1,
                            [(t * P, P) for t in range(4)])
                if k == 7:
                    pe.wait_ge(*when("projected", tm, SLOT1[GATE]))
                    for g in range(2):
                        pe.matmul(take("gate_in", l, g), wgate[0:32, l, g * P:(g + 1) * P],
                                  proj1[0:32, GATE, 0:N1], start=True, stop=True).then_inc(*made("gate_in", l, g))
                if 8 <= k < 11:
                    head_mean(tm, k - 4, norm_items(l)[k - 4][2])
                if k == 11 or (k == 12 and l == 0):
                    dft_features(l, k - 11)
                if k == 13 or (k == 14 and l == 0):
                    dft_tokens(l, k - 13)
                if k >= 13:
                    pe.wait_ge(*when("head_normed", tm, k - 9))
                    rotation(tm, k - 13, proj1, cst(C_PERM64), rope_items[k - 13], NX)

            def beside_gqa(l, k):
                if k == 0:
                    gla_pairs(l, -1)
                if k == 1:
                    gla_khat(l)
                if k == 2:
                    gla_state(l)
                if 4 <= k <= 4 + LEVELS:
                    gla_pairs(l, k - 4)

            def beside_fox(l, k):
                tp = ("b2", l)
                if k < 16:
                    project(tp, PROJ2, 13 + k, N2, N2, proj2, VTEMP2, TILES2)
                if 6 <= k < 14:
                    pe.wait_ge(*when("projected", tp, 11 + k))
                    rotation(tp, k - 6, proj2, cst2(C_PERM128), RQ + k - 6, N2)
                if 16 <= k < 20:
                    ret_pairs(l, k - 16)
                if 17 <= k < 21:
                    ret_values(l, k - 17)
                if k >= 20:
                    ret_stat(l, "ret_mean", k - 20)

            def ret_pairs(l, h):
                pe.wait_ge(*when("roped", ("b2", l), h))
                pe.wait_ge(*when("roped", ("b2", l), 4 + h))
                p = take("ret_pairs", l, h)
                at = 0
                for j, (t0, tn) in enumerate(TILES2):
                    mm = pe.matmul(p[0:tn, at:at + N2 - t0], proj2[:, RK + h, t0:t0 + tn],
                                   proj2[:, RQ + h, t0:N2], start=True, stop=True, skip_group_check=True)
                    at += N2 - t0
                mm.then_inc(*made("ret_pairs", l, h))

            def ret_values(l, h):
                p = take("ret_out", l, h)
                for j, (t0, tn) in enumerate(TILES2):
                    pe.wait_ge(*when("ret_decayed", l, h, j))
                    mm = pe.matmul(p[:, t0:N2], v2[0:tn, j, 512 + h * P:512 + (h + 1) * P],
                                   ret_p[0:tn, h % 2, j, t0:N2], start=(j == 0), stop=(j == 2))
                mm.then_inc(*made("ret_out", l, h))

            def ret_stat(l, what, h):
                if what == "ret_mean":
                    pe.wait_ge(*when("ret_sb", l, h))
                    x = proj2[:, RQ + h, :]
                else:
                    pe.wait_ge(*when("ret_squares", l, h))
                    x = squares[:, h % 2, 0:N2]
                pe.matmul(take(what, l, h)[:, 0:N2], cst2(C_ONES128), x, start=True, stop=True).then_inc(
                    *made(what, l, h))

            pe.wait_ge(*when("c_cols_silu", 0))
            for j in range(FIRST_MOD):
                if j % 4 == 0:
                    p = take("first_rows", j // 4)
                pe.wait_ge(*when(f"first_mod_loaded{j % FIRST_SLOTS}", j))
                for k in range(2):
                    c = 2 * (j % 4) + k
                    mm = pe.matmul(p[0:2, :], c_cols[:, c], first_mod[:, j % FIRST_SLOTS, k], start=(c == 0),
                                   stop=(c == KC - 1))
                mm.then_inc(*made("first_mod", j))
                if j == 11:
                    pe.wait_ge(*when("consts_loaded", 0))
                    mean_square(("start",), N1)
            p = take("first_turned")
            for g in range(4):
                pe.wait_ge(*when("first_rows_sb", g))
                for j in range(4 * g, 4 * g + 4):
                    mm = pe.transpose(p[:, 2 * j:2 * j + 2], first_rows[:, j * P:(j + 1) * P], cst(C_IDENT, 2, 2))
            mm.then_inc(*made("first_turned"))
            for l in range(DEPTH):
                t1, tm, to, t2 = ("ffn1", l), ("mix1", l), ("out1", l), ("ffn2", l)
                n = N1 if l == 0 else NX
                ffn(t1, N1, N1, 2)
                mean_square(t1, N1)
                for i in range(12):
                    project(tm, PROJ1, i, N1, width1(l, PROJ1[i]), proj1, VTEMP1, [(t * P, P) for t in range(4)])
                    if i >= 9:
                        head_mean(tm, i - 9, norm_items(l)[i - 9][2])
                head_mean(tm, 3, N1)
                for i in range(4):
                    pe.wait_ge(*when("head_normed", tm, i))
                per = 1 + l
                attention(na_heads(l), lambda i: [beside_na(l, k) for k in range(per * i, per * (i + 1))])
                for i in range(3):
                    pe.wait_ge(*when("roped", tm, i))
                attention(gqa_heads(l), lambda i: [beside_gqa(l, k) for k in range(per * i, per * (i + 1))])
                pe.wait_ge(*when("state_sb", l))
                pe.wait_ge(*when("q_from_start", l))
                for s in range(2 - l):
                    for h in range(4):
                        gla_out(l, s, h)
                for i in range(2):
                    head_mean(("gla", l), i, n)
                project_out(to, N1, n, [0, 1, 2, 3, 6, 7, 4, 5])
                mean_square(to, n)
                ffn(t2, N1, n, 2 - l)
                mean_square(t2, n if l == 0 else N2)
            pe.wait_ge(*when("consts2_loaded", 0))
            for l in range(DEPTH):
                tp, to, tf = ("b2", l), ("out2", l), ("ffn", l)
                for i in range(13):
                    project(tp, PROJ2, i, N2, N2, proj2, VTEMP2, TILES2)
                pe.wait_ge(*when("negc", l))
                pe.wait_ge(*when("projected", tp, 11))
                pe.wait_ge(*when("projected", tp, 12))
                attention(fox_heads(l), lambda i: beside_fox(l, i))
                for h in range(4):
                    ret_stat(l, "ret_var", h)
                project_out(to, N2, N2, list(range(KC)))
                mean_square(to, N2)
                ffn(tf, N2, N2, 1)
                mean_square(tf, N2)
            assert unit[0] == UNITS, (unit[0], UNITS)

        @block.scalar
        def _(act):
            split = [0, 0]

            def split_ahead(used):
                split[1] += used
                while split[0] < min(split[1] + RING, UNITS):
                    u = split[0]
                    split[0] += 1
                    if u >= RING:
                        act.wait_ge(*when("unit_used", u - RING))
                    act.wait_ge(unit_loaded[u % RING], 16 * (u // RING + 1))
                    act.activation(high[:, u % RING], ring[:, u % RING], ACT.Copy).then_inc(high_parts, 1)

            def ln_exp():
                act.preload_act_table_set(LN_EXP)

            def inverse_root(out, p, n, tag, frees):
                act.activation(out[:, 0:n], p[:, 0:n], ACT.Ln, bias=eps_one[:, 0:1]).then_inc(
                    *made("ln_mean", tag, frees=frees))
                act.wait_ge(*when("ln_mean", tag))
                act.activation(out[:, 0:n], out[:, 0:n], ACT.Exp, scale=-0.5).then_inc(*made("rstd", tag))

            def square(tag, cols, n, d):
                out = sumsq[:, 0:n] if d == 0 else squares[:, d % 2, 0:n]
                if d >= 3:
                    act.wait_ge(*when("sumsq", tag, d - 2))
                act.activation(out, resid[:, d, cols:cols + n], ACT.Square).then_inc(*made("resid_squares", tag, d))

            def root_of_mean(tag, n):
                ln_exp()
                act.wait_ge(*when("mean", tag))
                p = bank("mean", tag)
                inverse_root(rstd[:, 0], p, n, tag, ("mean", tag))

            def high_part(tag, out, c, n, whole, ready):
                act.wait_ge(*ready)
                act.activation(out[0][:, c, 0:n], whole, ACT.Copy).then_inc(*made("x_high", tag, c))

            def norm1(to, l, m, n):
                hi, _ = x_parts(N1)
                act.wait_ge(*when("mod", l, m))
                for c in range(KC):
                    act.wait_ge(*when("scaled", to, c))
                    for s, a, b in BOTH if n == N1 else ONLY_X:
                        last = act.activation(hi[:, c, a:b], scaled[:, c, a:b], ACT.Identity,
                                              bias=mod[:, l, s, m * KC + c:m * KC + c + 1])
                    last.then_inc(*made("x_high", to, c))
                    if c % 2:
                        for s, a, b in BOTH if n == N1 else ONLY_X:
                            last = act.activation(scaled[:, c, a:b], scaled[:, c, a:b], ACT.Identity,
                                                  bias=mod[:, l, s, m * KC + c:m * KC + c + 1])
                        last.then_inc(*made("shifted", to, c))

            def norm2(to):
                for c in range(KC):
                    high_part(to, x_parts(N2), c, N2, scaled[:, c, 0:N2], when("scaled", to, c))

            def ffn(tag, n, parts, cols, nsq):
                hh, _ = hidden_parts(n, parts)
                nf = FC // parts
                for h in range(parts):
                    for f in range(nf + 1):
                        if f < nf:
                            act.wait_ge(*when("gate", tag, h, f))
                            p = bank("gate", tag, h, f)
                            if f >= 2:
                                act.wait_ge(*when("hidden", tag, h, f - 2))
                            act.activation(act_out[:, f % 2, 0:n], p[:, 0:n], ACT.Silu).then_inc(
                                *made("silu", tag, h, f, frees=("gate", tag, h, f)))
                            split_ahead(1)
                        if f >= 1:
                            act.wait_ge(*when("hidden", tag, h, f - 1))
                            act.activation(hh[:, f - 1], fresh[:, (f - 1) % 2, 0:n], ACT.Copy).then_inc(
                                *made("hidden_high", tag, h, f - 1))
                        if f < nf:
                            split_ahead(1)
                    for d in range(KC):
                        split_ahead((d + 1) * nf // KC - d * nf // KC)
                        if h == parts - 1:
                            act.wait_ge(*when("resid", tag, h, d))
                            square(tag, cols, nsq, d)

            def project(tag, plan, i, n, src, vtemp, l):
                kind, dst, width = plan[i][:3]
                if i and plan[i - 1][0] == "V" and (i - 1) % 2:
                    act.wait_ge(*when("v_turned", tag, i - 1))
                    p = bank("v_turned", tag, i - 1).rearrange("p (t n) -> p t n", t=4)
                    v0 = plan[i - 1][1]
                    if tag[0] == "mix1":
                        act.activation(v1[:, :, v0:v0 + P], p, ACT.Copy).then_inc(
                            *made("v_placed_act", tag, i - 1, frees=("v_turned", tag, i - 1)))
                    else:
                        act.activation(v2[:, 0:2, v0:v0 + P], p[:, 0:2], ACT.Copy)
                        act.activation(v2[0:META, 2, v0:v0 + P], p[0:META, 2], ACT.Copy).then_inc(
                            *made("v_placed_act", tag, i - 1, frees=("v_turned", tag, i - 1)))
                if on_act(tag, i):
                    act.wait_ge(*when("proj", tag, i))
                    p = bank("proj", tag, i)
                    func, scale = ACT.Copy, 1.0
                    if kind == "V":
                        dst, width = vtemp[i], P
                    elif tag[0] == "mix1":
                        scale = 32 ** -0.5 if dst == GLAQ else 1.0
                        func = ACT.Silu if GLAR <= dst < GLAR + 2 else ACT.Copy
                    else:
                        scale = HD ** -0.5 if FQ <= dst < FQ + 4 else 1.0
                        func = ACT.Silu if dst >= RG else ACT.Copy
                    out = negc[0:8, 0, :] if dst == FLOG else src[0:width, dst, 0:n]
                    act.activation(out, p[0:width, 0:n], func, scale=scale).then_inc(
                        *made("projected_act", tag, i, frees=("proj", tag, i)))
                    ev.table[("projected", tag, i)] = ev.table[("projected_act", tag, i)]
                    if func == ACT.Silu and not (i + 1 < len(plan) and plan[i + 1][1] in (GLAR + 1,)):
                        ln_exp()
                split_ahead(1)

            def head_square(tag, i, ready, x, n):
                act.wait_ge(*ready)
                if i >= 2:
                    act.wait_ge(*when("head_mean", tag, i - 2))
                act.activation(squares[:, i % 2, 0:n], x, ACT.Square).then_inc(*made("head_squares", tag, i))

            def head_root(tag, i, n):
                act.wait_ge(*when("head_mean", tag, i))
                p = bank("head_mean", tag, i)
                if i >= 2:
                    act.wait_ge(*when("head_normed", tag, i - 2))
                inverse_root(rstd[:, i % 2], p, n, (tag, i), ("head_mean", tag, i))

            def qk_square(l, i):
                tm, (slot, _, n) = ("mix1", l), norm_items(l)[i]
                head_square(tm, i, when("projected", tm, SLOT1[slot]), proj1[:, slot, 0:n], n)

            def attention(heads, beside):
                tiles = [(hd, j) for hd in heads for j in range(len(hd["tiles"]))]

                def exps(i):
                    hd, j = tiles[i]
                    q0, nq, nk = hd["tiles"][j]
                    key = (*hd["id"], j)
                    no = tile_no[key]
                    st = stat[0:nq, no % 4]
                    act.wait_ge(*when("row_max", *key))
                    if no >= 2:
                        act.wait_ge(*when("turned", *tile_keys[no - 2]))
                    out = probs[0:nq, no % 2]
                    p = bank("scores", *key)
                    if hd["kind"] == "na":
                        act.activation(out[:, 0:NX], biased_x[:, no % 2], ACT.Exp, bias=st[:, 3:4],
                                       accum_out=st[:, 4:5])
                        act.activation(out[:, NX:N1], p[:, NX:N1], ACT.Exp, bias=st[:, 3:4],
                                       accum_out=st[:, 5:6]).then_inc(*made("exps", *key, frees=("scores", *key)))
                    elif hd["kind"] == "fox":
                        act.activation(out[:, 0:nk], biased[0:nq, no % 2, 0:nk], ACT.Exp, bias=st[:, 3:4],
                                       accum_out=st[:, 4:5]).then_inc(*made("exps", *key))
                    else:
                        act.activation(out[:, 0:nk], p[:, 0:nk], ACT.Exp, bias=st[:, 3:4],
                                       accum_out=st[:, 4:5]).then_inc(*made("exps", *key, frees=("scores", *key)))

                def turned(i):
                    hd, j = tiles[i]
                    q0, nq, nk = hd["tiles"][j]
                    key = (*hd["id"], j)
                    no = head_no[hd["id"]]
                    act.wait_ge(*when("turned", *key))
                    p = bank("turned", *key).rearrange("p (k n) -> p k n", k=4)
                    if no >= 2 and j == 0:
                        act.wait_ge(*when("attended", *every[no - 2]["id"]))
                    full = nk // P
                    last = act.activation(probs_t[:, no % 2, 0:full, q0:q0 + nq], p[:, 0:full, 0:nq], ACT.Copy)
                    if nk % P:
                        last = act.activation(probs_t[0:nk % P, no % 2, full, q0:q0 + nq],
                                              p[0:nk % P, full, 0:nq], ACT.Copy)
                    last.then_inc(*made("probs_t", *key, frees=("turned", *key)))

                for i in range(len(tiles)):
                    exps(i)
                    if i >= 1:
                        turned(i - 1)
                    beside(i)
                turned(len(tiles) - 1)

            biased_x = biased.rearrange("p b n -> p (b n)")[:, 0:2 * NX].rearrange("p (b n) -> p b n", b=2)

            def gla_gates(l):
                for g in range(2):
                    act.wait_ge(*when("neg_abs", l, g))
                    act.activation(decay[:, 0, g], decay[:, 0, g], ACT.Exp).then_inc(*made("gate_exp", l, g))
                for g in range(2):
                    act.wait_ge(*when("gate_exp", l, g))
                    act.activation(decay[:, 0, g], decay[:, 0, g], ACT.Ln, bias=eps_one[:, 1:2]).then_inc(
                        *made("gate_ln", l, g))

            def gla_ends(l):
                act.wait_ge(*when("z_exponents", l, 1))
                act.activation(act_out[:, 0, :], act_out[:, 0, :], ACT.Exp, scale=1.0 / 16).then_inc(
                    *made("z_decays", l))
                for g in range(2):
                    act.activation(act_out[:, 1, g * NX:(g + 1) * NX], gates[:, g, 0:NX], ACT.Exp,
                                   scale=1.0 / 16).then_inc(*made("x_decays", l, g))

            def beside_na(l, k):
                tm = ("mix1", l)
                if k < 7:
                    project(tm, PROJ1, 12 + k, width1(l, PROJ1[12 + k]), proj1, VTEMP1, l)
                if k == 8:
                    gla_gates(l)
                if 8 <= k < 11:
                    qk_square(l, k - 4)
                if 9 <= k < 12:
                    head_root(tm, k - 5, norm_items(l)[k - 5][2])
                if k == 11:
                    gla_ends(l)

            def beside_gqa(l, k):
                n = N1 if l == 0 else NX
                if k == 1:
                    act.wait_ge(*when("khat", l))
                    p = bank("khat", l)
                    act.activation(khat, p.rearrange("p (t n) -> p t n", t=4), ACT.Copy).then_inc(
                        *made("khat_sb", l, frees=("khat", l)))
                if k == 2:
                    act.wait_ge(*when("state", l))
                    p = bank("state", l)
                    act.activation(state, p.rearrange("p (g n) -> p g n", g=2), ACT.Copy).then_inc(
                        *made("state_sb", l, frees=("state", l)))
                if 3 <= k <= 3 + LEVELS:
                    v = k - 3
                    act.wait_ge(*when("exponents", l, v, 3))
                    act.activation(decay[:, v % 2, :, 0:n], decay[:, v % 2, :, 0:n], ACT.Exp,
                                   scale=1.0 / 16).then_inc(*made("decays", l, v))
                if k == 5 + LEVELS:
                    for h in range(4):
                        act.wait_ge(*when("pairs", l, LEVELS, h))
                        p = bank("pairs", l, LEVELS, h)
                        act.activation(cross[:, h, 0:n // P], p[:, 0:n].rearrange("p (t n) -> p t n", n=P),
                                       ACT.Copy).then_inc(*made("gla_cross", l, h, frees=("pairs", l, LEVELS, h)))

            def beside_fox(l, k):
                if k < 16:
                    project(("b2", l), PROJ2, 13 + k, N2, proj2, VTEMP2, l)
                if 17 <= k < 21:
                    h = k - 17
                    act.wait_ge(*when("ret_out", l, h))
                    p = bank("ret_out", l, h)
                    act.activation(proj2[:, RQ + h, :], p[:, 0:N2], ACT.Copy).then_inc(
                        *made("ret_sb", l, h, frees=("ret_out", l, h)))
                if k >= 22:
                    ret_square(l, k - 22)

            def ret_square(l, h):
                act.wait_ge(*when("ret_centred", l, h))
                if h >= 2:
                    act.wait_ge(*when("ret_var", l, h - 2))
                act.activation(squares[:, h % 2, 0:N2], proj2[:, RQ + h, :], ACT.Square).then_inc(
                    *made("ret_squares", l, h))

            def ret_root(l, h):
                act.wait_ge(*when("ret_var", l, h))
                p = bank("ret_var", l, h)
                if h >= 2:
                    act.wait_ge(*when("ret_normed", l, h - 2))
                inverse_root(rstd[:, h % 2], p, N2, ("ret", l, h), ("ret_var", l, h))

            act.wait_ge(*when("c_cols_loaded", 0))
            act.activation(c_cols, c_cols, ACT.Silu).then_inc(*made("c_cols_silu", 0))
            act.wait_ge(*when("eps_one", 1))
            act.wait_ge(*when("x_loaded", 0))
            act.wait_ge(*when("ctx_loaded", 0))
            for d in range(KC):
                square(("start",), META, N1, d)
            split_ahead(0)
            root_of_mean(("start",), N1)
            norm1(("ffn1", 0), 0, 0, N1)
            for s in range(2):
                act.wait_ge(*when("c_ctx_loaded" if s else "c_loaded"))
                act.activation(csilu[:, s], csilu[:, s], ACT.Silu).then_inc(*made("c_silu", s))
            for l in range(DEPTH):
                t1, tm, to, t2 = ("ffn1", l), ("mix1", l), ("out1", l), ("ffn2", l)
                n = N1 if l == 0 else NX
                ffn(t1, N1, 2, META, N1)
                root_of_mean(t1, N1)
                norm1(tm, l, 3, N1)
                for i in range(12):
                    project(tm, PROJ1, i, width1(l, PROJ1[i]), proj1, VTEMP1, l)
                    if i >= 8:
                        qk_square(l, i - 8)
                    if i >= 9:
                        head_root(tm, i - 9, norm_items(l)[i - 9][2])
                head_root(tm, 3, N1)
                per = 1 + l
                attention(na_heads(l), lambda i: [beside_na(l, k) for k in range(per * i, per * (i + 1))])
                attention(gqa_heads(l), lambda i: [beside_gqa(l, k) for k in range(per * i, per * (i + 1))])
                act.wait_ge(*when("gla_out", l, 1 - l, 3))
                for c in range(4):
                    s = MIX1[c]
                    high_part(to, x_parts(N1), c, n, proj1[:, s, 0:n],
                              when("attended_sb", "nax" if l else "naz", l, 3) if c > 1 else when("dft_mix", l, 1 - l))
                for i in range(2):
                    head_square(("gla", l), i, when("gla_out_sb", l, 1 - l, 2 * i + 1), proj1[:, GLAQ + i, 0:n], n)
                for i in range(2):
                    head_root(("gla", l), i, n)
                for c in (6, 7, 4, 5):
                    high_part(to, x_parts(N1), c, n, proj1[:, MIX1[c], 0:n],
                              when("attended_sb", "gqax" if l else "gqaz", l, 3) if c > 5 else when("mix_gla", l, c - 4))
                for d in range(KC):
                    split_ahead(1)
                    act.wait_ge(*when("resid", to, 0, d))
                    square(to, META, n, d)
                root_of_mean(to, n)
                norm1(t2, l, 6, n)
                if l == 1:
                    act.wait_ge(*when("meta_loaded", 0))
                ffn(t2, n, 2 - l, META if l == 0 else 0, n if l == 0 else N2)
                root_of_mean(t2, n if l == 0 else N2)
                if l == 0:
                    norm1(("ffn1", 1), 1, 0, N1)
                else:
                    norm2(("b2", 0))
            for l in range(DEPTH):
                tp, to, tf = ("b2", l), ("out2", l), ("ffn", l)
                for i in range(13):
                    project(tp, PROJ2, i, N2, proj2, VTEMP2, l)
                    if i == 6:
                        act.wait_ge(*when("flog_neg_abs", l))
                        act.activation(negc[0:8, 1, :], negc[0:8, 1, :], ACT.Exp).then_inc(*made("flog_exp", l))
                        act.wait_ge(*when("flog_exp", l))
                        act.activation(negc[0:8, 1, :], negc[0:8, 1, :], ACT.Ln, bias=eps_one[0:8, 1:2]).then_inc(
                            *made("flog_ln", l))
                attention(fox_heads(l), lambda i: beside_fox(l, i))
                ret_root(l, 0)
                ret_square(l, 2)
                ret_root(l, 1)
                ret_square(l, 3)
                ret_root(l, 2)
                ret_root(l, 3)
                act.wait_ge(*when("ret_out", l, 3))
                for c in range(KC):
                    high_part(to, x_parts(N2), c, N2, proj2[:, MIX2[c], :],
                              when("attended_sb", "fox", l, 7) if c < 4 else when("mix_ret", l, c - 4))
                for d in range(KC):
                    split_ahead(1)
                    act.wait_ge(*when("resid", to, 0, d))
                    square(to, 0, N2, d)
                root_of_mean(to, N2)
                norm2(tf)
                ffn(tf, N2, 1, 0, N2)
                root_of_mean(tf, N2)
                if l + 1 < DEPTH:
                    norm2(("b2", l + 1))

        @block.vector
        def _(dve):
            split = [0, 0]

            def split_ahead(used):
                split[1] += used
                while split[0] < min(split[1] + RING, UNITS):
                    u = split[0]
                    split[0] += 1
                    dve.wait_ge(high_parts, u + 1)
                    dve.tensor_tensor(low[:, u % RING], ring[:, u % RING], high_f[:, u % RING],
                                      ALU.subtract).then_inc(low_parts, 1)

            def mod_dot(l, j):
                n = l * NMOD * KC + j
                streams = 1 if (l == 1 and j >= 5 * KC) else 2
                dve.wait_ge(*when(f"mod_loaded{n % MOD_RING}", n))
                for s in range(streams):
                    dve.wait_ge(*when("c_silu", s))
                    if dots[s] is not None:
                        dve.wait_ge(*when(*dots[s]))
                    dots[s] = ("mod_dot", n) if s == streams - 1 else ("mod_dot_x", n)
                    dve.tensor_tensor_reduce(junk[:, s], mod_ring[:, n % MOD_RING], csilu[:, s], 1.0, 0.0,
                                             ALU.mult, ALU.add, mod_raw[:, l, s, j:j + 1]).then_inc(*made(*dots[s]))
                if j % KC == KC - 1:
                    mod_finish(l, j // KC, streams)

            dots = [None, None]

            def mod_finish(l, m, streams):
                cols = slice(m * KC, (m + 1) * KC)
                if l == 0 and m < 2:
                    dve.wait_ge(*when("first_mod_raw"))
                else:
                    dve.wait_ge(*when("mod_dot", l * NMOD * KC + m * KC + KC - 1))
                at = l * SW1 + S_L1["bmod"] + m * KC
                b = small[:, at:at + KC].unsqueeze(1).broadcast_to([P, streams, KC])
                add = 1.0 if m in (1, 4, 7) else 0.0
                dve.scalar_tensor_tensor(mod[:, l, 0:streams, cols], mod_raw[:, l, 0:streams, cols], add, b,
                                         ALU.add, ALU.add).then_inc(*made("mod_sum", l, m))
                dve.wait_ge(*when("mod_sum", l, m))
                half = 0.5 if m in (2, 8) else 1.0
                dve.tensor_scalar(mod[:, l, 0:streams, cols], mod[:, l, 0:streams, cols], half, None,
                                  ALU.mult).then_inc(*made("mod", l, m))

            def sum_squares(tag, n, d):
                dve.wait_ge(*when("resid_squares", tag, d))
                if d == 0:
                    return
                if d >= 2:
                    dve.wait_ge(*when("sumsq", tag, d - 1))
                dve.tensor_tensor(sumsq[:, 0:n], sumsq[:, 0:n], squares[:, d % 2, 0:n], ALU.add).then_inc(
                    *made("sumsq", tag, d))

            def low_part(tag, out, c, n, whole):
                dve.wait_ge(*when("x_high", tag, c))
                dve.tensor_tensor(out[1][:, c, 0:n], whole, out[0][:, c, 0:n].bitcast(F32),
                                  ALU.subtract).then_inc(*made("x_low_dve", tag, c))
                ev.table[("x_low", tag, c)] = ev.table[("x_low_dve", tag, c)]

            def norm1(tag, to, l, m, n):
                streams = BOTH if n == N1 else ONLY_X
                hi, lo = x_parts(N1)
                dve.wait_ge(*when("mod", l, m))
                dve.wait_ge(*when("mod", l, m + 1))
                dve.wait_ge(*when("rstd", tag))
                for c in range(KC + 1):
                    if c < KC:
                        for s, a, b in streams:
                            last = dve.scalar_tensor_tensor(scaled[:, c, a:b], resid[:, c, META + a:META + b],
                                                            mod[:, l, s, (m + 1) * KC + c:(m + 1) * KC + c + 1],
                                                            rstd[:, 0, a:b], ALU.mult, ALU.mult)
                        last.then_inc(*made("scaled", to, c))
                    if c % 2:
                        e = c - 1
                        dve.wait_ge(*when("x_high", to, e))
                        for s, a, b in streams:
                            last = dve.scalar_tensor_tensor(lo[:, e, a:b], scaled[:, e, a:b],
                                                            mod[:, l, s, m * KC + e:m * KC + e + 1],
                                                            hi[:, e, a:b].bitcast(F32), ALU.add, ALU.subtract)
                        last.then_inc(*made("x_low_dve", to, e))
                        ev.table[("x_low", to, e)] = ev.table[("x_low_dve", to, e)]

            def norm2(tag, to, l, name):
                dve.wait_ge(*when("rstd", tag))
                for c in range(KC + 1):
                    if c < KC:
                        dve.scalar_tensor_tensor(scaled[:, c, 0:N2], resid[:, c, 0:N2], scalar2(l, name, c),
                                                 rstd[:, 0, 0:N2], ALU.mult, ALU.mult).then_inc(
                                                     *made("scaled", to, c))
                    if c % 2:
                        low_part(to, x_parts(N2), c - 1, N2, scaled[:, c - 1, 0:N2])

            def ffn(tag, n, parts, l=None):
                nf = FC // parts
                for f in range(parts * nf):
                    h, g = f // nf, f % nf
                    split_ahead(1)
                    todo = list(mod_chunks(l, f)) if l is not None else []
                    for j in todo[:len(todo) // 2]:
                        mod_dot(l, j)
                    dve.wait_ge(*when("up", tag, h, g))
                    p = bank("up", tag, h, g)
                    dve.wait_ge(*when("silu", tag, h, g))
                    if g >= 2:
                        dve.wait_ge(*when("hidden_low", tag, h, g - 2))
                    dve.tensor_tensor(fresh[:, g % 2, 0:n], act_out[:, g % 2, 0:n], p[:, 0:n], ALU.mult).then_inc(
                        *made("hidden", tag, h, g, frees=("up", tag, h, g)))
                    split_ahead(1)
                    for j in todo[len(todo) // 2:]:
                        mod_dot(l, j)
                    if g == nf - 1:
                        yield h

            def residual(tag, l, m, streams, n, cols, nsq, h, last_part, ahead):
                for d in range(KC):
                    split_ahead(ahead(d))
                    dve.wait_ge(*when("down", tag, h, d))
                    p = bank("down", tag, h, d)
                    if m is None:
                        last = dve.tensor_tensor(resid[:, d, cols:cols + n], resid[:, d, cols:cols + n], p[:, 0:n],
                                                 ALU.add)
                    else:
                        dve.wait_ge(*when("mod", l, m))
                        for s, a, b in streams:
                            last = dve.scalar_tensor_tensor(resid[:, d, META + a:META + b], p[:, a:b],
                                                            mod[:, l, s, m * KC + d:m * KC + d + 1],
                                                            resid[:, d, META + a:META + b], ALU.mult, ALU.add)
                    last.then_inc(*made("resid", tag, h, d, frees=("down", tag, h, d)))
                    if d >= 1 and last_part:
                        sum_squares(tag, nsq, d - 1)
                if last_part:
                    sum_squares(tag, nsq, KC - 1)

            def project(tag, plan, i, n, src, vtemp):
                kind, dst, width = plan[i][:3]
                if i and plan[i - 1][0] == "V" and (i - 1) % 2 == 0:
                    dve.wait_ge(*when("v_turned", tag, i - 1))
                    p = bank("v_turned", tag, i - 1).rearrange("p (t n) -> p t n", t=4)
                    v0 = plan[i - 1][1]
                    if tag[0] == "mix1":
                        dve.tensor_copy(v1[:, :, v0:v0 + P], p).then_inc(
                            *made("v_placed_dve", tag, i - 1, frees=("v_turned", tag, i - 1)))
                    else:
                        dve.tensor_copy(v2[:, 0:2, v0:v0 + P], p[:, 0:2])
                        dve.tensor_copy(v2[0:META, 2, v0:v0 + P], p[0:META, 2]).then_inc(
                            *made("v_placed_dve", tag, i - 1, frees=("v_turned", tag, i - 1)))
                if not on_act(tag, i):
                    dve.wait_ge(*when("proj", tag, i))
                    p = bank("proj", tag, i)
                    scale = 1.0
                    if kind == "V":
                        dst, width = vtemp[i], P
                    elif tag[0] == "b2" and FQ <= dst < FQ + 4:
                        scale = HD ** -0.5
                    out = negc[0:8, 0, :] if dst == FLOG else src[0:width, dst, 0:n]
                    dve.tensor_scalar(out, p[0:width, 0:n], scale, None, ALU.mult).then_inc(
                        *made("projected_dve", tag, i, frees=("proj", tag, i)))
                    ev.table[("projected", tag, i)] = ev.table[("projected_dve", tag, i)]
                split_ahead(1)

            def head_norm(tag, i, x, gain, n, *ready):
                dve.wait_ge(*when("rstd", (tag, i)))
                dve.wait_ge(*when(*ready))
                dve.scalar_tensor_tensor(x, x, gain, rstd[:, i % 2, 0:n], ALU.mult, ALU.mult).then_inc(
                    *made("head_normed", tag, i))

            def qk_norm(l, i):
                slot, gain, n = norm_items(l)[i]
                head_norm(("mix1", l), i, proj1[:, slot, 0:n], scalar1(l, gain), n, "projected", ("mix1", l),
                          SLOT1[slot])

            def rope(tag, i, x, cos, sin, n, *ready):
                dve.wait_ge(*when("rotated", tag, i))
                p = bank("rotated", tag, i)
                if i >= 1:
                    dve.wait_ge(*when("roped", tag, i - 1))
                dve.wait_ge(*when(*ready))
                dve.tensor_tensor(fresh[:, 0, 0:n], p[:, 0:n], sin, ALU.mult).then_inc(
                    *made("rope_sin", tag, i, frees=("rotated", tag, i)))
                dve.tensor_tensor(fresh[:, 1, 0:n], x, cos, ALU.mult).then_inc(*made("rope_cos", tag, i))
                dve.wait_ge(*when("rope_cos", tag, i))
                dve.tensor_tensor(x, fresh[:, 0, 0:n], fresh[:, 1, 0:n], ALU.add).then_inc(*made("roped", tag, i))

            biased_x = biased.rearrange("p b n -> p (b n)")[:, 0:2 * NX].rearrange("p (b n) -> p b n", b=2)

            def attention(heads, beside):
                tiles = [(hd, j) for hd in heads for j in range(len(hd["tiles"]))]

                def maxima(i):
                    hd, j = tiles[i]
                    q0, nq, nk = hd["tiles"][j]
                    key = (*hd["id"], j)
                    no = tile_no[key]
                    st = stat[0:nq, no % 4]
                    dve.wait_ge(*when("scores", *key))
                    p = bank("scores", *key)
                    if no >= 2:
                        dve.wait_ge(*when("exps", *tile_keys[no - 2]))
                    if hd["kind"] == "na":
                        dve.wait_ge(*when("bias_loaded", hd["id"][1]))
                        at = hd["h"] * 6 * 64 + (2 - 2 * j) * 64
                        dve.tensor_tensor_reduce(biased_x[:, no % 2], p[:, 0:NX], bias[:, at:at + NX], 1.0, -3e38,
                                                 ALU.add, ALU.max, st[:, 0:1]).then_inc(*made("win_max", *key))
                        dve.tensor_reduce(st[:, 1:2], p[:, NX:N1], AX.X, ALU.max).then_inc(*made("ctx_max", *key))
                        dve.wait_ge(*when("win_max", *key))
                        dve.wait_ge(*when("ctx_max", *key))
                        dve.tensor_scalar(st[:, 3:4], st[:, 0:1], st[:, 1:2], -1.0, ALU.max, ALU.mult).then_inc(
                            *made("row_max", *key))
                        return
                    if hd["kind"] == "fox":
                        dve.tensor_tensor_reduce(biased[0:nq, no % 2, 0:nk], p[0:nq, 0:nk],
                                                 cst2(C_CAUSAL + 2 * P - q0, nk, nq), 1.0, -3e38, ALU.add, ALU.max,
                                                 st[:, 0:1]).then_inc(*made("win_max", *key, frees=("scores", *key)))
                    else:
                        dve.tensor_reduce(st[:, 0:1], p[0:nq, 0:nk], AX.X, ALU.max).then_inc(*made("win_max", *key))
                    dve.wait_ge(*when("win_max", *key))
                    dve.tensor_scalar(st[:, 3:4], st[:, 0:1], -1.0, None, ALU.mult).then_inc(*made("row_max", *key))

                def normalise(i):
                    hd, j = tiles[i]
                    q0, nq, nk = hd["tiles"][j]
                    key = (*hd["id"], j)
                    no = tile_no[key]
                    st = stat[0:nq, no % 4]
                    dve.wait_ge(*when("exps", *key))
                    src = st[:, 4:5]
                    if hd["kind"] == "na":
                        dve.tensor_tensor(st[:, 6:7], st[:, 4:5], st[:, 5:6], ALU.add).then_inc(*made("row_sum", *key))
                        dve.wait_ge(*when("row_sum", *key))
                        src = st[:, 6:7]
                    dve.reciprocal(st[:, 7:8], src).then_inc(*made("row_inv", *key))
                    dve.wait_ge(*when("row_inv", *key))
                    dve.tensor_scalar(probs[0:nq, no % 2, 0:nk], probs[0:nq, no % 2, 0:nk], st[:, 7:8], None,
                                      ALU.mult).then_inc(*made("probs", *key))

                def attended(hd):
                    dve.wait_ge(*when("attended", *hd["id"]))
                    p = bank("attended", *hd["id"])
                    dve.tensor_copy(hd["out"], p[hd["po"]:hd["po"] + HD, 0:hd["n"]]).then_inc(
                        *made("attended_sb", *hd["id"], frees=("attended", *hd["id"])))

                maxima(0)
                owed = []
                for i, (hd, j) in enumerate(tiles):
                    if i + 1 < len(tiles):
                        maxima(i + 1)
                    normalise(i)
                    beside(i)
                    if owed and owed[0][0] < i:
                        attended(owed.pop()[1])
                    if j == len(hd["tiles"]) - 1:
                        owed = [(i, hd)]
                attended(owed[0][1])

            def gla_log_gates(l):
                for g in range(2):
                    dve.wait_ge(*when("gate_in", l, g))
                    p = bank("gate_in", l, g)
                    y, e = decay[:, 1, g], decay[:, 0, g]
                    dve.tensor_scalar(y, p, scalar1(l, "bf" if g == 0 else "bb"), None, ALU.add).then_inc(
                        *made("gate_y", l, g, frees=("gate_in", l, g)))
                    dve.wait_ge(*when("gate_y", l, g))
                    dve.scalar_tensor_tensor(e, y, -1.0, y, ALU.mult, ALU.min).then_inc(*made("neg_abs", l, g))

            def gla_sums(l):
                for g in range(2):
                    y, e = decay[:, 1, g], decay[:, 0, g]
                    dve.wait_ge(*when("gate_ln", l, g))
                    dve.scalar_tensor_tensor(e, y, 0.0, e, ALU.min, ALU.subtract).then_inc(*made("log_gate", l, g))
                    dve.wait_ge(*when("log_gate", l, g))
                    for s in range(2):
                        a, b = s * NX, (s + 1) * NX
                        if g == 0:
                            o, i = gates[:, 0, a:b], e[:, a:b]
                        else:
                            stop = a - 1 if a else None
                            o, i = gates[:, 1, b - 1:stop:-1], e[:, b - 1:stop:-1]
                        dve.tensor_tensor_scan(o, eps_one[:, 1:2].broadcast_to([P, NX]), i, 0.0, ALU.mult,
                                               ALU.add).then_inc(*made("gate_sums", l, g, s))
                dve.wait_ge(*when("gate_sums", l, 1, 1))
                for g, edge in ((0, N1 - 1), (1, NX)):
                    dve.tensor_scalar(act_out[:, 0, g * NZ:(g + 1) * NZ], gates[:, g, NX:N1], gates[:, g, edge:edge + 1],
                                      -1.0, ALU.subtract, ALU.mult).then_inc(*made("z_exponents", l, g))

            def gla_ends(l):
                dve.wait_ge(*when("projected", ("mix1", l), SLOT1[GLAQ]))
                dve.wait_ge(*when("projected", ("mix1", l), SLOT1[GLAK]))
                dve.wait_ge(*when("z_decays", l))
                dve.tensor_tensor(act_out[:, 0].rearrange("p (g n) -> p g n", g=2),
                                  act_out[:, 0].rearrange("p (g n) -> p g n", g=2),
                                  proj1[:, GLAK:GLAK + 1, NX:N1].broadcast_to([P, 2, NZ]), ALU.mult).then_inc(
                                      *made("khat_t", l))
                dve.wait_ge(*when("x_decays", l, 1))
                dve.tensor_tensor(act_out[:, 1].rearrange("p (g n) -> p g n", g=2),
                                  act_out[:, 1].rearrange("p (g n) -> p g n", g=2),
                                  proj1[:, GLAQ:GLAQ + 1, 0:NX].broadcast_to([P, 2, NX]), ALU.mult).then_inc(
                                      *made("q_from_start", l))

            def beside_na(l, k):
                tm = ("mix1", l)
                if k < 7:
                    project(tm, PROJ1, 12 + k, width1(l, PROJ1[12 + k]), proj1, VTEMP1)
                if k == 7:
                    gla_log_gates(l)
                if k == 9:
                    gla_sums(l)
                if 9 <= k < 12:
                    qk_norm(l, k - 5)
                if k == 11 or (k == 12 and l == 0):
                    for t in range(2):
                        dve.wait_ge(*when("dft_d", l, k - 11, t))
                        p = bank("dft_d", l, k - 11, t)
                        dve.tensor_copy(dft_ab[:, k - 11, t], p).then_inc(
                            *made("dft_ab", l, k - 11, t, frees=("dft_d", l, k - 11, t)))
                if k == 12:
                    gla_ends(l)
                if k == 13 or (k == 14 and l == 0):
                    s = k - 13
                    dve.wait_ge(*when("dft_l", l, s))
                    p = bank("dft_l", l, s)
                    dve.tensor_copy(proj1[:, FOUR:FOUR + 2, s * NX:(s + 1) * NX],
                                    p.rearrange("p (g n) -> p g n", g=2)).then_inc(
                                        *made("dft_mix", l, s, frees=("dft_l", l, s)))
                if k >= 13:
                    i = k - 13
                    rope(tm, i, proj1[:, rope_items[i], 0:NX], cst(C_COS1, NX), cst(C_SIN1, NX), NX,
                         "head_normed", tm, 4 + i)

            def beside_gqa(l, k):
                n = N1 if l == 0 else NX
                ntile = n // P
                if k == 0:
                    for h in range(4):
                        dve.wait_ge(*when("pairs", l, -1, h))
                        p = bank("pairs", l, -1, h)
                        dve.tensor_scalar(gla_s[:, h, 0:ntile], p[:, 0:n].rearrange("p (t n) -> p t n", n=P), 2.0,
                                          None, ALU.mult).then_inc(
                                              *made("gla_scores", l, -1, h, frees=("pairs", l, -1, h)))
                if 3 <= k <= 3 + LEVELS:
                    v = k - 3
                    dve.wait_ge(*when("decays", l, v))
                    dve.tensor_tensor(decay[:, v % 2, :, 0:n], decay[:, v % 2, :, 0:n],
                                      proj1[:, GLAQ:GLAK + 1, 0:n], ALU.mult).then_inc(*made("decayed", l, v))
                if 4 <= k < 4 + LEVELS:
                    v = k - 4
                    dve.wait_ge(*when("masks_loaded", 0))
                    for h in range(4):
                        dve.wait_ge(*when("pairs", l, v, h))
                        p = bank("pairs", l, v, h)
                        dve.wait_ge(*when("gla_scores", l, v - 1, h))
                        dve.copy_predicated(gla_s[:, h, 0:ntile], masks[:, v:v + 1].broadcast_to([P, ntile, P]),
                                            p[:, 0:n].rearrange("p (t n) -> p t n", n=P)).then_inc(
                                                *made("gla_scores", l, v, h, frees=("pairs", l, v, h)))

            def beside_fox(l, k):
                tp = ("b2", l)
                if k < 16:
                    project(tp, PROJ2, 13 + k, N2, proj2, VTEMP2)
                if 6 <= k < 14:
                    rope(tp, k - 6, proj2[:, RQ + k - 6, :], cst2(C_COS2, N2), cst2(C_SIN2, N2), N2,
                         "projected", tp, 11 + k)
                if 16 <= k < 20:
                    h = k - 16
                    dve.wait_ge(*when("ret_pairs", l, h))
                    p = bank("ret_pairs", l, h)
                    if h >= 2:
                        dve.wait_ge(*when("ret_out", l, h - 2))
                    at = 0
                    for j, (t0, tn) in enumerate(TILES2):
                        n = N2 - t0
                        dve.tensor_tensor(ret_p[0:tn, h % 2, j, t0:N2], p[0:tn, at:at + n],
                                          cst2(C_DECAY + h * N2, n, tn), ALU.mult).then_inc(
                                              *made("ret_decayed", l, h, j, frees=("ret_pairs", l, h)))
                        at += n
                if k >= 20:
                    h = k - 20
                    dve.wait_ge(*when("ret_mean", l, h))
                    p = bank("ret_mean", l, h)
                    dve.tensor_tensor(proj2[:, RQ + h, :], proj2[:, RQ + h, :], p[:, 0:N2], ALU.subtract).then_inc(
                        *made("ret_centred", l, h, frees=("ret_mean", l, h)))

            dve.memset(eps_one[:, 0:1], EPS).then_inc(*made("eps_one", 0))
            dve.memset(eps_one[:, 1:2], 1.0).then_inc(*made("eps_one", 1))
            dve.wait_ge(*when("small_loaded", 0))
            for l in range(DEPTH):
                for name in ("naq", "gqaq"):
                    dve.tensor_scalar(scalar1(l, name), scalar1(l, name), HD ** -0.5, None, ALU.mult).then_inc(
                        *made("gain_scaled", l, name))
            dve.wait_ge(*when("gain_scaled", DEPTH - 1, "gqaq"))
            for d in range(KC):
                sum_squares(("start",), N1, d)
            for g in range(4):
                dve.wait_ge(*when("first_mod", 4 * g + 3))
                dve.tensor_copy(first_rows[:, g * 512:(g + 1) * 512], bank("first_rows", g)[0:2, :]).then_inc(
                    *made("first_rows_sb", g, frees=("first_rows", g)))
                if g == 0:
                    split_ahead(0)
            dve.wait_ge(*when("first_turned"))
            dve.tensor_copy(mod_raw[:, 0, :, 0:FIRST_MOD],
                            bank("first_turned")[:, 0:2 * FIRST_MOD].rearrange("p (j s) -> p s j", s=2)).then_inc(
                                *made("first_mod_raw", frees=("first_turned",)))
            for m in range(2):
                mod_finish(0, m, 2)
            norm1(("start",), ("ffn1", 0), 0, 0, N1)
            for l in range(DEPTH):
                t1, tm, to, t2 = ("ffn1", l), ("mix1", l), ("out1", l), ("ffn2", l)
                n = N1 if l == 0 else NX
                streams = BOTH if l == 0 else ONLY_X
                for h in ffn(t1, N1, 2, 0 if l == 0 else None):
                    residual(t1, l, 2, BOTH, N1, META, N1, h, h == 1, lambda d: (d + 1) * 11 // 8 - d * 11 // 8)
                norm1(t1, tm, l, 3, N1)
                for i in range(12):
                    project(tm, PROJ1, i, width1(l, PROJ1[i]), proj1, VTEMP1)
                    if i >= 10:
                        qk_norm(l, i - 10)
                qk_norm(l, 2)
                qk_norm(l, 3)
                per = 1 + l
                attention(na_heads(l), lambda i: [beside_na(l, k) for k in range(per * i, per * (i + 1))])
                attention(gqa_heads(l), lambda i: [beside_gqa(l, k) for k in range(per * i, per * (i + 1))])
                for s in range(2 - l):
                    for h in range(4):
                        po = (h % 2) * HD
                        dve.wait_ge(*when("gla_out", l, s, h))
                        p = bank("gla_out", l, s, h)
                        dve.tensor_copy(proj1[po:po + HD, GLAQ + h // 2, s * NX:(s + 1) * NX],
                                        p[po:po + HD, 0:NX]).then_inc(
                                            *made("gla_out_sb", l, s, h, frees=("gla_out", l, s, h)))
                for c in (0, 2):
                    low_part(to, x_parts(N1), c, n, proj1[:, MIX1[c], 0:n])
                for c in range(2):
                    x = proj1[:, GLAQ + c, 0:n]
                    head_norm(("gla", l), c, x, scalar1(l, "gla"), n, "gla_out_sb", l, 1 - l, 2 * c + 1)
                    dve.wait_ge(*when("head_normed", ("gla", l), c))
                    dve.tensor_tensor(x, x, proj1[:, GLAR + c, 0:n], ALU.mult).then_inc(*made("mix_gla", l, c))
                for c in (6, 4):
                    low_part(to, x_parts(N1), c, n, proj1[:, MIX1[c], 0:n])
                residual(to, l, 5, streams, n, META, n, 0, True, lambda d: 1)
                norm1(to, t2, l, 6, n)
                for h in ffn(t2, n, 2 - l, 1 if l == 0 else None):
                    nf = FC // (2 - l)
                    residual(t2, l, 8, streams, n, META if l == 0 else 0, n if l == 0 else N2, h, h == 1 - l,
                             lambda d: (d + 1) * nf // 8 - d * nf // 8)
                if l == 0:
                    norm1(t2, ("ffn1", 1), 1, 0, N1)
                else:
                    norm2(t2, ("b2", 0), 0, "attn")
            for l in range(DEPTH):
                tp, to, tf = ("b2", l), ("out2", l), ("ffn", l)
                y, e = negc[0:8, 0, :], negc[0:8, 1, :]
                for i in range(13):
                    project(tp, PROJ2, i, N2, proj2, VTEMP2)
                    if i == 5:
                        dve.wait_ge(*when("projected", tp, 4))
                        dve.tensor_scalar(y, y, scalar2(l, "bfg", 0, 8), None, ALU.add).then_inc(*made("flog_y", l))
                        dve.wait_ge(*when("flog_y", l))
                        dve.scalar_tensor_tensor(e, y, -1.0, y, ALU.mult, ALU.min).then_inc(*made("flog_neg_abs", l))
                    if i == 7:
                        dve.wait_ge(*when("flog_ln", l))
                        dve.scalar_tensor_tensor(e, y, 0.0, e, ALU.min, ALU.subtract).then_inc(*made("flog_log", l))
                        dve.wait_ge(*when("flog_log", l))
                        dve.tensor_tensor_scan(negc[0:8, 2, :], eps_one[0:8, 1:2].broadcast_to([8, N2]), e, 0.0,
                                               ALU.mult, ALU.subtract).then_inc(*made("negc", l))
                attention(fox_heads(l), lambda i: beside_fox(l, i))
                for h in range(4):
                    dve.wait_ge(*when("rstd", ("ret", l, h)))
                    x = proj2[:, RQ + h, :]
                    dve.scalar_tensor_tensor(x, x, scalar2(l, "gn", h), rstd[:, h % 2, 0:N2], ALU.mult,
                                             ALU.mult).then_inc(*made("ret_normed", l, h))
                    dve.wait_ge(*when("ret_normed", l, h))
                    dve.tensor_tensor(x, x, proj2[:, RG + h, :], ALU.mult).then_inc(*made("mix_ret", l, h))
                for c in range(0, KC, 2):
                    low_part(to, x_parts(N2), c, N2, proj2[:, MIX2[c], :])
                residual(to, l, None, None, N2, 0, N2, 0, True, lambda d: 1)
                norm2(to, tf, l, "ffn")
                for h in ffn(tf, N2, 1):
                    residual(tf, l, None, None, N2, 0, N2, 0, True, lambda d: (d + 1) * FC // 8 - d * FC // 8)
                if l + 1 < DEPTH:
                    norm2(tf, ("b2", l + 1), l + 1, "attn")
                else:
                    dve.wait_ge(*when("rstd", tf))
                    for c in range(KC):
                        dve.scalar_tensor_tensor(xf[:, c * NX:(c + 1) * NX], resid[:, c, META:META + NX],
                                                 small[:, S_FINAL + c:S_FINAL + c + 1], rstd[:, 0, META:META + NX],
                                                 ALU.mult, ALU.mult).then_inc(*made("final_norm", c))
    return ev


def blocks(w):
    k, m = w.shape
    mb = -(-m // P)
    if m % P:
        w = np.concatenate([w, np.zeros((k, mb * P - m), w.dtype)], 1)
    return w.reshape(k // P, P, mb, P).transpose(2, 1, 0, 3).reshape(mb, P, -1)


def ffn_units(w1, w3, w2, halves):
    up = np.stack([blocks(w1), blocks(w3)], 1)
    down = w2.reshape(halves, FC // halves, P, KC, P).transpose(0, 3, 1, 2, 4).reshape(FC, 8, P, P)
    down = down.transpose(0, 2, 1, 3).reshape(halves, FC // halves, P, UNIT)
    out = []
    for h in range(halves):
        n = FC // halves
        out += [up[h * n:(h + 1) * n].reshape(2 * n, P, UNIT), down[h]]
    return out


def swap_heads(w, at, axis):
    idx = np.arange(w.shape[axis])
    idx[at:at + 4 * HD] = at + np.concatenate([np.arange(HD) + HD * h for h in (0, 2, 1, 3)])
    return np.take(w, idx, axis)


def columns(v):
    return v.reshape(-1, P).T


def kernel(**inputs):
    import concourse.bacc as bacc
    from concourse.bass_utils import run_bass_kernel_spmd

    a = {k: np.asarray(v) for k, v in inputs.items()}
    units = []
    off = np.concatenate([[0], np.cumsum([256, 256, 256, 256, 128, 128, 256, 256, 32, 256, 128, 128])])
    names = ("four", "naq", "nak", "nav", "glaq", "glak", "glav", "glar", "gate", "gqaq", "gqak", "gqav")
    order = ("nav", "gqav", "glav", "naq", "nak", "gqaq", "gqak", "gate", "glak", "glaq", "glar", "four")
    for l in range(DEPTH):
        units += ffn_units(a["ffn1_w1"][l], a["ffn1_w3"][l], a["ffn1_w2"][l], 2)
        w = swap_heads(a["w_in"][l], off[names.index("gqaq")], 1)
        units += [blocks(w[:, off[i]:off[i + 1]]) for i in map(names.index, order)]
        units.append(blocks(swap_heads(a["w_out"][l], 768, 0)))
        units += ffn_units(a["ffn2_w1"][l], a["ffn2_w3"][l], a["ffn2_w2"][l], 2 - l)
    for l in range(DEPTH):
        w = a["w_in_2"][l]
        for lo, hi in ((1024, 1536), (1536, 1544), (0, 1024), (1544 + 1024, 1544 + 1536), (1544, 1544 + 1024),
                       (1544 + 1536, 1544 + 2048)):
            units.append(blocks(w[:, lo:hi]))
        units.append(blocks(a["w_out_2"][l]))
        units += ffn_units(a["w_gate_2"][l], a["w_up_2"][l], a["w_down_2"][l], 1)

    two = lambda v: np.concatenate([v, v])[:, None]
    small = []
    for l in range(DEPTH):
        small += [two(a[n][l]) for n in ("na_q_norm", "na_k_norm", "gqa_q_norm", "gqa_k_norm", "gla_norm")]
        small += [a["gla_b_gate_f"][l][:, None], a["gla_b_gate_b"][l][:, None], columns(a["b_mod"][l])]
    for l in range(DEPTH):
        fg = np.zeros((P, 1), np.float32)
        fg[:8, 0] = a["b_fgate_2"][l]
        small += [columns(a["attn_norm_2"][l]), columns(a["ffn_norm_2"][l]), columns(a["ret_gn_2"][l]), fg]
    small.append(columns(a["final_norm_2"]))

    wgate = np.zeros((32, DEPTH, 2 * P), np.float32)
    for l in range(DEPTH):
        wgate[0:16, l, 0:P] = a["gla_w_gate_f"][l]
        wgate[16:32, l, P:2 * P] = a["gla_w_gate_b"][l]

    cq = np.arange(64)
    start = np.clip(cq - 8, 0, 48)
    ck = np.arange(64)
    inside = (ck[None] >= start[:, None]) & (ck[None] < start[:, None] + 16)
    col = np.clip(ck[None] - cq[:, None] + 15, 0, 30)
    na_bias = np.full((DEPTH, 2, 64, 4, 6, 64), NEG, np.float32)
    for half in range(2):
        for j in range(6):
            rows = a["na_rpb"][:, :, j - 2 - half + 7]
            got = rows[:, :, col]
            na_bias[:, half, :, :, j] = np.where(inside[None, None], got, np.float32(NEG)).transpose(0, 2, 1, 3)
    na_bias = na_bias.reshape(DEPTH, P, 4 * 6 * 64)

    kept, dft, second = constants()
    tr = lambda v: v.T.reshape(KC, P, -1).transpose(1, 0, 2)
    arrays = {
        "stream": np.concatenate(units, 0),
        "w_mod": np.ascontiguousarray(a["w_mod"].transpose(0, 2, 1)).reshape(DEPTH, NMOD * KC, P, D),
        "w_mod_first": a["w_mod"][0, :, 0:FIRST_MOD * P].reshape(4, 2, P, 4, 512).transpose(3, 0, 2, 1, 4).reshape(
            FIRST_MOD, P, D),
        "c_cols": np.stack([a["c"][0].reshape(KC, P).T, a["c_ctx"].reshape(KC, P).T], 2).reshape(P, 2 * KC),
        "x": tr(a["x"][0]), "ctx": tr(a["ctx"][0]), "meta": tr(a["meta_tokens_2"]),
        "c": a["c"].reshape(1, D), "c_ctx": a["c_ctx"].reshape(1, D),
        "small": np.concatenate(small, 1), "consts": kept, "dft": dft, "consts2": second, "masks": level_masks(),
        "wgate": wgate, "na_bias": na_bias,
    }
    arrays = {k: np.ascontiguousarray(v) for k, v in arrays.items()}

    def program(old):
        nc = bacc.Bacc("TRN2", target_bir_lowering=False, num_devices=1)
        A = {k: nc.dram_tensor(f"{k}_dram", v.shape, mybir.dt.from_np(v.dtype), kind="ExternalInput").ap()
             for k, v in arrays.items()}
        A["out"] = nc.dram_tensor("out_dram", (P, KC * NX), F32, kind="ExternalOutput").ap()
        return nc, build(nc, A, old)

    _, counted = program(None)
    nc, _ = program((counted.table, counted.banks))
    r = run_bass_kernel_spmd(nc, [{f"{k}_dram": v for k, v in arrays.items()}], core_ids=[0])
    out = r.results[0]["out_dram"].reshape(P, KC, NX)
    return np.ascontiguousarray(out.transpose(2, 1, 0)).reshape(1, NX, D)
```

```python
import math
from contextlib import ExitStack

import numpy as np
import concourse.bass as bass
import concourse.mybir as mybir

F32 = mybir.dt.float32
F32R = mybir.dt.float32r
I32 = mybir.dt.int32
ALU = mybir.AluOpType
ACT = mybir.ActivationFunctionType
AX = mybir.AxisListType

P = 128
D = 1024
KC = D // P
SEQ = 256
NX, NZ = 256, 256
N1 = NX + NZ
META = 16
N2 = META + SEQ
DEPTH = 2
FF = 2816
FC = FF // P
NMOD = 9
EPS = 1e-6
HD = 64
RING = 3
MOD_RING = 3
UNIT = 8 * P
NEG = -1e30
LN_EXP = "natural_log_exp_and_others"

FIRST_MOD = 2 * KC
FIRST_SLOTS = 9

FOUR, NAQ, NAK, GLAQ, GLAK, GLAR, GATE, GQAQ, GQAK = 0, 2, 4, 6, 7, 8, 10, 11, 13
NSLOT1 = 14
NAV, GLAV, GQAV = 0, 256, 512
NV1 = 640
PROJ1 = [("V", NAV, P, True), ("V", NAV + P, P, True), ("V", GQAV, P, True), ("V", GLAV, P, True),
         ("V", GLAV + P, P, True),
         ("T", NAQ, P, False), ("T", NAQ + 1, P, False), ("T", NAK, P, True), ("T", NAK + 1, P, True),
         ("T", GQAQ, P, False), ("T", GQAQ + 1, P, False), ("T", GQAK, P, True),
         ("T", GATE, 32, True), ("T", GLAK, P, True), ("T", GLAQ, P, False),
         ("T", GLAR, P, False), ("T", GLAR + 1, P, False), ("T", FOUR, P, False), ("T", FOUR + 1, P, False)]
VTEMP1 = {0: GLAR, 1: GLAR + 1, 2: FOUR, 3: FOUR + 1, 4: GATE}
MIX1 = [FOUR, FOUR + 1, NAQ, NAQ + 1, GLAQ, GLAK, GQAQ, GQAQ + 1]
FQ, FK, RQ, RK, RG = 0, 4, 8, 12, 16
NSLOT2 = 24
FLOG = -1
PROJ2 = ([("V", P * i, P) for i in range(4)] + [("T", FLOG, 8)]
         + [("T", FQ + i, P) for i in range(4)] + [("T", FK + i, P) for i in range(4)]
         + [("T", RG + i, P) for i in range(4)] + [("T", RQ + i, P) for i in range(4)]
         + [("V", 512 + P * i, P) for i in range(4)] + [("T", RK + i, P) for i in range(4)])
BESIDE2 = 17
VTEMP2 = {i: RG + i for i in range(4)} | {21 + i: 20 + i for i in range(4)}
MIX2 = [FQ, FQ + 1, FQ + 2, FQ + 3, RQ, RQ + 1, RQ + 2, RQ + 3]
SLOT1 = {item[1]: i for i, item in enumerate(PROJ1) if item[0] == "T"}
SLOT2 = {item[1]: i for i, item in enumerate(PROJ2) if item[0] == "T"}
NV2 = 1024
TILES2 = [(0, 128), (128, 128), (256, 16)]

UNITS = DEPTH * (6 * FC + len(PROJ1) + KC) + DEPTH * (len(PROJ2) + KC + 3 * FC)

S_L1 = {"naq": 0, "nak": 1, "gqaq": 2, "gqak": 3, "gla": 4, "bf": 5, "bb": 6, "bmod": 7}
SW1 = 7 + NMOD * KC
S_L2 = {"attn": 0, "ffn": KC, "gn": 2 * KC, "bfg": 2 * KC + 4}
SW2 = 2 * KC + 5
S_FINAL = DEPTH * (SW1 + SW2)
SMALL = S_FINAL + KC

C_ONESD, C_ONES64, C_IDENT, C_PERM64 = (P * i for i in range(4))
C_COS1 = 4 * P
C_SIN1 = C_COS1 + SEQ
CONSTS = C_SIN1 + SEQ
C_DFTD = 0
C_DFTL = C_DFTD + 2 * P
DFT = C_DFTL + 2 * 2 * SEQ
C_ONES128, C_PERM128 = 0, P
C_COS2 = 2 * P
C_SIN2 = C_COS2 + N2
C_CAUSAL = C_SIN2 + N2
C_DECAY = C_CAUSAL + 3 * P
CONSTS2 = C_DECAY + 4 * N2
LEVELS = 7


def constants():
    c = np.zeros((P, CONSTS), np.float64)
    f = np.zeros((P, DFT), np.float64)
    d = np.zeros((P, CONSTS2), np.float64)
    c[:, C_ONESD:C_ONESD + P] = 1.0 / D
    half = np.arange(P) // HD
    c[:, C_ONES64:C_ONES64 + P] = (half[:, None] == half[None, :]) / HD
    d[:, C_ONES128:C_ONES128 + P] = 1.0 / P
    c[:, C_IDENT:C_IDENT + P] = np.eye(P)
    for t, at, n in ((c, C_PERM64, HD), (d, C_PERM128, P)):
        for i in range(P):
            j = i + n // 2 if i % n < n // 2 else i - n // 2
            t[j, at + i] = -1.0 if i % n < n // 2 else 1.0
    jd = np.arange(HD)
    ang = 2 * np.pi * (np.outer(jd, jd) % HD) / HD
    for g in range(2):
        s = slice(g * HD, (g + 1) * HD)
        f[s, C_DFTD + g * HD:C_DFTD + (g + 1) * HD] = np.cos(ang)
        f[s, C_DFTD + P + g * HD:C_DFTD + P + (g + 1) * HD] = np.sin(ang)
    jl = np.arange(SEQ)
    ang = 2 * np.pi * (np.outer(jl, jl) % SEQ) / SEQ
    norm = 1.0 / math.sqrt(SEQ * HD)
    for t in range(2):
        rows = ang[t * P:(t + 1) * P]
        at = C_DFTL + t * 2 * SEQ
        f[:, at:at + SEQ] = np.cos(rows) * norm
        f[:, at + SEQ:at + 2 * SEQ] = -np.sin(rows) * norm
    nf = HD // 4
    inv = 10000.0 ** (-np.arange(nf, dtype=np.float64) / nf)
    tok = np.arange(SEQ)
    ang = np.concatenate([(tok // 64)[None] * inv[:, None], (tok % 64)[None] * inv[:, None]], 0)
    c[:, C_COS1:C_COS1 + SEQ] = np.tile(np.cos(ang), (4, 1))
    c[:, C_SIN1:C_SIN1 + SEQ] = np.tile(np.sin(ang), (4, 1))
    inv = 10000.0 ** (-np.arange(0, P, 2, dtype=np.float64) / P)
    ang = inv[:, None] * np.arange(N2)[None]
    d[:, C_COS2:C_COS2 + N2] = np.tile(np.cos(ang), (2, 1))
    d[:, C_SIN2:C_SIN2 + N2] = np.tile(np.sin(ang), (2, 1))
    q = np.arange(P)
    d[:, C_CAUSAL + 2 * P:C_CAUSAL + 3 * P] = np.where(q[None, :] <= q[:, None], 0.0, NEG)
    for h in range(4):
        g = math.log(1.0 - 2.0 ** (-5 - h))
        diff = np.arange(N2)[None, :] - q[:, None]
        d[:, C_DECAY + h * N2:C_DECAY + (h + 1) * N2] = np.where(
            diff >= 0, np.exp(np.maximum(diff, 0) * g), 0.0) * P ** -0.5
    return c.astype(np.float32), f.astype(np.float32), d.astype(np.float32)


def level_masks():
    i = np.arange(P)
    out = np.zeros((P, LEVELS, P), np.int32)
    for v in range(LEVELS):
        m = 1 << v
        same = (i[:, None] // (2 * m)) == (i[None, :] // (2 * m))
        out[:, v] = same & ((i[:, None] // m) != (i[None, :] // m))
    return out.reshape(P, LEVELS * P)


class Events:

    def __init__(self, table=None, banks=None):
        self.known = table or {}
        self.bank_known = banks or {}
        self.counting = table is None
        self.table, self.banks, self.count = {}, {}, {}
        self.sems = {}


class Events:

    def __init__(self, table=None, banks=None):
        self.known = table or {}
        self.bank_known = banks or {}
        self.counting = table is None
        self.table, self.banks, self.count = {}, {}, {}
        self.sems = {}


MOD_STEPS = FC + KC


def mod_chunks(l, part, i):
    step = FC // 2 + i if part is None else part * (FC // 2 + KC) + i
    first, n = (2 * KC, 7 * KC) if l == 0 else (0, NMOD * KC)
    return range(first + n * step // MOD_STEPS, first + n * (step + 1) // MOD_STEPS)


def build(nc, A, old=None):
    ev = Events(*(old or (None, None)))
    ctx = ExitStack()
    with ctx:
        top = [nc.sbuf_base + (-nc.sbuf_base) % 64]

        def sb(name, cols, dt=F32, over=None):
            if over is None:
                over = top[0] = -(-top[0] // 64) * 64
                top[0] += cols * mybir.dt.size(dt)
            place_of[name] = over
            return nc.alloc_sbuf_tensor_at(name, [P, cols], dt, offset=over)[:, :]

        place_of = {}

        def sem(name):
            return ctx.enter_context(nc.semaphore(name))

        def made(name, *key, by=1, frees=None, unit=None):
            if name not in ev.sems:
                ev.sems[name] = sem(name)
            ev.count[name] = ev.count.get(name, 0) + by
            ev.table[(name, *key)] = (name, ev.count[name])
            if frees is not None:
                ev.table[("free",) + frees] = (name, ev.count[name])
            if unit is not None:
                ev.table[("unit_used", unit)] = (name, ev.count[name])
            return ev.sems[name], by

        def when(name, *key):
            if ev.counting:
                return high_parts, 1
            family, value = ev.known[(name, *key)]
            if family not in ev.sems:
                ev.sems[family] = sem(family)
            return ev.sems[family], value

        def bank(*key):
            return psum[ev.bank_known.get(key, 0)]

        resid = sb("resid", KC * (META + N1)).rearrange("p (c n) -> p c n", c=KC)
        const = sb("const", CONSTS)
        small = sb("small", SMALL)
        eps_one = sb("eps_one", 2)
        ring = sb("ring", RING * UNIT).rearrange("p (s n) -> p s n", s=RING)
        high = sb("ring_high", RING * UNIT, F32R)
        low = sb("ring_low", RING * UNIT, F32R)
        high_f = high.bitcast(F32).rearrange("p (s n) -> p s n", s=RING)
        high = high.rearrange("p (s n) -> p s n", s=RING)
        low = low.rearrange("p (s n) -> p s n", s=RING)
        xr = sb("x_parts", 2 * KC * N1, F32R)
        xf = sb("x_place", 2 * KC * N1, F32, over=place_of["x_parts"])
        dft_ab = xf[:, 0:2048].rearrange("p (s t n) -> p s t n", s=2, t=2)
        cross = xf[:, 0:2048].rearrange("p (h t n) -> p h t n", h=4, t=4)
        gla_s = xf[:, 2048:4096].rearrange("p (h t n) -> p h t n", h=4, t=4)
        gates = xf[:, 4096:5120].rearrange("p (g n) -> p g n", g=2)
        decay = xf[:, 5120:7168].rearrange("p (b g n) -> p b g n", b=2, g=2)
        decay_x = xf[:, 5120:7168].rearrange("p (b g n) -> p b g n", b=4, g=2)
        khat = xf[:, 7168:7680].rearrange("p (t n) -> p t n", t=4)
        state = xf[:, 7680:8192].rearrange("p (g n) -> p g n", g=2)
        ret_p = xf[:, 0:2 * 3 * N2].rearrange("p (b k n) -> p b k n", b=2, k=3)
        HID = 2 * FC * N2
        top[0] = -(-top[0] // 64) * 64
        hid_r = sb("hidden_parts", HID, F32R, over=top[0])
        arena = sb("arena", 15008)
        proj1 = arena[:, 0:NSLOT1 * N1].rearrange("p (c n) -> p c n", c=NSLOT1)
        v1 = arena[:, NSLOT1 * N1:NSLOT1 * N1 + 4 * NV1].rearrange("p (t n) -> p t n", t=4)
        proj2 = arena[:, 0:NSLOT2 * N2].rearrange("p (c n) -> p c n", c=NSLOT2)
        v2 = arena[:, NSLOT2 * N2:NSLOT2 * N2 + 3 * NV2].rearrange("p (t n) -> p t n", t=3)
        probs_t = arena[:, 9728:11904].rearrange("p (b k n) -> p b k n", b=2, k=4)
        probs = arena[:, 11904:12928].rearrange("p (b n) -> p b n", b=2)
        biased = arena[:, 12928:13472].rearrange("p (b n) -> p b n", b=2)
        bias = arena[:, 13472:15008]
        negc = bias[:, 0:3 * N2].rearrange("p (g n) -> p g n", g=3)
        scaled = arena[:, 0:KC * N1].rearrange("p (c n) -> p c n", c=KC)
        first_mod = arena[:, KC * N1:KC * N1 + FIRST_SLOTS * UNIT].rearrange("p (s k n) -> p s k n", s=FIRST_SLOTS, k=2)
        first_rows = arena[0:2, 0:FIRST_MOD * P]
        mod_flat = sb("mod_ring", MOD_RING * D)
        mod_ring = mod_flat.rearrange("p (s n) -> p s n", s=MOD_RING)
        const2 = mod_flat[:, 0:CONSTS2]
        c_cols = sb("c_cols", 2 * KC).rearrange("p (c s) -> p c s", c=KC)
        csilu = sb("csilu", 2 * D).rearrange("p (s n) -> p s n", s=2)
        junk = sb("mod_products", 2 * D, mybir.dt.bfloat16).rearrange("p (s n) -> p s n", s=2)
        mod_raw = sb("mod_raw", DEPTH * 2 * NMOD * KC).rearrange("p (l s n) -> p l s n", l=DEPTH, s=2)
        mod = sb("mod", DEPTH * 2 * NMOD * KC).rearrange("p (l s n) -> p l s n", l=DEPTH, s=2)
        dft = sb("dft", DFT)
        masks = sb("masks", LEVELS * P, I32).rearrange("p (v n) -> p v n", v=LEVELS)
        wgate = sb("wgate", DEPTH * 2 * P).rearrange("p (l n) -> p l n", l=DEPTH)
        squares = sb("squares", 2 * N1).rearrange("p (b n) -> p b n", b=2)
        sumsq = sb("sumsq", N1)
        rstd = sb("rstd", 2 * N1).rearrange("p (b n) -> p b n", b=2)
        act_out = sb("act_out", 2 * N1).rearrange("p (b n) -> p b n", b=2)
        fresh = sb("fresh", 2 * N1).rearrange("p (b n) -> p b n", b=2)
        stat = sb("softmax_stats", 4 * 8).rearrange("p (b n) -> p b n", b=4)
        assert top[0] <= nc.sbuf_usable_end, (top[0], nc.sbuf_usable_end)
        psum = [ctx.enter_context(nc.psum_tensor(f"bank{i}", [P, 512], F32))[:, :] for i in range(8)]

        def x_parts(n):
            v = xr[:, 0:2 * KC * n].rearrange("p (k c n) -> p k c n", k=2, c=KC)
            return v[:, 0], v[:, 1]

        def hidden_parts(n, parts):
            nf = FC // parts
            v = hid_r[:, 0:2 * nf * n].rearrange("p (k c n) -> p k c n", k=2, c=nf)
            return v[:, 0], v[:, 1]

        def cst(at, n=P, rows=P):
            return const[0:rows, at:at + n]

        def cst2(at, n=P, rows=P):
            return const2[0:rows, at:at + n]

        def scalar1(l, name, j=0):
            at = l * SW1 + S_L1[name] + j
            return small[:, at:at + 1]

        def scalar2(l, name, j=0, rows=P):
            at = DEPTH * SW1 + l * SW2 + S_L2[name] + j
            return small[0:rows, at:at + 1]

        unit_loaded = [sem(f"unit_loaded{i}") for i in range(RING)]
        high_parts = sem("high_parts")
        low_parts = sem("low_parts")

        BOTH = [(0, 0, NX), (1, NX, N1)]
        ONLY_X = [(0, 0, NX)]

        def after(tag):
            both = [(0, NX, 0, NX), (NX, N1, NX, N1)]
            second = [(0, N2, 0, N2)]
            name, l = tag[0], tag[-1]
            if name in ("out2", "ffn") and l == 1:
                return [], [(0, NX, 0, NX)], META, ("ffn", 1) if name == "out2" else None, (l, "ffn")
            if name == "start":
                return [], both, META, ("ffn1", 0), (0, 0)
            if name == "ffn1":
                return [6, 7], both, META, ("mix1", l), (l, 3)
            if name == "out1" and l == 0:
                return [5, 6, 7], both, META, ("ffn2", l), (l, 6)
            if name == "out1":
                return [], [(0, NX, 0, NX)], META, ("ffn2", l), (l, 6)
            if name == "ffn2" and l == 0:
                return [6, 7], both, META, ("ffn1", 1), (1, 0)
            if name == "ffn2":
                return [], [(0, NX, 0, N2)], 0, ("b2", 0), (0, "attn")
            if name == "out2":
                return [], second, 0, ("ffn", l), (l, "ffn")
            return [], second, 0, ("b2", 1) if l == 0 else None, (l + 1, "attn")

        def first_late(tag):
            return KC - len(after(tag)[0])

        def splits(d, nb):
            before = ((d + 1) * nb - 1) // KC
            return before - d * nb // KC, (d + 1) * nb // KC - before

        def decays(l, v):
            return decay[:, v % 2] if l == 0 else decay_x[:, v % 4]

        def rope_steps(k):
            return [k - 2] if 2 <= k < 6 else [k - 6] if 10 <= k < 14 else []

        def gla_outs(l, k):
            out = [(s, h) for s in range(2 - l) for h in range(4)]
            return out[(k - 5 - LEVELS) * (2 - l):(k - 4 - LEVELS) * (2 - l)]

        def groups_of(tag):
            return range(len(after(tag)[1]))

        def sum_key(tag, d, g):
            return (tag, d, g if d in after(tag)[0] else "all")

        def norm_cols(tag, g):
            groups = after(tag)[1]
            return (groups[0][2], groups[-1][3]) if g == "all" else groups[g][2:]

        def parts_for(to):
            return x_parts(N2 if to[0] in ("b2", "ffn") else N1)

        def stream_of(tag, g):
            return g

        def width1(l, item):
            return N1 if l == 0 or item[3] else NX

        def na_heads(l):
            out = []
            for h in range(4):
                c, po = h // 2, (h % 2) * HD
                out.append(dict(id=("nax", l, h), po=po, q=proj1[po:po + HD, NAQ + c, 0:NX],
                                k=proj1[po:po + HD, NAK + c, 0:N1], tiles=[(0, P, N1), (P, P, N1)],
                                v=[(P, v1[:, t, NAV + h * HD:NAV + (h + 1) * HD]) for t in range(4)],
                                kind="na", h=h, out=proj1[po:po + HD, NAQ + c, 0:NX], n=NX))
                if l == 0:
                    out.append(dict(id=("naz", l, h), po=po, q=proj1[po:po + HD, NAQ + c, NX:N1],
                                    k=proj1[po:po + HD, NAK + c, NX:N1], tiles=[(0, P, NZ), (P, P, NZ)],
                                    v=[(P, v1[:, t, NAV + h * HD:NAV + (h + 1) * HD]) for t in (2, 3)],
                                    kind="plain", h=h, out=proj1[po:po + HD, NAQ + c, NX:N1], n=NZ))
            return out

        def gqa_heads(l):
            out = []
            for h in range(4):
                c, po, kv = h // 2, (h % 2) * HD, h % 2
                out.append(dict(id=("gqax", l, h), po=po, q=proj1[po:po + HD, GQAQ + c, 0:NX],
                                k=proj1[po:po + HD, GQAK, 0:N1], tiles=[(0, P, N1), (P, P, N1)],
                                v=[(P, v1[:, t, GQAV + kv * HD:GQAV + (kv + 1) * HD]) for t in range(4)],
                                kind="plain", h=h, out=proj1[po:po + HD, GQAQ + c, 0:NX], n=NX))
                if l == 0:
                    out.append(dict(id=("gqaz", l, h), po=po, q=proj1[po:po + HD, GQAQ + c, NX:N1],
                                    k=proj1[po:po + HD, GQAK, NX:N1], tiles=[(0, P, NZ), (P, P, NZ)],
                                    v=[(P, v1[:, t, GQAV + kv * HD:GQAV + (kv + 1) * HD]) for t in (2, 3)],
                                    kind="plain", h=h, out=proj1[po:po + HD, GQAQ + c, NX:N1], n=NZ))
            return out

        def fox_heads(l):
            out = []
            for h in range(8):
                c, po = h // 2, (h % 2) * HD
                out.append(dict(id=("fox", l, h), po=po, q=proj2[po:po + HD, FQ + c, :],
                                k=proj2[po:po + HD, FK + c, :],
                                tiles=[(0, P, P), (P, P, 2 * P), (2 * P, META, N2)],
                                v=[(n, v2[0:n, t, h * HD:(h + 1) * HD]) for t, (_, n) in enumerate(TILES2)],
                                kind="fox", h=h, out=proj2[po:po + HD, FQ + c, :], n=N2))
            return out

        def norm_items(l):
            nq = N1 if l == 0 else NX
            return ([(NAQ, "naq", nq), (NAQ + 1, "naq", nq), (NAK, "nak", N1), (NAK + 1, "nak", N1),
                     (GQAQ, "gqaq", nq), (GQAQ + 1, "gqaq", nq), (GQAK, "gqak", N1)])

        rope_items = [GQAQ, GQAQ + 1, GQAK]

        def on_act(tag, i):
            plan = PROJ1 if tag[0] == "mix1" else PROJ2
            kind, dst = plan[i][:2]
            if kind == "T" and (dst in (GLAQ, GLAR, GLAR + 1) if tag[0] == "mix1" else dst >= RG):
                return True
            return i % 2 == 0

        every = [hd for l in range(DEPTH) for hd in na_heads(l) + gqa_heads(l)] + \
                [hd for l in range(DEPTH) for hd in fox_heads(l)]
        tile_keys = [(*hd["id"], j) for hd in every for j in range(len(hd["tiles"]))]
        tile_no = {key: i for i, key in enumerate(tile_keys)}
        head_no = {hd["id"]: i for i, hd in enumerate(every)}
        block = ctx.enter_context(nc.Block())

        @block.sync
        def _(sp):
            sp.dma_start(c_cols, A["c_cols"].rearrange("p (c s) -> p c s", c=KC)).then_inc(
                *made("c_cols_loaded", 0, by=16))
            sp.dma_start(resid[:, :, META:META + NX], A["x"]).then_inc(*made("x_loaded", 0, by=16))
            sp.dma_start(resid[:, :, META + NX:META + N1], A["ctx"]).then_inc(*made("ctx_loaded", 0, by=16))
            sp.dma_start(const, A["consts"]).then_inc(*made("consts_loaded", 0, by=16))
            sp.dma_start(small, A["small"]).then_inc(*made("small_loaded", 0, by=16))
            for s in range(RING):
                sp.dma_start(ring[:, s], A["stream"][s]).then_inc(unit_loaded[s], 16)
            sp.dma_start(resid[:, :, 0:META], A["meta"]).then_inc(*made("meta_loaded", 0, by=16))
            turns = UNITS // RING
            with sp.Fori(1, turns) as turn:
                for s in range(RING):
                    sp.wait_ge(low_parts, turn * RING + (s + 1 - RING))
                    sp.dma_start(ring[:, s], A["stream"][turn * RING + s]).then_inc(unit_loaded[s], 16)
            for u in range(turns * RING, UNITS):
                sp.wait_ge(low_parts, u - RING + 1)
                sp.dma_start(ring[:, u % RING], A["stream"][u]).then_inc(unit_loaded[u % RING], 16)
            for g in range(2):
                sp.wait_ge(*when("final_norm", (g + 1) * KC // 2 - 1))
                cols = slice(g * KC * NX // 2, (g + 1) * KC * NX // 2)
                sp.dma_start(A["out"][:, cols], xf[:, cols]).then_inc(*made("out_stored", g, by=16))
            sp.wait_ge(*when("out_stored", 1))

        @block.gpsimd
        def _(pool):
            loaded = [FIRST_MOD]

            def mod_loads(upto):
                for n in range(loaded[0], min(upto, DEPTH * NMOD * KC)):
                    if n >= FIRST_MOD + MOD_RING:
                        pool.wait_ge(*when("mod_dot", n - MOD_RING))
                    pool.dma_start(mod_ring[:, n % MOD_RING], A["w_mod"][n // (NMOD * KC), n % (NMOD * KC)]).then_inc(
                        *made(f"mod_loaded{n % MOD_RING}", n, by=16))
                loaded[0] = max(loaded[0], upto)

            def low_part(tag, out, c, n, whole):
                pool.wait_ge(*when("x_high", tag, c))
                hi, lo = out
                pool.tensor_tensor(lo[:, c, 0:n], whole, hi[:, c, 0:n].bitcast(F32), ALU.subtract).then_inc(
                    *made("x_low_pool", tag, c))
                ev.table[("x_low", tag, c)] = ev.table[("x_low_pool", tag, c)]

            def norm(tag):
                _, _, _, to, how = after(tag)
                hi, lo = parts_for(to)
                for g in groups_of(tag):
                    a, b = norm_cols(tag, g)
                    for c in range(1, KC, 2):
                        pool.wait_ge(*when("x_high" if isinstance(how[1], str) else "shifted", to, c, g))
                        pool.tensor_tensor(lo[:, c, a:b], scaled[:, c, a:b], hi[:, c, a:b].bitcast(F32),
                                           ALU.subtract).then_inc(*made("x_low_pool", to, c, g))
                        ev.table[("x_low", to, c, g)] = ev.table[("x_low_pool", to, c, g)]

            def hidden_low(tag, n, parts, l=None):
                hi, lo = hidden_parts(n, parts)
                nf = FC // parts
                for h in range(parts):
                    for f in range(nf):
                        pool.wait_ge(*when("hidden_high", tag, h, f))
                        pool.tensor_tensor(lo[:, f], fresh[:, f % 2, 0:n], hi[:, f].bitcast(F32),
                                           ALU.subtract).then_inc(*made("hidden_low", tag, h, f))
                        if l is not None:
                            mod_loads(l * NMOD * KC + mod_chunks(l, h, f).stop + MOD_RING)
                    if l is not None and h == 0:
                        for d in range(KC):
                            mod_loads(l * NMOD * KC + mod_chunks(l, None, d).stop + MOD_RING)

            def gla_exponents(l):
                n = N1 if l == 0 else NX
                b, c = gates[:, 0, 0:n], gates[:, 1, 0:n]
                pool.wait_ge(*when("gate_sums", l, 1, 1))
                for v in range(LEVELS + 1):
                    m = 1 << v
                    if v >= 2 + 2 * l:
                        pool.wait_ge(*when("pairs", l, v - 2 - 2 * l, 3))
                    bv = b.rearrange("p (k t m) -> p k t m", t=2, m=m)
                    cv = c.rearrange("p (k t m) -> p k t m", t=2, m=m)
                    dq = decays(l, v)[:, 0].rearrange("p (k t m) -> p k t m", t=2, m=m)
                    dk = decays(l, v)[:, 1].rearrange("p (k t m) -> p k t m", t=2, m=m)
                    shape = [P, n // (2 * m), m]
                    b_mid = bv[:, :, 0, m - 1:m].broadcast_to(shape)
                    c_mid = cv[:, :, 1, 0:1].broadcast_to(shape)
                    pool.tensor_tensor(dq[:, :, 0, :], cv[:, :, 0, :], c_mid, ALU.subtract).then_inc(
                        *made("exponents", l, v, 0))
                    pool.tensor_tensor(dq[:, :, 1, :], bv[:, :, 1, :], b_mid, ALU.subtract).then_inc(
                        *made("exponents", l, v, 1))
                    pool.tensor_tensor(dk[:, :, 0, :], b_mid, bv[:, :, 0, :], ALU.subtract).then_inc(
                        *made("exponents", l, v, 2))
                    pool.tensor_tensor(dk[:, :, 1, :], c_mid, cv[:, :, 1, :], ALU.subtract).then_inc(
                        *made("exponents", l, v, 3))

            def mixed_low(tag, slots, src, n, nn, at=0):
                for c in range(1, KC, 2):
                    low_part(tag, x_parts(n), c, nn, src[:, slots[c], at:at + nn])

            for j in range(FIRST_MOD):
                if j >= FIRST_SLOTS:
                    pool.wait_ge(*when("first_mod", j - FIRST_SLOTS))
                pool.dma_start(first_mod[:, j % FIRST_SLOTS], A["w_mod_first"][j].rearrange("p (k n) -> p k n", k=2)).then_inc(
                    *made(f"first_mod_loaded{j % FIRST_SLOTS}", j, by=16))
            pool.dma_start(csilu[:, 0, :], A["c"].broadcast_to([P, D])).then_inc(*made("c_loaded", by=16))
            pool.dma_start(csilu[:, 1, :], A["c_ctx"].broadcast_to([P, D])).then_inc(*made("c_ctx_loaded", by=16))
            mod_loads(2 * KC + MOD_RING)
            pool.dma_start(masks, A["masks"].rearrange("p (v n) -> p v n", v=LEVELS)).then_inc(
                *made("masks_loaded", 0, by=16))
            pool.dma_start(wgate[0:32], A["wgate"]).then_inc(*made("wgate_loaded", 0, by=16))
            pool.dma_start(dft, A["dft"]).then_inc(*made("dft_loaded", 0, by=16))
            pool.dma_start(bias, A["na_bias"][0]).then_inc(*made("bias_loaded", 0, by=16))
            norm(("start",))
            for l in range(DEPTH):
                n = N1 if l == 0 else NX
                hidden_low(("ffn1", l), N1, 2, 0 if l == 0 else None)
                norm(("ffn1", l))
                gla_exponents(l)
                mixed_low(("out1", l), MIX1, proj1, N1, n)
                norm(("out1", l))
                if l == 0:
                    pool.wait_ge(*when("exps", "nax", 0, 3, 1))
                    pool.dma_start(bias, A["na_bias"][1]).then_inc(*made("bias_loaded", 1, by=16))
                hidden_low(("ffn2", l), n, 2 - l, 1 if l == 0 else None)
                if l == 0:
                    pool.wait_ge(*when("mod_dot", DEPTH * NMOD * KC - 1))
                    pool.dma_start(const2, A["consts2"]).then_inc(*made("consts2_loaded", 0, by=16))
                norm(("ffn2", l))
            for l in range(DEPTH):
                n = N2 if l == 0 else NX
                mixed_low(("out2", l), MIX2, proj2, N2, n, N2 - n)
                norm(("out2", l))
                hidden_low(("ffn", l), n, 1)
                if l + 1 < DEPTH:
                    norm(("ffn", l))

        @block.tensor
        def _(pe):
            taken = [0]
            bank_user = {}

            def take(*key):
                b = taken[0] % 8
                taken[0] += 1
                if b in bank_user:
                    pe.wait_ge(*when("free", *bank_user[b]))
                bank_user[b] = key
                ev.banks[key] = b
                return psum[b]

            unit = [0]

            def weights():
                u = unit[0]
                unit[0] += 1
                pe.wait_ge(low_parts, u + 1)
                return [w[:, u % RING].rearrange("p (b n) -> p b n", b=8) for w in (high, low)]

            def product(out, w, b, xh, xl, start, stop):
                pe.matmul(out, w[0][:, b], xh, start=start, stop=False)
                pe.matmul(out, w[0][:, b], xl, start=False, stop=False)
                return pe.matmul(out, w[1][:, b], xh, start=False, stop=stop)

            def mean_square(tag, g):
                a, b = norm_cols(tag, g)
                pe.wait_ge(*when("sumsq", *sum_key(tag, KC - 1, g)))
                pe.matmul(take("mean", tag, g)[:, 0:b - a], cst(C_ONESD), sumsq[:, a:b], start=True,
                          stop=True).then_inc(*made("mean", tag, g))

            def first_units(tag, keys, n, xh, xl, order, prev=None):
                ps = [take(*key) for key in keys]
                ws = [weights() for key in keys]
                groups = list(groups_of(prev)) if prev else [None]
                for g in groups:
                    a, b = norm_cols(prev, g) if prev else (0, n)
                    for c in order:
                        pe.wait_ge(*when("x_low", tag, c, *([] if g is None else [g])))
                        for i, key in enumerate(keys):
                            mm = product(ps[i][:, a:b], ws[i], c, xh[:, c, a:b], xl[:, c, a:b],
                                         c == order[0], c == order[-1])
                            if c == order[-1] and g == groups[-1]:
                                mm.then_inc(*made(*key, unit=unit[0] - len(keys) + i))
                        if g == 0 and c == 2 and after(prev)[0]:
                            mean_square(prev, 1)

            def late_products(tag, h, nb, w, hi, lo, order):
                late, groups, *_ = after(tag)
                if not late:
                    mean_square(tag, 0)
                    return
                held = {late[0] * nb // 8: (w, unit[0] - 1)} if late[0] * nb % 8 else {}
                count = 0
                for g, (a, b, _, _) in enumerate(groups):
                    for d in late:
                        p = take("down", tag, h, d, g)
                        for i in range(nb):
                            j = d * nb + i
                            if j // 8 not in held:
                                held[j // 8] = (weights(), unit[0] - 1)
                            w, u = held[j // 8]
                            f = order[i]
                            mm = product(p[:, 0:b - a], w, f if nb == 8 else j % 8, hi[:, f, a:b], lo[:, f, a:b],
                                         i == 0, i == nb - 1)
                            used = u if g == 1 and j % 8 == 7 else None
                            if i == nb - 1:
                                mm.then_inc(*made("down", tag, h, d, g, unit=used))
                            elif used is not None:
                                mm.then_inc(*made("unit_read", used, unit=used))
                            count += 1
                            if count == len(late) * nb + 5:
                                mean_square(tag, 0)
                assert len(held) <= RING

            def ffn(tag, nx, n, parts, prev):
                xh, xl = x_parts(nx)
                hh, hl = hidden_parts(n, parts)
                nf = FC // parts
                for h in range(parts):
                    for f in range(nf):
                        if h == 0 and f == 0:
                            first_units(tag, [("gate", tag, 0, 0), ("up", tag, 0, 0)], n, xh, xl, range(KC), prev)
                            continue
                        for what in ("gate", "up"):
                            p = take(what, tag, h, f)
                            w = weights()
                            for c in range(KC):
                                mm = product(p[:, 0:n], w, c, xh[:, c, 0:n], xl[:, c, 0:n],
                                             c == 0, c == KC - 1)
                            mm.then_inc(*made(what, tag, h, f, unit=unit[0] - 1))
                    j = 0
                    for d in range(first_late(tag) if h == parts - 1 else KC):
                        p = take("down", tag, h, d)
                        for f in range(nf):
                            if j % 8 == 0:
                                w = weights()
                            if d == 0:
                                pe.wait_ge(*when("hidden_low", tag, h, f))
                            mm = product(p[:, 0:n], w, j % 8, hh[:, f], hl[:, f], f == 0, f == nf - 1)
                            j += 1
                            if f < nf - 1 and j % 8 == 0:
                                mm.then_inc(*made("unit_read", unit[0] - 1, unit=unit[0] - 1))
                        mm.then_inc(*made("down", tag, h, d, unit=unit[0] - 1 if j % 8 == 0 else None))
                    if h == parts - 1:
                        late_products(tag, h, nf, w, hh, hl, range(nf))

            def project(tag, plan, i, nx, n, src, vtemp, vtiles, prev=None):
                xh, xl = x_parts(nx)
                if i == 0:
                    first_units(tag, [("proj", tag, 0), ("proj", tag, 1)], n, xh, xl, range(KC), prev)
                    return
                if i >= 2:
                    w = weights()
                    p = take("proj", tag, i)
                    for c in range(KC):
                        mm = product(p[:, 0:n], w, c, xh[:, c, 0:n], xl[:, c, 0:n], c == 0, c == KC - 1)
                    mm.then_inc(*made("proj", tag, i, unit=unit[0] - 1))
                if i and plan[i - 1][0] == "V":
                    pe.wait_ge(*when("projected", tag, i - 1))
                    p = take("v_turned", tag, i - 1)
                    for t, (t0, tn) in enumerate(vtiles):
                        mm = pe.transpose(p[0:tn, t * P:(t + 1) * P], src[:, vtemp[i - 1], t0:t0 + tn], cst(C_IDENT))
                    mm.then_inc(*made("v_turned", tag, i - 1))

            def project_out(tag, nx, n, order):
                xh, xl = x_parts(nx)
                first_units(tag, [("down", tag, 0, 0), ("down", tag, 0, 1)], n, xh, xl, order)
                for d in range(2, first_late(tag)):
                    w = weights()
                    p = take("down", tag, 0, d)
                    for c in range(KC):
                        mm = product(p[:, 0:n], w, c, xh[:, c, 0:n], xl[:, c, 0:n], c == 0, c == KC - 1)
                    mm.then_inc(*made("down", tag, 0, d, unit=unit[0] - 1))
                late_products(tag, 0, KC, None, xh, xl, order)

            def dft_features(l, s):
                s0 = s * NX
                for t in range(2):
                    p = take("dft_d", l, s, t)
                    for g in range(2):
                        pe.wait_ge(*when("projected", ("mix1", l), SLOT1[FOUR + g]))
                        mm = pe.matmul(p[:, g * 2 * P:(g + 1) * 2 * P],
                                       proj1[:, FOUR + g, s0 + t * P:s0 + (t + 1) * P],
                                       dft[:, C_DFTD:C_DFTD + 2 * P], start=True, stop=True)
                    mm.then_inc(*made("dft_d", l, s, t))

            def dft_tokens(l, s):
                p = take("dft_l", l, s)
                for t in range(2):
                    pe.wait_ge(*when("dft_ab", l, s, t))
                for g in range(2):
                    n = 0
                    for t in range(2):
                        for part in range(2):
                            at = C_DFTL + (2 * t + part) * SEQ
                            mm = pe.matmul(p[:, g * SEQ:(g + 1) * SEQ],
                                           dft_ab[:, s, t, (2 * g + part) * P:(2 * g + part + 1) * P],
                                           dft[:, at:at + SEQ], start=(n == 0), stop=(n == 3))
                            n += 1
                mm.then_inc(*made("dft_l", l, s))

            def head_mean(tag, i, n):
                pe.wait_ge(*when("head_squares", tag, i))
                pe.matmul(take("head_mean", tag, i)[:, 0:n], cst(C_ONES64),
                          squares[:, i % 2, 0:n], start=True, stop=True).then_inc(*made("head_mean", tag, i))

            def attention(heads, beside):
                tiles = [(hd, j) for hd in heads for j in range(len(hd["tiles"]))]

                def scores(i):
                    hd, j = tiles[i]
                    q0, nq, nk = hd["tiles"][j]
                    p = take("scores", *hd["id"], j)
                    fox = hd["kind"] == "fox"
                    mm = pe.matmul(p[0:nq, 0:nk], hd["q"][:, q0:q0 + nq], hd["k"][:, 0:nk],
                                   start=True, stop=not fox)
                    if fox:
                        one_hot = const[0:8, C_IDENT + hd["h"]:C_IDENT + hd["h"] + 1].broadcast_to([8, nq])
                        mm = pe.matmul(p[0:nq, 0:nk], one_hot, negc[0:8, 2, 0:nk], start=False, stop=True)
                    mm.then_inc(*made("scores", *hd["id"], j))

                def turn(i):
                    hd, j = tiles[i]
                    _, nq, nk = hd["tiles"][j]
                    b = tile_no[(*hd["id"], j)] % 2
                    pe.wait_ge(*when("probs", *hd["id"], j))
                    p = take("turned", *hd["id"], j)
                    for kt in range((nk + P - 1) // P):
                        rows = min(P, nk - kt * P)
                        mm = pe.transpose(p[0:rows, kt * P:kt * P + nq],
                                          probs[0:nq, b, kt * P:kt * P + rows], cst(C_IDENT, nq, nq))
                    mm.then_inc(*made("turned", *hd["id"], j))

                def values(hd):
                    for j in range(len(hd["tiles"])):
                        pe.wait_ge(*when("probs_t", *hd["id"], j))
                    p = take("attended", *hd["id"])
                    po, n, b = hd["po"], hd["n"], head_no[hd["id"]] % 2
                    for kt, (rows, v) in enumerate(hd["v"]):
                        q0 = kt * P if hd["kind"] == "fox" else 0
                        mm = pe.matmul(p[po:po + HD, q0:n], v, probs_t[0:rows, b, kt, q0:n],
                                       start=(kt == 0), stop=(kt == len(hd["v"]) - 1))
                    mm.then_inc(*made("attended", *hd["id"]))

                scores(0)
                owed = None
                for i, (hd, j) in enumerate(tiles):
                    if i + 1 < len(tiles):
                        scores(i + 1)
                    beside(i)
                    turn(i)
                    if owed is not None:
                        values(owed)
                        owed = None
                    if j == len(hd["tiles"]) - 1:
                        owed = hd
                values(owed)

            def gla_pairs(l, v):
                ntile = 4 if l == 0 else 2
                if v < 0:
                    pe.wait_ge(*when("projected", ("mix1", l), SLOT1[GLAQ]))
                    pe.wait_ge(*when("projected", ("mix1", l), SLOT1[GLAK]))
                else:
                    pe.wait_ge(*when("decayed", l, v))
                ps = [take("pairs", l, v, h) for h in range(4)]
                for t in range(ntile):
                    other = t ^ 1 if v == LEVELS else t
                    for h in range(4):
                        r = slice(32 * h, 32 * h + 32)
                        if v < 0:
                            q, k = proj1[r, GLAQ], proj1[r, GLAK]
                        else:
                            q, k = decays(l, v)[r, 0], decays(l, v)[r, 1]
                        mm = pe.matmul(ps[h][:, t * P:(t + 1) * P], k[:, t * P:(t + 1) * P],
                                       q[:, other * P:(other + 1) * P], start=True, stop=True,
                                       skip_group_check=True)
                        if t == ntile - 1:
                            mm.then_inc(*made("pairs", l, v, h))

            def gla_khat(l):
                pe.wait_ge(*when("khat_t", l))
                p = take("khat", l)
                for g in range(2):
                    for t in range(2):
                        mm = pe.transpose(p[:, (2 * g + t) * P:(2 * g + t + 1) * P],
                                          act_out[:, 0, g * NZ + t * P:g * NZ + (t + 1) * P], cst(C_IDENT))
                mm.then_inc(*made("khat", l))

            def gla_state(l):
                pe.wait_ge(*when("khat_sb", l))
                p = take("state", l)
                for g in range(2):
                    for t in range(2):
                        mm = pe.matmul(p[:, g * SEQ:(g + 1) * SEQ], khat[:, 2 * g + t],
                                       v1[:, 2 + t, GLAV:GLAV + 256], start=(t == 0), stop=(t == 1))
                mm.then_inc(*made("state", l))

            def gla_out(l, s, h):
                po = (h % 2) * HD
                p = take("gla_out", l, s, h)
                vcol = slice(GLAV + h * HD, GLAV + (h + 1) * HD)
                pe.wait_ge(*when("gla_scores", l, LEVELS - 1, h))
                pe.wait_ge(*when("gla_cross", l, h))
                for i in range(2):
                    out = p[po:po + HD, i * P:(i + 1) * P]
                    t, u = 2 * s + i, 2 * s + 1 - i
                    pe.matmul(out, v1[:, t, vcol], gla_s[:, h, t], start=True, stop=False)
                    mm = pe.matmul(out, v1[:, u, vcol], cross[:, h, u], start=False, stop=(s == 1))
                    if s == 0:
                        r = slice(32 * h, 32 * h + 32)
                        for g in range(2):
                            mm = pe.matmul(out, state[r, g, h * HD:(h + 1) * HD],
                                           act_out[r, 1, g * NX + i * P:g * NX + (i + 1) * P],
                                           start=False, stop=(g == 1))
                mm.then_inc(*made("gla_out", l, s, h))

            def rotation(tag, i, src, at, slot, n):
                pe.matmul(take("rotated", tag, i)[:, 0:n], at, src[:, slot, 0:n],
                          start=True, stop=True).then_inc(*made("rotated", tag, i))

            def beside_na(l, k):
                tm = ("mix1", l)
                if 1 <= k < 7:
                    project(tm, PROJ1, 12 + k, N1, width1(l, PROJ1[12 + k]), proj1, VTEMP1,
                            [(t * P, P) for t in range(4)])
                if k == 7:
                    pe.wait_ge(*when("projected", tm, SLOT1[GATE]))
                    for g in range(2):
                        pe.matmul(take("gate_in", l, g), wgate[0:32, l, g * P:(g + 1) * P],
                                  proj1[0:32, GATE, 0:N1], start=True, stop=True).then_inc(*made("gate_in", l, g))
                if 8 <= k < 11:
                    head_mean(tm, k - 4, norm_items(l)[k - 4][2])
                if k == 11 or (k == 12 and l == 0):
                    dft_features(l, k - 11)
                if k == 13 or (k == 14 and l == 0):
                    dft_tokens(l, k - 13)
                if k >= 13:
                    pe.wait_ge(*when("head_normed", tm, k - 9))
                    rotation(tm, k - 13, proj1, cst(C_PERM64), rope_items[k - 13], NX)

            def beside_gqa(l, k):
                if k == 0:
                    gla_pairs(l, -1)
                if k == 1:
                    gla_khat(l)
                if k == 2:
                    gla_state(l)
                if 4 <= k <= 4 + LEVELS:
                    gla_pairs(l, k - 4)
                if k >= 5 + LEVELS:
                    pe.wait_ge(*when("state_sb", l))
                    pe.wait_ge(*when("q_from_start", l))
                    for s, h in gla_outs(l, k):
                        gla_out(l, s, h)

            def beside_fox(l, k):
                tp = ("b2", l)
                if k < 12:
                    project(tp, PROJ2, BESIDE2 + k, N2, N2, proj2, VTEMP2, TILES2)
                for i in rope_steps(k):
                    pe.wait_ge(*when("projected", tp, SLOT2[RQ + i]))
                    rotation(tp, i, proj2, cst2(C_PERM128), RQ + i, N2)
                if 12 <= k < 16:
                    ret_pairs(l, k - 12)
                if 13 <= k < 17:
                    ret_values(l, k - 13)
                if 16 <= k < 20:
                    ret_stat(l, "ret_mean", k - 16)
                if 19 <= k < 23:
                    ret_stat(l, "ret_var", k - 19)

            def ret_pairs(l, h):
                pe.wait_ge(*when("roped", ("b2", l), h))
                pe.wait_ge(*when("roped", ("b2", l), 4 + h))
                p = take("ret_pairs", l, h)
                at = 0
                for j, (t0, tn) in enumerate(TILES2):
                    mm = pe.matmul(p[0:tn, at:at + N2 - t0], proj2[:, RK + h, t0:t0 + tn],
                                   proj2[:, RQ + h, t0:N2], start=True, stop=True, skip_group_check=True)
                    at += N2 - t0
                mm.then_inc(*made("ret_pairs", l, h))

            def ret_values(l, h):
                p = take("ret_out", l, h)
                for j, (t0, tn) in enumerate(TILES2):
                    pe.wait_ge(*when("ret_decayed", l, h, j))
                    mm = pe.matmul(p[:, t0:N2], v2[0:tn, j, 512 + h * P:512 + (h + 1) * P],
                                   ret_p[0:tn, h % 2, j, t0:N2], start=(j == 0), stop=(j == 2))
                mm.then_inc(*made("ret_out", l, h))

            def ret_stat(l, what, h):
                if what == "ret_mean":
                    pe.wait_ge(*when("ret_sb", l, h))
                    x = proj2[:, RQ + h, :]
                else:
                    pe.wait_ge(*when("ret_squares", l, h))
                    x = squares[:, h % 2, 0:N2]
                pe.matmul(take(what, l, h)[:, 0:N2], cst2(C_ONES128), x, start=True, stop=True).then_inc(
                    *made(what, l, h))

            pe.wait_ge(*when("c_cols_silu", 0))
            for j in range(FIRST_MOD):
                if j % 4 == 0:
                    p = take("first_rows", j // 4)
                pe.wait_ge(*when(f"first_mod_loaded{j % FIRST_SLOTS}", j))
                for k in range(2):
                    c = 2 * (j % 4) + k
                    mm = pe.matmul(p[0:2, :], c_cols[:, c], first_mod[:, j % FIRST_SLOTS, k], start=(c == 0),
                                   stop=(c == KC - 1))
                mm.then_inc(*made("first_mod", j))
                if j == 11:
                    pe.wait_ge(*when("consts_loaded", 0))
                    for g in range(2):
                        mean_square(("start",), g)
            p = take("first_turned")
            for g in range(4):
                pe.wait_ge(*when("first_rows_sb", g))
                for j in range(4 * g, 4 * g + 4):
                    mm = pe.transpose(p[:, 2 * j:2 * j + 2], first_rows[:, j * P:(j + 1) * P], cst(C_IDENT, 2, 2))
            mm.then_inc(*made("first_turned"))
            for l in range(DEPTH):
                t1, tm, to, t2 = ("ffn1", l), ("mix1", l), ("out1", l), ("ffn2", l)
                n = N1 if l == 0 else NX
                ffn(t1, N1, N1, 2, ("ffn2", 0) if l else ("start",))
                for i in range(12):
                    project(tm, PROJ1, i, N1, width1(l, PROJ1[i]), proj1, VTEMP1, [(t * P, P) for t in range(4)],
                            t1)
                    if i >= 9:
                        head_mean(tm, i - 9, norm_items(l)[i - 9][2])
                head_mean(tm, 3, N1)
                project(tm, PROJ1, 12, N1, width1(l, PROJ1[12]), proj1, VTEMP1, [])
                for i in range(4):
                    pe.wait_ge(*when("head_normed", tm, i))
                per = 1 + l
                attention(na_heads(l), lambda i: [beside_na(l, k) for k in range(per * i, per * (i + 1))])
                for i in range(3):
                    pe.wait_ge(*when("roped", tm, i))
                attention(gqa_heads(l), lambda i: [beside_gqa(l, k) for k in range(per * i, per * (i + 1))])
                for i in range(2):
                    head_mean(("gla", l), i, n)
                project_out(to, N1, n, [0, 1, 2, 3, 6, 7, 4, 5])
                ffn(t2, N1, n, 2 - l, to)
            pe.wait_ge(*when("consts2_loaded", 0))
            for l in range(DEPTH):
                tp, to, tf = ("b2", l), ("out2", l), ("ffn", l)
                for i in range(BESIDE2):
                    project(tp, PROJ2, i, N2, N2, proj2, VTEMP2, TILES2, ("ffn", 0) if l else ("ffn2", 1))
                pe.wait_ge(*when("negc", l))
                pe.wait_ge(*when("projected", tp, 11))
                pe.wait_ge(*when("projected", tp, 12))
                attention(fox_heads(l), lambda i: beside_fox(l, i))
                n = N2 if l == 0 else NX
                project_out(to, N2, n, list(range(KC)))
                ffn(tf, N2, n, 1, to)
            assert unit[0] == UNITS, (unit[0], UNITS)

        @block.scalar
        def _(act):
            split = [0, 0]

            def split_ahead(used):
                split[1] += used
                while split[0] < min(split[1] + RING, UNITS):
                    u = split[0]
                    split[0] += 1
                    if u >= RING:
                        act.wait_ge(*when("unit_used", u - RING))
                    act.wait_ge(unit_loaded[u % RING], 16 * (u // RING + 1))
                    act.activation(high[:, u % RING], ring[:, u % RING], ACT.Copy).then_inc(high_parts, 1)

            def ln_exp():
                act.preload_act_table_set(LN_EXP)

            def inverse_root(out, p, n, tag, frees):
                act.activation(out[:, 0:n], p[:, 0:n], ACT.Ln, bias=eps_one[:, 0:1]).then_inc(
                    *made("ln_mean", tag, frees=frees))
                act.wait_ge(*when("ln_mean", tag))
                act.activation(out[:, 0:n], out[:, 0:n], ACT.Exp, scale=-0.5).then_inc(*made("rstd", tag))

            def square(tag, d, g, *ready):
                if ready:
                    act.wait_ge(*when(*ready))
                base = after(tag)[2]
                a, b = norm_cols(tag, g)
                out = sumsq[:, a:b] if d == 0 else squares[:, d % 2, a:b]
                if d >= 3:
                    act.wait_ge(*when("sumsq", *sum_key(tag, d - 2, g)))
                act.activation(out, resid[:, d, base + a:base + b], ACT.Square).then_inc(
                    *made("resid_squares", tag, d, g))

            def root_of_mean(tag, g):
                act.wait_ge(*when("mean", tag, g))
                p = bank("mean", tag, g)
                a, b = norm_cols(tag, g)
                inverse_root(rstd[:, 0, a:b], p, b - a, (tag, g), ("mean", tag, g))

            def high_part(tag, out, c, n, whole, ready):
                act.wait_ge(*ready)
                act.activation(out[0][:, c, 0:n], whole, ACT.Copy).then_inc(*made("x_high", tag, c))

            def norm(tag, g, chunks):
                _, _, _, to, (l, m) = after(tag)
                hi, _ = parts_for(to)
                a, b = norm_cols(tag, g)
                s = stream_of(tag, g)
                for c in chunks:
                    act.wait_ge(*when("scaled", to, c, g))
                    if isinstance(m, str):
                        act.activation(hi[:, c, a:b], scaled[:, c, a:b], ACT.Copy).then_inc(*made("x_high", to, c, g))
                        continue
                    shift = mod[:, l, s, m * KC + c:m * KC + c + 1]
                    act.wait_ge(*when("mod", l, m))
                    act.activation(hi[:, c, a:b], scaled[:, c, a:b], ACT.Identity, bias=shift).then_inc(
                        *made("x_high", to, c, g))
                    if c % 2:
                        act.activation(scaled[:, c, a:b], scaled[:, c, a:b], ACT.Identity, bias=shift).then_inc(
                            *made("shifted", to, c, g))

            def late_chunks(tag, h):
                late, _, _, to, _ = after(tag)
                if not late:
                    root_of_mean(tag, 0)
                    if to:
                        norm(tag, 0, range(4))
                    split_ahead(1)
                    if to:
                        norm(tag, 0, range(4, KC))
                    return
                for d in late:
                    square(tag, d, 0, "resid", tag, h, d, 0)
                root_of_mean(tag, 0)
                split_ahead(1)
                norm(tag, 0, range(2))
                for d in late[:-1]:
                    square(tag, d, 1, "resid", tag, h, d, 1)
                split_ahead(1)
                norm(tag, 0, range(2, 4))
                square(tag, KC - 1, 1, "resid", tag, h, KC - 1, 1)
                norm(tag, 0, range(4, KC))
                root_of_mean(tag, 1)
                split_ahead(1)
                norm(tag, 1, range(KC))

            def ffn(tag, n, parts):
                hh, _ = hidden_parts(n, parts)
                nf = FC // parts
                for h in range(parts):
                    for f in range(nf + 1):
                        if f < nf:
                            act.wait_ge(*when("gate", tag, h, f))
                            p = bank("gate", tag, h, f)
                            if f >= 2:
                                act.wait_ge(*when("hidden", tag, h, f - 2))
                            act.activation(act_out[:, f % 2, 0:n], p[:, 0:n], ACT.Silu).then_inc(
                                *made("silu", tag, h, f, frees=("gate", tag, h, f)))
                            split_ahead(1)
                        if f >= 1:
                            act.wait_ge(*when("hidden", tag, h, f - 1))
                            act.activation(hh[:, f - 1], fresh[:, (f - 1) % 2, 0:n], ACT.Copy).then_inc(
                                *made("hidden_high", tag, h, f - 1))
                        if f < nf:
                            split_ahead(1)
                    last = h == parts - 1
                    if last:
                        ln_exp()
                    for d in range(first_late(tag) if last else KC):
                        before, then = splits(d, nf)
                        split_ahead(before)
                        if d < KC - 1 or not last:
                            split_ahead(then)
                        if last:
                            square(tag, d, "all", "resid", tag, h, d)
                    if last:
                        late_chunks(tag, h)

            def project(tag, plan, i, n, src, vtemp, l):
                kind, dst, width = plan[i][:3]
                if i and plan[i - 1][0] == "V" and (i - 1) % 2:
                    act.wait_ge(*when("v_turned", tag, i - 1))
                    p = bank("v_turned", tag, i - 1).rearrange("p (t n) -> p t n", t=4)
                    v0 = plan[i - 1][1]
                    if tag[0] == "mix1":
                        act.activation(v1[:, :, v0:v0 + P], p, ACT.Copy).then_inc(
                            *made("v_placed_act", tag, i - 1, frees=("v_turned", tag, i - 1)))
                    else:
                        act.activation(v2[:, 0:2, v0:v0 + P], p[:, 0:2], ACT.Copy)
                        act.activation(v2[0:META, 2, v0:v0 + P], p[0:META, 2], ACT.Copy).then_inc(
                            *made("v_placed_act", tag, i - 1, frees=("v_turned", tag, i - 1)))
                if on_act(tag, i):
                    act.wait_ge(*when("proj", tag, i))
                    p = bank("proj", tag, i)
                    func, scale = ACT.Copy, 1.0
                    if kind == "V":
                        dst, width = vtemp[i], P
                    elif tag[0] == "mix1":
                        scale = 32 ** -0.5 if dst == GLAQ else 1.0
                        func = ACT.Silu if GLAR <= dst < GLAR + 2 else ACT.Copy
                    else:
                        scale = HD ** -0.5 if FQ <= dst < FQ + 4 else 1.0
                        func = ACT.Silu if dst >= RG else ACT.Copy
                    out = negc[0:8, 0, :] if dst == FLOG else src[0:width, dst, 0:n]
                    act.activation(out, p[0:width, 0:n], func, scale=scale).then_inc(
                        *made("projected_act", tag, i, frees=("proj", tag, i)))
                    ev.table[("projected", tag, i)] = ev.table[("projected_act", tag, i)]
                    if func == ACT.Silu and dst == (GLAR + 1 if tag[0] == "mix1" else RG + 3):
                        ln_exp()
                split_ahead(1)

            def head_square(tag, i, ready, x, n):
                act.wait_ge(*ready)
                if i >= 2:
                    act.wait_ge(*when("head_mean", tag, i - 2))
                act.activation(squares[:, i % 2, 0:n], x, ACT.Square).then_inc(*made("head_squares", tag, i))

            def head_root(tag, i, n):
                act.wait_ge(*when("head_mean", tag, i))
                p = bank("head_mean", tag, i)
                if i >= 2:
                    act.wait_ge(*when("head_normed", tag, i - 2))
                inverse_root(rstd[:, i % 2], p, n, (tag, i), ("head_mean", tag, i))

            def qk_square(l, i):
                tm, (slot, _, n) = ("mix1", l), norm_items(l)[i]
                head_square(tm, i, when("projected", tm, SLOT1[slot]), proj1[:, slot, 0:n], n)

            def attention(heads, beside):
                tiles = [(hd, j) for hd in heads for j in range(len(hd["tiles"]))]

                def exps(i):
                    hd, j = tiles[i]
                    q0, nq, nk = hd["tiles"][j]
                    key = (*hd["id"], j)
                    no = tile_no[key]
                    st = stat[0:nq, no % 4]
                    act.wait_ge(*when("row_max", *key))
                    if no >= 2:
                        act.wait_ge(*when("turned", *tile_keys[no - 2]))
                    out = probs[0:nq, no % 2]
                    p = bank("scores", *key)
                    if hd["kind"] == "na":
                        act.activation(out[:, 0:NX], biased_x[:, no % 2], ACT.Exp, bias=st[:, 3:4],
                                       accum_out=st[:, 4:5])
                        act.activation(out[:, NX:N1], p[:, NX:N1], ACT.Exp, bias=st[:, 3:4],
                                       accum_out=st[:, 5:6]).then_inc(*made("exps", *key, frees=("scores", *key)))
                    elif hd["kind"] == "fox":
                        act.activation(out[:, 0:nk], biased[0:nq, no % 2, 0:nk], ACT.Exp, bias=st[:, 3:4],
                                       accum_out=st[:, 4:5]).then_inc(*made("exps", *key))
                    else:
                        act.activation(out[:, 0:nk], p[:, 0:nk], ACT.Exp, bias=st[:, 3:4],
                                       accum_out=st[:, 4:5]).then_inc(*made("exps", *key, frees=("scores", *key)))

                def turned(i):
                    hd, j = tiles[i]
                    q0, nq, nk = hd["tiles"][j]
                    key = (*hd["id"], j)
                    no = head_no[hd["id"]]
                    act.wait_ge(*when("turned", *key))
                    p = bank("turned", *key).rearrange("p (k n) -> p k n", k=4)
                    if no >= 2 and j == 0:
                        act.wait_ge(*when("attended", *every[no - 2]["id"]))
                    full = nk // P
                    last = act.activation(probs_t[:, no % 2, 0:full, q0:q0 + nq], p[:, 0:full, 0:nq], ACT.Copy)
                    if nk % P:
                        last = act.activation(probs_t[0:nk % P, no % 2, full, q0:q0 + nq],
                                              p[0:nk % P, full, 0:nq], ACT.Copy)
                    last.then_inc(*made("probs_t", *key, frees=("turned", *key)))

                for i in range(len(tiles)):
                    exps(i)
                    if i >= 1:
                        turned(i - 1)
                    beside(i)
                turned(len(tiles) - 1)

            biased_x = biased.rearrange("p b n -> p (b n)")[:, 0:2 * NX].rearrange("p (b n) -> p b n", b=2)

            def gla_gates(l):
                for g in range(2):
                    act.wait_ge(*when("neg_abs", l, g))
                    act.activation(decay[:, 0, g], decay[:, 0, g], ACT.Exp).then_inc(*made("gate_exp", l, g))
                for g in range(2):
                    act.wait_ge(*when("gate_exp", l, g))
                    act.activation(decay[:, 0, g], decay[:, 0, g], ACT.Ln, bias=eps_one[:, 1:2]).then_inc(
                        *made("gate_ln", l, g))

            def gla_ends(l):
                act.wait_ge(*when("z_exponents", l, 1))
                act.activation(act_out[:, 0, :], act_out[:, 0, :], ACT.Exp, scale=1.0 / 16).then_inc(
                    *made("z_decays", l))
                for g in range(2):
                    act.activation(act_out[:, 1, g * NX:(g + 1) * NX], gates[:, g, 0:NX], ACT.Exp,
                                   scale=1.0 / 16).then_inc(*made("x_decays", l, g))

            def beside_na(l, k):
                tm = ("mix1", l)
                if 1 <= k < 7:
                    project(tm, PROJ1, 12 + k, width1(l, PROJ1[12 + k]), proj1, VTEMP1, l)
                if k == 8:
                    gla_gates(l)
                if 8 <= k < 11:
                    qk_square(l, k - 4)
                if 9 <= k < 12:
                    head_root(tm, k - 5, norm_items(l)[k - 5][2])
                if k == 11:
                    gla_ends(l)

            def beside_gqa(l, k):
                n = N1 if l == 0 else NX
                if k == 1:
                    act.wait_ge(*when("khat", l))
                    p = bank("khat", l)
                    act.activation(khat, p.rearrange("p (t n) -> p t n", t=4), ACT.Copy).then_inc(
                        *made("khat_sb", l, frees=("khat", l)))
                if k == 2:
                    act.wait_ge(*when("state", l))
                    p = bank("state", l)
                    act.activation(state, p.rearrange("p (g n) -> p g n", g=2), ACT.Copy).then_inc(
                        *made("state_sb", l, frees=("state", l)))
                if 3 <= k <= 3 + LEVELS:
                    v = k - 3
                    act.wait_ge(*when("exponents", l, v, 3))
                    act.activation(decays(l, v), decays(l, v), ACT.Exp,
                                   scale=1.0 / 16).then_inc(*made("decays", l, v))
                if k == 5 + LEVELS:
                    for h in range(4):
                        act.wait_ge(*when("pairs", l, LEVELS, h))
                        p = bank("pairs", l, LEVELS, h)
                        act.activation(cross[:, h, 0:n // P], p[:, 0:n].rearrange("p (t n) -> p t n", n=P),
                                       ACT.Copy).then_inc(*made("gla_cross", l, h, frees=("pairs", l, LEVELS, h)))

            def beside_fox(l, k):
                if k < 12:
                    project(("b2", l), PROJ2, BESIDE2 + k, N2, proj2, VTEMP2, l)
                if 13 <= k < 17:
                    h = k - 13
                    act.wait_ge(*when("ret_out", l, h))
                    p = bank("ret_out", l, h)
                    act.activation(proj2[:, RQ + h, :], p[:, 0:N2], ACT.Copy).then_inc(
                        *made("ret_sb", l, h, frees=("ret_out", l, h)))
                if 18 <= k < 22:
                    ret_square(l, k - 18)
                if k >= 20:
                    ret_root(l, k - 20)

            def ret_square(l, h):
                act.wait_ge(*when("ret_centred", l, h))
                if h >= 2:
                    act.wait_ge(*when("ret_var", l, h - 2))
                act.activation(squares[:, h % 2, 0:N2], proj2[:, RQ + h, :], ACT.Square).then_inc(
                    *made("ret_squares", l, h))

            def ret_root(l, h):
                act.wait_ge(*when("ret_var", l, h))
                p = bank("ret_var", l, h)
                if h >= 2:
                    act.wait_ge(*when("ret_normed", l, h - 2))
                inverse_root(rstd[:, h % 2], p, N2, ("ret", l, h), ("ret_var", l, h))

            act.wait_ge(*when("c_cols_loaded", 0))
            act.activation(c_cols, c_cols, ACT.Silu).then_inc(*made("c_cols_silu", 0))
            act.wait_ge(*when("eps_one", 1))
            act.wait_ge(*when("x_loaded", 0))
            act.wait_ge(*when("ctx_loaded", 0))
            for d in range(KC):
                square(("start",), d, "all")
            split_ahead(0)
            ln_exp()
            for g in range(2):
                root_of_mean(("start",), g)
            for g in range(2):
                norm(("start",), g, range(KC))
            for s in range(2):
                act.wait_ge(*when("c_ctx_loaded" if s else "c_loaded"))
                act.activation(csilu[:, s], csilu[:, s], ACT.Silu).then_inc(*made("c_silu", s))
            for l in range(DEPTH):
                t1, tm, to, t2 = ("ffn1", l), ("mix1", l), ("out1", l), ("ffn2", l)
                n = N1 if l == 0 else NX
                ffn(t1, N1, 2)
                for i in range(12):
                    project(tm, PROJ1, i, width1(l, PROJ1[i]), proj1, VTEMP1, l)
                    if i >= 8:
                        qk_square(l, i - 8)
                    if i >= 9:
                        head_root(tm, i - 9, norm_items(l)[i - 9][2])
                head_root(tm, 3, N1)
                project(tm, PROJ1, 12, width1(l, PROJ1[12]), proj1, VTEMP1, l)
                per = 1 + l
                attention(na_heads(l), lambda i: [beside_na(l, k) for k in range(per * i, per * (i + 1))])
                attention(gqa_heads(l), lambda i: [beside_gqa(l, k) for k in range(per * i, per * (i + 1))])
                act.wait_ge(*when("gla_out", l, 1 - l, 3))
                for c in range(4):
                    s = MIX1[c]
                    high_part(to, x_parts(N1), c, n, proj1[:, s, 0:n],
                              when("attended_sb", "nax" if l else "naz", l, 3) if c > 1 else when("dft_mix", l, 1 - l))
                for i in range(2):
                    head_square(("gla", l), i, when("gla_out_sb", l, 1 - l, 2 * i + 1), proj1[:, GLAQ + i, 0:n], n)
                for i in range(2):
                    head_root(("gla", l), i, n)
                for c in (6, 7, 4, 5):
                    high_part(to, x_parts(N1), c, n, proj1[:, MIX1[c], 0:n],
                              when("attended_sb", "gqax" if l else "gqaz", l, 3) if c > 5 else when("mix_gla", l, c - 4))
                for d in range(first_late(to)):
                    if d < KC - 1:
                        split_ahead(1)
                    square(to, d, "all", "resid", to, 0, d)
                late_chunks(to, 0)
                if l == 1:
                    act.wait_ge(*when("meta_loaded", 0))
                ffn(t2, n, 2 - l)
            for l in range(DEPTH):
                tp, to, tf = ("b2", l), ("out2", l), ("ffn", l)
                for i in range(BESIDE2):
                    project(tp, PROJ2, i, N2, proj2, VTEMP2, l)
                    if i == 6:
                        act.wait_ge(*when("flog_neg_abs", l))
                        act.activation(negc[0:8, 1, :], negc[0:8, 1, :], ACT.Exp).then_inc(*made("flog_exp", l))
                        act.wait_ge(*when("flog_exp", l))
                        act.activation(negc[0:8, 1, :], negc[0:8, 1, :], ACT.Ln, bias=eps_one[0:8, 1:2]).then_inc(
                            *made("flog_ln", l))
                attention(fox_heads(l), lambda i: beside_fox(l, i))
                n = N2 if l == 0 else NX
                act.wait_ge(*when("ret_out", l, 3))
                for c in range(KC):
                    high_part(to, x_parts(N2), c, n, proj2[:, MIX2[c], N2 - n:N2],
                              when("attended_sb", "fox", l, 7) if c < 4 else when("mix_ret", l, c - 4))
                for d in range(first_late(to)):
                    if d < KC - 1:
                        split_ahead(1)
                    square(to, d, "all", "resid", to, 0, d)
                late_chunks(to, 0)
                ffn(tf, n, 1)

        @block.vector
        def _(dve):
            split = [0, 0]

            def split_ahead(used):
                split[1] += used
                while split[0] < min(split[1] + RING, UNITS):
                    u = split[0]
                    split[0] += 1
                    dve.wait_ge(high_parts, u + 1)
                    dve.tensor_tensor(low[:, u % RING], ring[:, u % RING], high_f[:, u % RING],
                                      ALU.subtract).then_inc(low_parts, 1)

            def mod_dot(l, j):
                n = l * NMOD * KC + j
                streams = 1 if (l == 1 and j >= 5 * KC) else 2
                dve.wait_ge(*when(f"mod_loaded{n % MOD_RING}", n))
                for s in range(streams):
                    dve.wait_ge(*when("c_silu", s))
                    if dots[s] is not None:
                        dve.wait_ge(*when(*dots[s]))
                    dots[s] = ("mod_dot", n) if s == streams - 1 else ("mod_dot_x", n)
                    dve.tensor_tensor_reduce(junk[:, s], mod_ring[:, n % MOD_RING], csilu[:, s], 1.0, 0.0,
                                             ALU.mult, ALU.add, mod_raw[:, l, s, j:j + 1]).then_inc(*made(*dots[s]))
                if j % KC == KC - 1:
                    mod_finish(l, j // KC, streams)

            dots = [None, None]

            def mod_finish(l, m, streams):
                cols = slice(m * KC, (m + 1) * KC)
                if l == 0 and m < 2:
                    dve.wait_ge(*when("first_mod_raw"))
                else:
                    dve.wait_ge(*when("mod_dot", l * NMOD * KC + m * KC + KC - 1))
                at = l * SW1 + S_L1["bmod"] + m * KC
                b = small[:, at:at + KC].unsqueeze(1).broadcast_to([P, streams, KC])
                add = 1.0 if m in (1, 4, 7) else 0.0
                dve.scalar_tensor_tensor(mod[:, l, 0:streams, cols], mod_raw[:, l, 0:streams, cols], add, b,
                                         ALU.add, ALU.add).then_inc(*made("mod_sum", l, m))
                dve.wait_ge(*when("mod_sum", l, m))
                half = 0.5 if m in (2, 8) else 1.0
                dve.tensor_scalar(mod[:, l, 0:streams, cols], mod[:, l, 0:streams, cols], half, None,
                                  ALU.mult).then_inc(*made("mod", l, m))

            def sum_squares(tag, d, g):
                a, b = norm_cols(tag, g)
                dve.wait_ge(*when("resid_squares", tag, d, g))
                if d == 0:
                    return
                if d >= 2:
                    dve.wait_ge(*when("sumsq", *sum_key(tag, d - 1, g)))
                dve.tensor_tensor(sumsq[:, a:b], sumsq[:, a:b], squares[:, d % 2, a:b], ALU.add).then_inc(
                    *made("sumsq", tag, d, g))
                if g == "all" and d == KC - 1:
                    for k in range(2):
                        ev.table[("sumsq", tag, d, k)] = ev.table[("sumsq", tag, d, g)]

            def low_part(tag, out, c, n, whole):
                dve.wait_ge(*when("x_high", tag, c))
                dve.tensor_tensor(out[1][:, c, 0:n], whole, out[0][:, c, 0:n].bitcast(F32),
                                  ALU.subtract).then_inc(*made("x_low_dve", tag, c))
                ev.table[("x_low", tag, c)] = ev.table[("x_low_dve", tag, c)]

            def norm(tag, g, chunks):
                _, _, base, to, (l, m) = after(tag)
                hi, lo = parts_for(to)
                a, b = norm_cols(tag, g)
                s = stream_of(tag, g)
                gain = isinstance(m, str)
                if not gain:
                    dve.wait_ge(*when("mod", l, m + 1))
                dve.wait_ge(*when("rstd", (tag, g)))
                for c in chunks:
                    scale = scalar2(l, m, c) if gain else mod[:, l, s, (m + 1) * KC + c:(m + 1) * KC + c + 1]
                    dve.scalar_tensor_tensor(scaled[:, c, a:b], resid[:, c, base + a:base + b], scale,
                                             rstd[:, 0, a:b], ALU.mult, ALU.mult).then_inc(*made("scaled", to, c, g))
                    if c % 2:
                        e = c - 1
                        dve.wait_ge(*when("x_high", to, e, g))
                        high_e = hi[:, e, a:b].bitcast(F32)
                        if gain:
                            last = dve.tensor_tensor(lo[:, e, a:b], scaled[:, e, a:b], high_e, ALU.subtract)
                        else:
                            last = dve.scalar_tensor_tensor(lo[:, e, a:b], scaled[:, e, a:b],
                                                            mod[:, l, s, m * KC + e:m * KC + e + 1], high_e,
                                                            ALU.add, ALU.subtract)
                        last.then_inc(*made("x_low_dve", to, e, g))
                        ev.table[("x_low", to, e, g)] = ev.table[("x_low_dve", to, e, g)]

            def ffn(tag, n, parts, l=None):
                nf = FC // parts
                for f in range(parts * nf):
                    h, g = f // nf, f % nf
                    split_ahead(1)
                    todo = list(mod_chunks(l, h, g)) if l is not None else []
                    for j in todo[:len(todo) // 2]:
                        mod_dot(l, j)
                    dve.wait_ge(*when("up", tag, h, g))
                    p = bank("up", tag, h, g)
                    dve.wait_ge(*when("silu", tag, h, g))
                    if g >= 2:
                        dve.wait_ge(*when("hidden_low", tag, h, g - 2))
                    dve.tensor_tensor(fresh[:, g % 2, 0:n], act_out[:, g % 2, 0:n], p[:, 0:n], ALU.mult).then_inc(
                        *made("hidden", tag, h, g, frees=("up", tag, h, g)))
                    split_ahead(1)
                    for j in todo[len(todo) // 2:]:
                        mod_dot(l, j)
                    if g == nf - 1:
                        yield h

            def residual(tag, l, m, streams, h, nb, last_part, dots_of=None):
                late, groups, base, to, _ = after(tag)
                if m is None:
                    streams = [(None, 0, groups[-1][1])]
                else:
                    dve.wait_ge(*when("mod", l, m))
                base = META if m is not None else base

                def add(d, parts, *g):
                    dve.wait_ge(*when("down", tag, h, d, *g))
                    p = bank("down", tag, h, d, *g)
                    at = parts[0][1]
                    for s, a, b in parts:
                        x = resid[:, d, base + a:base + b]
                        if s is None:
                            last = dve.tensor_tensor(x, x, p[:, a - at:b - at], ALU.add)
                        else:
                            last = dve.scalar_tensor_tensor(x, p[:, a - at:b - at],
                                                            mod[:, l, s, m * KC + d:m * KC + d + 1], x,
                                                            ALU.mult, ALU.add)
                    last.then_inc(*made("resid", tag, h, d, *g, frees=("down", tag, h, d, *g)))

                def add_group(d, g):
                    a, b = groups[g][:2]
                    add(d, [(None if m is None else stream_of(tag, g), a, b)], g)

                for d in range(first_late(tag) if last_part else KC):
                    before, then = splits(d, nb)
                    split_ahead(before)
                    add(d, streams)
                    if d >= 1 and last_part:
                        sum_squares(tag, d - 1, "all")
                    if d < KC - 1 or not last_part:
                        split_ahead(then)
                    if dots_of is not None and not last_part:
                        for j in mod_chunks(dots_of, None, d):
                            mod_dot(dots_of, j)
                if not last_part:
                    return
                if not late:
                    sum_squares(tag, KC - 1, "all")
                    if to:
                        norm(tag, 0, range(4))
                    split_ahead(1)
                    if to:
                        norm(tag, 0, range(4, KC))
                    return
                for d in late:
                    add_group(d, 0)
                    sum_squares(tag, d - 1, "all" if d == late[0] else 0)
                sum_squares(tag, KC - 1, 0)
                norm(tag, 0, [0])
                split_ahead(1)
                norm(tag, 0, [1])
                for d in late[:-1]:
                    add_group(d, 1)
                    if d > late[0]:
                        sum_squares(tag, d - 1, 1)
                split_ahead(1)
                norm(tag, 0, range(2, 4))
                add_group(KC - 1, 1)
                sum_squares(tag, KC - 2, 1)
                sum_squares(tag, KC - 1, 1)
                norm(tag, 0, range(4, KC))
                split_ahead(1)
                norm(tag, 1, range(KC))

            def project(tag, plan, i, n, src, vtemp):
                kind, dst, width = plan[i][:3]
                if i and plan[i - 1][0] == "V" and (i - 1) % 2 == 0:
                    dve.wait_ge(*when("v_turned", tag, i - 1))
                    p = bank("v_turned", tag, i - 1).rearrange("p (t n) -> p t n", t=4)
                    v0 = plan[i - 1][1]
                    if tag[0] == "mix1":
                        dve.tensor_copy(v1[:, :, v0:v0 + P], p).then_inc(
                            *made("v_placed_dve", tag, i - 1, frees=("v_turned", tag, i - 1)))
                    else:
                        dve.tensor_copy(v2[:, 0:2, v0:v0 + P], p[:, 0:2])
                        dve.tensor_copy(v2[0:META, 2, v0:v0 + P], p[0:META, 2]).then_inc(
                            *made("v_placed_dve", tag, i - 1, frees=("v_turned", tag, i - 1)))
                if not on_act(tag, i):
                    dve.wait_ge(*when("proj", tag, i))
                    p = bank("proj", tag, i)
                    scale = 1.0
                    if kind == "V":
                        dst, width = vtemp[i], P
                    elif tag[0] == "b2" and FQ <= dst < FQ + 4:
                        scale = HD ** -0.5
                    out = negc[0:8, 0, :] if dst == FLOG else src[0:width, dst, 0:n]
                    dve.tensor_scalar(out, p[0:width, 0:n], scale, None, ALU.mult).then_inc(
                        *made("projected_dve", tag, i, frees=("proj", tag, i)))
                    ev.table[("projected", tag, i)] = ev.table[("projected_dve", tag, i)]
                split_ahead(1)

            def head_norm(tag, i, x, gain, n, *ready):
                dve.wait_ge(*when("rstd", (tag, i)))
                dve.wait_ge(*when(*ready))
                dve.scalar_tensor_tensor(x, x, gain, rstd[:, i % 2, 0:n], ALU.mult, ALU.mult).then_inc(
                    *made("head_normed", tag, i))

            def qk_norm(l, i):
                slot, gain, n = norm_items(l)[i]
                head_norm(("mix1", l), i, proj1[:, slot, 0:n], scalar1(l, gain), n, "projected", ("mix1", l),
                          SLOT1[slot])

            def rope(tag, i, x, cos, sin, n, *ready):
                dve.wait_ge(*when("rotated", tag, i))
                p = bank("rotated", tag, i)
                if i >= 1:
                    dve.wait_ge(*when("roped", tag, i - 1))
                dve.wait_ge(*when(*ready))
                dve.tensor_tensor(fresh[:, 0, 0:n], p[:, 0:n], sin, ALU.mult).then_inc(
                    *made("rope_sin", tag, i, frees=("rotated", tag, i)))
                dve.tensor_tensor(fresh[:, 1, 0:n], x, cos, ALU.mult).then_inc(*made("rope_cos", tag, i))
                dve.wait_ge(*when("rope_cos", tag, i))
                dve.tensor_tensor(x, fresh[:, 0, 0:n], fresh[:, 1, 0:n], ALU.add).then_inc(*made("roped", tag, i))

            biased_x = biased.rearrange("p b n -> p (b n)")[:, 0:2 * NX].rearrange("p (b n) -> p b n", b=2)

            def attention(heads, beside):
                tiles = [(hd, j) for hd in heads for j in range(len(hd["tiles"]))]

                def maxima(i):
                    hd, j = tiles[i]
                    q0, nq, nk = hd["tiles"][j]
                    key = (*hd["id"], j)
                    no = tile_no[key]
                    st = stat[0:nq, no % 4]
                    dve.wait_ge(*when("scores", *key))
                    p = bank("scores", *key)
                    if no >= 2:
                        dve.wait_ge(*when("exps", *tile_keys[no - 2]))
                    if hd["kind"] == "na":
                        dve.wait_ge(*when("bias_loaded", hd["id"][1]))
                        at = hd["h"] * 6 * 64 + (2 - 2 * j) * 64
                        dve.tensor_tensor_reduce(biased_x[:, no % 2], p[:, 0:NX], bias[:, at:at + NX], 1.0, -3e38,
                                                 ALU.add, ALU.max, st[:, 0:1]).then_inc(*made("win_max", *key))
                        dve.tensor_reduce(st[:, 1:2], p[:, NX:N1], AX.X, ALU.max).then_inc(*made("ctx_max", *key))
                        dve.wait_ge(*when("win_max", *key))
                        dve.wait_ge(*when("ctx_max", *key))
                        dve.tensor_scalar(st[:, 3:4], st[:, 0:1], st[:, 1:2], -1.0, ALU.max, ALU.mult).then_inc(
                            *made("row_max", *key))
                        return
                    if hd["kind"] == "fox":
                        dve.tensor_tensor_reduce(biased[0:nq, no % 2, 0:nk], p[0:nq, 0:nk],
                                                 cst2(C_CAUSAL + 2 * P - q0, nk, nq), 1.0, -3e38, ALU.add, ALU.max,
                                                 st[:, 0:1]).then_inc(*made("win_max", *key, frees=("scores", *key)))
                    else:
                        dve.tensor_reduce(st[:, 0:1], p[0:nq, 0:nk], AX.X, ALU.max).then_inc(*made("win_max", *key))
                    dve.wait_ge(*when("win_max", *key))
                    dve.tensor_scalar(st[:, 3:4], st[:, 0:1], -1.0, None, ALU.mult).then_inc(*made("row_max", *key))

                def normalise(i):
                    hd, j = tiles[i]
                    q0, nq, nk = hd["tiles"][j]
                    key = (*hd["id"], j)
                    no = tile_no[key]
                    st = stat[0:nq, no % 4]
                    dve.wait_ge(*when("exps", *key))
                    src = st[:, 4:5]
                    if hd["kind"] == "na":
                        dve.tensor_tensor(st[:, 6:7], st[:, 4:5], st[:, 5:6], ALU.add).then_inc(*made("row_sum", *key))
                        dve.wait_ge(*when("row_sum", *key))
                        src = st[:, 6:7]
                    dve.reciprocal(st[:, 7:8], src).then_inc(*made("row_inv", *key))
                    dve.wait_ge(*when("row_inv", *key))
                    dve.tensor_scalar(probs[0:nq, no % 2, 0:nk], probs[0:nq, no % 2, 0:nk], st[:, 7:8], None,
                                      ALU.mult).then_inc(*made("probs", *key))

                def attended(hd):
                    dve.wait_ge(*when("attended", *hd["id"]))
                    p = bank("attended", *hd["id"])
                    dve.tensor_copy(hd["out"], p[hd["po"]:hd["po"] + HD, 0:hd["n"]]).then_inc(
                        *made("attended_sb", *hd["id"], frees=("attended", *hd["id"])))

                maxima(0)
                owed = []
                for i, (hd, j) in enumerate(tiles):
                    if i + 1 < len(tiles):
                        maxima(i + 1)
                    normalise(i)
                    beside(i)
                    if owed and owed[0][0] < i:
                        attended(owed.pop()[1])
                    if j == len(hd["tiles"]) - 1:
                        owed = [(i, hd)]
                attended(owed[0][1])

            def gla_log_gates(l):
                for g in range(2):
                    dve.wait_ge(*when("gate_in", l, g))
                    p = bank("gate_in", l, g)
                    y, e = decay[:, 1, g], decay[:, 0, g]
                    dve.tensor_scalar(y, p, scalar1(l, "bf" if g == 0 else "bb"), None, ALU.add).then_inc(
                        *made("gate_y", l, g, frees=("gate_in", l, g)))
                    dve.wait_ge(*when("gate_y", l, g))
                    dve.scalar_tensor_tensor(e, y, -1.0, y, ALU.mult, ALU.min).then_inc(*made("neg_abs", l, g))

            def gla_sums(l):
                for g in range(2):
                    y, e = decay[:, 1, g], decay[:, 0, g]
                    dve.wait_ge(*when("gate_ln", l, g))
                    dve.scalar_tensor_tensor(e, y, 0.0, e, ALU.min, ALU.subtract).then_inc(*made("log_gate", l, g))
                    dve.wait_ge(*when("log_gate", l, g))
                    for s in range(2):
                        a, b = s * NX, (s + 1) * NX
                        if g == 0:
                            o, i = gates[:, 0, a:b], e[:, a:b]
                        else:
                            stop = a - 1 if a else None
                            o, i = gates[:, 1, b - 1:stop:-1], e[:, b - 1:stop:-1]
                        dve.tensor_tensor_scan(o, eps_one[:, 1:2].broadcast_to([P, NX]), i, 0.0, ALU.mult,
                                               ALU.add).then_inc(*made("gate_sums", l, g, s))
                dve.wait_ge(*when("gate_sums", l, 1, 1))
                for g, edge in ((0, N1 - 1), (1, NX)):
                    dve.tensor_scalar(act_out[:, 0, g * NZ:(g + 1) * NZ], gates[:, g, NX:N1], gates[:, g, edge:edge + 1],
                                      -1.0, ALU.subtract, ALU.mult).then_inc(*made("z_exponents", l, g))

            def gla_ends(l):
                dve.wait_ge(*when("projected", ("mix1", l), SLOT1[GLAQ]))
                dve.wait_ge(*when("projected", ("mix1", l), SLOT1[GLAK]))
                dve.wait_ge(*when("z_decays", l))
                dve.tensor_tensor(act_out[:, 0].rearrange("p (g n) -> p g n", g=2),
                                  act_out[:, 0].rearrange("p (g n) -> p g n", g=2),
                                  proj1[:, GLAK:GLAK + 1, NX:N1].broadcast_to([P, 2, NZ]), ALU.mult).then_inc(
                                      *made("khat_t", l))
                dve.wait_ge(*when("x_decays", l, 1))
                dve.tensor_tensor(act_out[:, 1].rearrange("p (g n) -> p g n", g=2),
                                  act_out[:, 1].rearrange("p (g n) -> p g n", g=2),
                                  proj1[:, GLAQ:GLAQ + 1, 0:NX].broadcast_to([P, 2, NX]), ALU.mult).then_inc(
                                      *made("q_from_start", l))

            def beside_na(l, k):
                tm = ("mix1", l)
                if 1 <= k < 7:
                    project(tm, PROJ1, 12 + k, width1(l, PROJ1[12 + k]), proj1, VTEMP1)
                if k == 7:
                    gla_log_gates(l)
                if k == 9:
                    gla_sums(l)
                if 9 <= k < 12:
                    qk_norm(l, k - 5)
                if k == 11 or (k == 12 and l == 0):
                    for t in range(2):
                        dve.wait_ge(*when("dft_d", l, k - 11, t))
                        p = bank("dft_d", l, k - 11, t)
                        dve.tensor_copy(dft_ab[:, k - 11, t], p).then_inc(
                            *made("dft_ab", l, k - 11, t, frees=("dft_d", l, k - 11, t)))
                if k == 12:
                    gla_ends(l)
                if k == 13 or (k == 14 and l == 0):
                    s = k - 13
                    dve.wait_ge(*when("dft_l", l, s))
                    p = bank("dft_l", l, s)
                    dve.tensor_copy(proj1[:, FOUR:FOUR + 2, s * NX:(s + 1) * NX],
                                    p.rearrange("p (g n) -> p g n", g=2)).then_inc(
                                        *made("dft_mix", l, s, frees=("dft_l", l, s)))
                if k >= 13:
                    i = k - 13
                    rope(tm, i, proj1[:, rope_items[i], 0:NX], cst(C_COS1, NX), cst(C_SIN1, NX), NX,
                         "head_normed", tm, 4 + i)

            def beside_gqa(l, k):
                n = N1 if l == 0 else NX
                ntile = n // P
                if k == 0:
                    for h in range(4):
                        dve.wait_ge(*when("pairs", l, -1, h))
                        p = bank("pairs", l, -1, h)
                        dve.tensor_scalar(gla_s[:, h, 0:ntile], p[:, 0:n].rearrange("p (t n) -> p t n", n=P), 2.0,
                                          None, ALU.mult).then_inc(
                                              *made("gla_scores", l, -1, h, frees=("pairs", l, -1, h)))
                if 3 <= k <= 3 + LEVELS:
                    v = k - 3
                    dve.wait_ge(*when("decays", l, v))
                    dve.tensor_tensor(decays(l, v), decays(l, v),
                                      proj1[:, GLAQ:GLAK + 1, 0:n], ALU.mult).then_inc(*made("decayed", l, v))
                if 4 <= k < 4 + LEVELS:
                    v = k - 4
                    dve.wait_ge(*when("masks_loaded", 0))
                    for h in range(4):
                        dve.wait_ge(*when("pairs", l, v, h))
                        p = bank("pairs", l, v, h)
                        dve.wait_ge(*when("gla_scores", l, v - 1, h))
                        dve.copy_predicated(gla_s[:, h, 0:ntile], masks[:, v:v + 1].broadcast_to([P, ntile, P]),
                                            p[:, 0:n].rearrange("p (t n) -> p t n", n=P)).then_inc(
                                                *made("gla_scores", l, v, h, frees=("pairs", l, v, h)))
                if k >= 6 + LEVELS:
                    gla_outs_sb(l, k - 1)

            def gla_outs_sb(l, k):
                for s, h in gla_outs(l, k):
                    po = (h % 2) * HD
                    dve.wait_ge(*when("gla_out", l, s, h))
                    p = bank("gla_out", l, s, h)
                    dve.tensor_copy(proj1[po:po + HD, GLAQ + h // 2, s * NX:(s + 1) * NX],
                                    p[po:po + HD, 0:NX]).then_inc(
                                        *made("gla_out_sb", l, s, h, frees=("gla_out", l, s, h)))

            def ret_finish(l, h):
                dve.wait_ge(*when("rstd", ("ret", l, h)))
                x = proj2[:, RQ + h, :]
                dve.scalar_tensor_tensor(x, x, scalar2(l, "gn", h), rstd[:, h % 2, 0:N2], ALU.mult,
                                         ALU.mult).then_inc(*made("ret_normed", l, h))
                dve.wait_ge(*when("ret_normed", l, h))
                dve.tensor_tensor(x, x, proj2[:, RG + h, :], ALU.mult).then_inc(*made("mix_ret", l, h))

            def beside_fox(l, k):
                tp = ("b2", l)
                if k < 12:
                    project(tp, PROJ2, BESIDE2 + k, N2, proj2, VTEMP2)
                for i in rope_steps(k):
                    rope(tp, i, proj2[:, RQ + i, :], cst2(C_COS2, N2), cst2(C_SIN2, N2), N2,
                         "projected", tp, SLOT2[RQ + i])
                if k >= 21:
                    ret_finish(l, k - 21)
                if 12 <= k < 16:
                    h = k - 12
                    dve.wait_ge(*when("ret_pairs", l, h))
                    p = bank("ret_pairs", l, h)
                    if h >= 2:
                        dve.wait_ge(*when("ret_out", l, h - 2))
                    at = 0
                    for j, (t0, tn) in enumerate(TILES2):
                        n = N2 - t0
                        dve.tensor_tensor(ret_p[0:tn, h % 2, j, t0:N2], p[0:tn, at:at + n],
                                          cst2(C_DECAY + h * N2, n, tn), ALU.mult).then_inc(
                                              *made("ret_decayed", l, h, j, frees=("ret_pairs", l, h)))
                        at += n
                if 16 <= k < 20:
                    h = k - 16
                    dve.wait_ge(*when("ret_mean", l, h))
                    p = bank("ret_mean", l, h)
                    dve.tensor_tensor(proj2[:, RQ + h, :], proj2[:, RQ + h, :], p[:, 0:N2], ALU.subtract).then_inc(
                        *made("ret_centred", l, h, frees=("ret_mean", l, h)))

            dve.memset(eps_one[:, 0:1], EPS).then_inc(*made("eps_one", 0))
            dve.memset(eps_one[:, 1:2], 1.0).then_inc(*made("eps_one", 1))
            dve.wait_ge(*when("small_loaded", 0))
            for l in range(DEPTH):
                for name in ("naq", "gqaq"):
                    dve.tensor_scalar(scalar1(l, name), scalar1(l, name), HD ** -0.5, None, ALU.mult).then_inc(
                        *made("gain_scaled", l, name))
            dve.wait_ge(*when("gain_scaled", DEPTH - 1, "gqaq"))
            for d in range(KC):
                sum_squares(("start",), d, "all")
            for g in range(4):
                dve.wait_ge(*when("first_mod", 4 * g + 3))
                dve.tensor_copy(first_rows[:, g * 512:(g + 1) * 512], bank("first_rows", g)[0:2, :]).then_inc(
                    *made("first_rows_sb", g, frees=("first_rows", g)))
                if g == 0:
                    split_ahead(0)
            dve.wait_ge(*when("first_turned"))
            dve.tensor_copy(mod_raw[:, 0, :, 0:FIRST_MOD],
                            bank("first_turned")[:, 0:2 * FIRST_MOD].rearrange("p (j s) -> p s j", s=2)).then_inc(
                                *made("first_mod_raw", frees=("first_turned",)))
            for m in range(2):
                mod_finish(0, m, 2)
            for g in range(2):
                norm(("start",), g, range(KC))
            for l in range(DEPTH):
                t1, tm, to, t2 = ("ffn1", l), ("mix1", l), ("out1", l), ("ffn2", l)
                n = N1 if l == 0 else NX
                streams = BOTH if l == 0 else ONLY_X
                for h in ffn(t1, N1, 2, 0 if l == 0 else None):
                    residual(t1, l, 2, BOTH, h, FC // 2, h == 1, 0 if l == 0 else None)
                for i in range(12):
                    project(tm, PROJ1, i, width1(l, PROJ1[i]), proj1, VTEMP1)
                    if i >= 10:
                        qk_norm(l, i - 10)
                qk_norm(l, 2)
                qk_norm(l, 3)
                project(tm, PROJ1, 12, width1(l, PROJ1[12]), proj1, VTEMP1)
                per = 1 + l
                attention(na_heads(l), lambda i: [beside_na(l, k) for k in range(per * i, per * (i + 1))])
                attention(gqa_heads(l), lambda i: [beside_gqa(l, k) for k in range(per * i, per * (i + 1))])
                gla_outs_sb(l, 4 + LEVELS + 4)
                for c in (0, 2):
                    low_part(to, x_parts(N1), c, n, proj1[:, MIX1[c], 0:n])
                for c in range(2):
                    x = proj1[:, GLAQ + c, 0:n]
                    head_norm(("gla", l), c, x, scalar1(l, "gla"), n, "gla_out_sb", l, 1 - l, 2 * c + 1)
                    dve.wait_ge(*when("head_normed", ("gla", l), c))
                    dve.tensor_tensor(x, x, proj1[:, GLAR + c, 0:n], ALU.mult).then_inc(*made("mix_gla", l, c))
                for c in (6, 4):
                    low_part(to, x_parts(N1), c, n, proj1[:, MIX1[c], 0:n])
                residual(to, l, 5, streams, 0, KC, True)
                for h in ffn(t2, n, 2 - l, 1 if l == 0 else None):
                    residual(t2, l, 8, streams, h, FC // (2 - l), h == 1 - l, 1 if l == 0 else None)
            for l in range(DEPTH):
                tp, to, tf = ("b2", l), ("out2", l), ("ffn", l)
                y, e = negc[0:8, 0, :], negc[0:8, 1, :]
                for i in range(BESIDE2):
                    project(tp, PROJ2, i, N2, proj2, VTEMP2)
                    if i == 5:
                        dve.wait_ge(*when("projected", tp, 4))
                        dve.tensor_scalar(y, y, scalar2(l, "bfg", 0, 8), None, ALU.add).then_inc(*made("flog_y", l))
                        dve.wait_ge(*when("flog_y", l))
                        dve.scalar_tensor_tensor(e, y, -1.0, y, ALU.mult, ALU.min).then_inc(*made("flog_neg_abs", l))
                    if i == 7:
                        dve.wait_ge(*when("flog_ln", l))
                        dve.scalar_tensor_tensor(e, y, 0.0, e, ALU.min, ALU.subtract).then_inc(*made("flog_log", l))
                        dve.wait_ge(*when("flog_log", l))
                        dve.tensor_tensor_scan(negc[0:8, 2, :], eps_one[0:8, 1:2].broadcast_to([8, N2]), e, 0.0,
                                               ALU.mult, ALU.subtract).then_inc(*made("negc", l))
                attention(fox_heads(l), lambda i: beside_fox(l, i))
                ret_finish(l, 3)
                n = N2 if l == 0 else NX
                for c in range(0, KC, 2):
                    low_part(to, x_parts(N2), c, n, proj2[:, MIX2[c], N2 - n:N2])
                residual(to, l, None, None, 0, KC, True)
                for h in ffn(tf, n, 1):
                    residual(tf, l, None, None, h, FC, True)
            dve.wait_ge(*when("rstd", (("ffn", 1), 0)))
            for c in range(KC):
                dve.scalar_tensor_tensor(xf[:, c * NX:(c + 1) * NX], resid[:, c, META:META + NX],
                                         small[:, S_FINAL + c:S_FINAL + c + 1], rstd[:, 0, 0:NX],
                                         ALU.mult, ALU.mult).then_inc(*made("final_norm", c))
    return ev


def blocks(w):
    k, m = w.shape
    mb = -(-m // P)
    if m % P:
        w = np.concatenate([w, np.zeros((k, mb * P - m), w.dtype)], 1)
    return w.reshape(k // P, P, mb, P).transpose(2, 1, 0, 3).reshape(mb, P, -1)


def ffn_units(w1, w3, w2, halves):
    up = np.stack([blocks(w1), blocks(w3)], 1)
    down = w2.reshape(halves, FC // halves, P, KC, P).transpose(0, 3, 1, 2, 4).reshape(FC, 8, P, P)
    down = down.transpose(0, 2, 1, 3).reshape(halves, FC // halves, P, UNIT)
    out = []
    for h in range(halves):
        n = FC // halves
        out += [up[h * n:(h + 1) * n].reshape(2 * n, P, UNIT), down[h]]
    return out


def swap_heads(w, at, axis):
    idx = np.arange(w.shape[axis])
    idx[at:at + 4 * HD] = at + np.concatenate([np.arange(HD) + HD * h for h in (0, 2, 1, 3)])
    return np.take(w, idx, axis)


def columns(v):
    return v.reshape(-1, P).T


def kernel(**inputs):
    import concourse.bacc as bacc
    from concourse.bass_utils import run_bass_kernel_spmd

    a = {k: np.asarray(v) for k, v in inputs.items()}
    units = []
    off = np.concatenate([[0], np.cumsum([256, 256, 256, 256, 128, 128, 256, 256, 32, 256, 128, 128])])
    names = ("four", "naq", "nak", "nav", "glaq", "glak", "glav", "glar", "gate", "gqaq", "gqak", "gqav")
    order = ("nav", "gqav", "glav", "naq", "nak", "gqaq", "gqak", "gate", "glak", "glaq", "glar", "four")
    for l in range(DEPTH):
        units += ffn_units(a["ffn1_w1"][l], a["ffn1_w3"][l], a["ffn1_w2"][l], 2)
        w = swap_heads(a["w_in"][l], off[names.index("gqaq")], 1)
        units += [blocks(w[:, off[i]:off[i + 1]]) for i in map(names.index, order)]
        units.append(blocks(swap_heads(a["w_out"][l], 768, 0)))
        units += ffn_units(a["ffn2_w1"][l], a["ffn2_w3"][l], a["ffn2_w2"][l], 2 - l)
    for l in range(DEPTH):
        w = a["w_in_2"][l]
        for lo, hi in ((1024, 1536), (1536, 1544), (0, 1024), (1544 + 1536, 1544 + 2048), (1544, 1544 + 512),
                       (1544 + 1024, 1544 + 1536), (1544 + 512, 1544 + 1024)):
            units.append(blocks(w[:, lo:hi]))
        units.append(blocks(a["w_out_2"][l]))
        units += ffn_units(a["w_gate_2"][l], a["w_up_2"][l], a["w_down_2"][l], 1)

    two = lambda v: np.concatenate([v, v])[:, None]
    small = []
    for l in range(DEPTH):
        small += [two(a[n][l]) for n in ("na_q_norm", "na_k_norm", "gqa_q_norm", "gqa_k_norm", "gla_norm")]
        small += [a["gla_b_gate_f"][l][:, None], a["gla_b_gate_b"][l][:, None], columns(a["b_mod"][l])]
    for l in range(DEPTH):
        fg = np.zeros((P, 1), np.float32)
        fg[:8, 0] = a["b_fgate_2"][l]
        small += [columns(a["attn_norm_2"][l]), columns(a["ffn_norm_2"][l]), columns(a["ret_gn_2"][l]), fg]
    small.append(columns(a["final_norm_2"]))

    wgate = np.zeros((32, DEPTH, 2 * P), np.float32)
    for l in range(DEPTH):
        wgate[0:16, l, 0:P] = a["gla_w_gate_f"][l]
        wgate[16:32, l, P:2 * P] = a["gla_w_gate_b"][l]

    cq = np.arange(64)
    start = np.clip(cq - 8, 0, 48)
    ck = np.arange(64)
    inside = (ck[None] >= start[:, None]) & (ck[None] < start[:, None] + 16)
    col = np.clip(ck[None] - cq[:, None] + 15, 0, 30)
    na_bias = np.full((DEPTH, 2, 64, 4, 6, 64), NEG, np.float32)
    for half in range(2):
        for j in range(6):
            rows = a["na_rpb"][:, :, j - 2 - half + 7]
            got = rows[:, :, col]
            na_bias[:, half, :, :, j] = np.where(inside[None, None], got, np.float32(NEG)).transpose(0, 2, 1, 3)
    na_bias = na_bias.reshape(DEPTH, P, 4 * 6 * 64)

    kept, dft, second = constants()
    tr = lambda v: v.T.reshape(KC, P, -1).transpose(1, 0, 2)
    arrays = {
        "stream": np.concatenate(units, 0),
        "w_mod": np.ascontiguousarray(a["w_mod"].transpose(0, 2, 1)).reshape(DEPTH, NMOD * KC, P, D),
        "w_mod_first": a["w_mod"][0, :, 0:FIRST_MOD * P].reshape(4, 2, P, 4, 512).transpose(3, 0, 2, 1, 4).reshape(
            FIRST_MOD, P, D),
        "c_cols": np.stack([a["c"][0].reshape(KC, P).T, a["c_ctx"].reshape(KC, P).T], 2).reshape(P, 2 * KC),
        "x": tr(a["x"][0]), "ctx": tr(a["ctx"][0]), "meta": tr(a["meta_tokens_2"]),
        "c": a["c"].reshape(1, D), "c_ctx": a["c_ctx"].reshape(1, D),
        "small": np.concatenate(small, 1), "consts": kept, "dft": dft, "consts2": second, "masks": level_masks(),
        "wgate": wgate, "na_bias": na_bias,
    }
    arrays = {k: np.ascontiguousarray(v) for k, v in arrays.items()}

    def program(old):
        nc = bacc.Bacc("TRN2", target_bir_lowering=False, num_devices=1)
        A = {k: nc.dram_tensor(f"{k}_dram", v.shape, mybir.dt.from_np(v.dtype), kind="ExternalInput").ap()
             for k, v in arrays.items()}
        A["out"] = nc.dram_tensor("out_dram", (P, KC * NX), F32, kind="ExternalOutput").ap()
        return nc, build(nc, A, old)

    _, counted = program(None)
    nc, _ = program((counted.table, counted.banks))
    r = run_bass_kernel_spmd(nc, [{f"{k}_dram": v for k, v in arrays.items()}], core_ids=[0])
    out = r.results[0]["out_dram"].reshape(P, KC, NX)
    return np.ascontiguousarray(out.transpose(2, 1, 0)).reshape(1, NX, D)
```
